# Optimizing a Trainium2 kernel written in Bass

```python
import math
import jax, jax.numpy as jnp
from jax import lax
import numpy as np

D_MODEL = 1024
BATCH = 1
SEQ = 2048
DEPTH = 1
DEC_BATCH = 8
DEC_SEQ = 8
PAST_LEN = 4096
PAGE_SIZE = 128

HEAD_DIM = 64
N_GROUPS = 3
WINDOWS = (128, 512, 2048)
DILATIONS = (1, 4, 16)
N_BACK = 128
HEADS_PER_GROUP = D_MODEL // 128
A_HEADS = N_GROUPS * HEADS_PER_GROUP
A_QKV = A_HEADS * HEAD_DIM
A_OUT = HEADS_PER_GROUP * HEAD_DIM
ATTN_BLOCK = 128
ATTN_SCALE = HEAD_DIM ** -0.5
B_HEADS = D_MODEL // 256
B_F_HEAD = 128
B_I_HEAD = D_MODEL // (2 * B_HEADS)
B_F = B_HEADS * B_F_HEAD
B_I = B_HEADS * B_I_HEAD
B_OUT = B_I
CHUNK = 64
IN_COLS = 3 * A_QKV + A_OUT + 2 * B_F + B_I + B_OUT + 2 * D_MODEL
EPS = 1e-6

kernel_name = 'hybrid_dilated_attn_hgrn2_decode_step'

def rmsnorm(x, gain):
    xf = x.astype(jnp.float32)
    y = xf * lax.rsqrt(jnp.mean(xf * xf, axis=-1, keepdims=True) + EPS) * gain.astype(jnp.float32)
    return y.astype(x.dtype)

def alibi_slopes():
    s = 2.0 ** (-8.0 * (np.arange(A_HEADS) + 1) / A_HEADS)
    return jnp.asarray(s.astype(np.float32).reshape(N_GROUPS, HEADS_PER_GROUP))

def dilated_group_prompt(q, k, v, dil, slopes):
    n, t, h, hd = q.shape
    L = t // dil
    nb = -(-L // ATTN_BLOCK)
    lp = nb * ATTN_BLOCK

    def split(a):
        a = a.reshape(n, L, dil, h, hd).transpose(0, 2, 1, 3, 4)
        a = jnp.pad(a, ((0, 0), (0, 0), (0, lp - L), (0, 0), (0, 0)))
        return a.reshape(n, dil, nb, ATTN_BLOCK, h, hd)

    def with_prev(a):
        prev = jnp.pad(a[:, :, :-1], ((0, 0), (0, 0), (1, 0), (0, 0), (0, 0), (0, 0)))
        return jnp.concatenate([prev, a], axis=3)

    qb = split(q)
    kk = with_prev(split(k))
    vv = with_prev(split(v))
    s = jnp.einsum('brnqhd,brnkhd->brnhqk', qb, kk).astype(jnp.float32) * ATTN_SCALE
    delta = np.arange(ATTN_BLOCK)[:, None] + ATTN_BLOCK - np.arange(2 * ATTN_BLOCK)[None, :]
    key_pos = (np.arange(nb)[:, None, None] * ATTN_BLOCK
               + np.arange(2 * ATTN_BLOCK)[None, None, :] - ATTN_BLOCK)
    valid = (delta >= 0) & (delta <= N_BACK) & (key_pos >= 0)
    dist = jnp.asarray((delta * dil).astype(np.float32))
    s = s - slopes[:, None, None] * dist
    s = jnp.where(valid[:, None], s, -jnp.inf)
    m = jnp.max(s, axis=-1, keepdims=True)
    p = jnp.exp(s - m)
    l = jnp.sum(p, axis=-1, keepdims=True)
    o = jnp.einsum('brnhqk,brnkhd->brnqhd', p, vv.astype(jnp.float32)) / jnp.swapaxes(l, 3, 4)
    lse = jnp.swapaxes((m + jnp.log(l))[..., 0], 3, 4)
    o = o.reshape(n, dil, lp, h, hd)[:, :, :L].transpose(0, 2, 1, 3, 4).reshape(n, t, h, hd)
    lse = lse.reshape(n, dil, lp, h)[:, :, :L].transpose(0, 2, 1, 3).reshape(n, t, h)
    return o, lse

def dilated_group_sample(q, k, v, kv_buf, dil, slopes):
    n, t, h, hd = q.shape
    wb = kv_buf.shape[1]
    kcat = jnp.concatenate([kv_buf[:, :, 0], k], axis=1)
    vcat = jnp.concatenate([kv_buf[:, :, 1], v], axis=1)
    steps = np.arange(N_BACK + 1)
    idx = wb + np.arange(t)[:, None] - steps[None, :] * dil
    valid = idx >= 0
    idx = np.maximum(idx, 0)
    kg = kcat[:, idx]
    vg = vcat[:, idx]
    dist = jnp.asarray((steps * dil).astype(np.float32))
    s = jnp.einsum('nthd,ntkhd->nthk', q, kg).astype(jnp.float32) * ATTN_SCALE - slopes[:, None] * dist
    s = jnp.where(valid[:, None, :], s, -jnp.inf)
    m = jnp.max(s, axis=-1, keepdims=True)
    p = jnp.exp(s - m)
    l = jnp.sum(p, axis=-1, keepdims=True)
    o = jnp.einsum('nthk,ntkhd->nthd', p, vg.astype(jnp.float32)) / l
    lse = (m + jnp.log(l))[..., 0]
    return o, lse

def hgrn2_recurrence(q, k, v, log_f, s0):
    n, t, h, fd = q.shape
    iv = v.shape[-1]
    c = min(CHUNK, t)
    nc = -(-t // c)
    tp = nc * c

    def chunks(a):
        a = jnp.pad(a, ((0, 0), (0, tp - t), (0, 0), (0, 0)))
        return jnp.moveaxis(a.reshape(n, nc, c, h, a.shape[-1]), 1, 0)

    causal = np.tril(np.ones((c, c), dtype=bool))[None, :, :, None, None]

    def step(state, inp):
        qc, kc, vc, gc = inp
        b = jnp.cumsum(gc, axis=1)
        o_inter = jnp.einsum('nchf,nhfi->nchi', qc * jnp.exp(b), state)
        decay = jnp.exp(jnp.where(causal, b[:, :, None] - b[:, None, :], -jnp.inf))
        att = jnp.einsum('nthf,nshf,ntshf->nths', qc, kc, decay)
        o_intra = jnp.einsum('nths,nshi->nthi', att, vc)
        b_last = b[:, -1]
        state = (jnp.exp(b_last)[..., None] * state
                 + jnp.einsum('nshf,nshi->nhfi', kc * jnp.exp(b_last[:, None] - b), vc))
        return state, o_inter + o_intra

    s_fin, o = lax.scan(step, s0.astype(jnp.float32),
                        (chunks(q), chunks(k), chunks(v), chunks(log_f)))
    o = jnp.moveaxis(o, 0, 1).reshape(n, tp, h, iv)[:, :t]
    return o, s_fin

def mixer_layer(x, c, kv_bufs, hgrn_state, lb, norm_gain, w_ada, b_ada, w_in, q_gain, k_gain,
                o_gain, w_ba, w_bb, w_o):
    n, t, _ = x.shape
    shift, scale, gate = jnp.split(jax.nn.silu(c) @ w_ada + b_ada, 3, axis=-1)
    h = rmsnorm(x, norm_gain) * (1 + scale[:, None]) + shift[:, None]
    sizes = (A_QKV, A_QKV, A_QKV, A_OUT, B_F, B_F, B_I, B_OUT, D_MODEL, D_MODEL)
    cuts = np.cumsum(sizes)[:-1].tolist()
    qa, ka, va, za, qb, fb, ib, zb, ga, gb = jnp.split(h @ w_in, cuts, axis=-1)

    shp = (n, t, N_GROUPS, HEADS_PER_GROUP, HEAD_DIM)
    qa = rmsnorm(qa.reshape(shp), q_gain)
    ka = rmsnorm(ka.reshape(shp), k_gain)
    va = va.reshape(shp)
    slopes = alibi_slopes()
    outs, lses, new_kv = [], [], []
    for g in range(N_GROUPS):
        qg, kg, vg = qa[:, :, g], ka[:, :, g], va[:, :, g]
        kv_rows = jnp.stack([kg, vg], axis=2)
        if kv_bufs is None:
            o, lse = dilated_group_prompt(qg, kg, vg, DILATIONS[g], slopes[g])
            kv_rows = kv_rows[:, t - min(WINDOWS[g], t):]
        else:
            o, lse = dilated_group_sample(qg, kg, vg, kv_bufs[g], DILATIONS[g], slopes[g])
        outs.append(o)
        lses.append(lse)
        new_kv.append(kv_rows)
    alpha = jax.nn.softmax(jnp.stack(lses), axis=0)
    o_a = jnp.einsum('gnth,gnthd->nthd', alpha, jnp.stack(outs)).reshape(n, t, A_OUT).astype(x.dtype)
    branch_a = (o_a * jax.nn.silu(za)) @ w_ba

    lbh = lb.reshape(B_HEADS, B_F_HEAD)
    f = lbh + (1.0 - lbh) * jax.nn.sigmoid(fb.astype(jnp.float32).reshape(n, t, B_HEADS, B_F_HEAD))
    q_h = jax.nn.silu(qb.astype(jnp.float32)).reshape(n, t, B_HEADS, B_F_HEAD)
    i_h = ib.astype(jnp.float32).reshape(n, t, B_HEADS, B_I_HEAD)
    o_b, s_new = hgrn2_recurrence(q_h, 1.0 - f, i_h, jnp.log(f), hgrn_state)
    o_b = rmsnorm(o_b, o_gain).reshape(n, t, B_OUT).astype(x.dtype)
    branch_b = (o_b * jax.nn.silu(zb)) @ w_bb

    merged = jax.nn.sigmoid(ga) * branch_a + jax.nn.sigmoid(gb) * branch_b
    y = x + gate[:, None] * (merged @ w_o)
    return y, new_kv, s_new.astype(x.dtype)

def setup_inputs(seed: int = 0) -> dict:
    key = jax.random.key(seed)
    ks = jax.random.split(key, 20)

    def nrm(k, shape, s):
        return jax.random.normal(k, shape, jnp.float32) * s

    kv_shape = lambda g: (DEPTH, DEC_BATCH, min(WINDOWS[g], PAST_LEN), 2, HEADS_PER_GROUP, HEAD_DIM)
    return {
        'x_prompt': nrm(ks[0], (BATCH, SEQ, D_MODEL), 1.0),
        'x_sample': nrm(ks[1], (DEC_BATCH, DEC_SEQ, D_MODEL), 1.0),
        'cache_kv_g0': nrm(ks[2], kv_shape(0), 1.0),
        'cache_kv_g1': nrm(ks[3], kv_shape(1), 1.0),
        'cache_kv_g2': nrm(ks[4], kv_shape(2), 1.0),
        'state_hgrn': nrm(ks[5], (DEPTH, DEC_BATCH, B_HEADS, B_F_HEAD, B_I_HEAD), 0.3),
        'c_prompt': nrm(ks[6], (BATCH, D_MODEL), 1.0),
        'c_sample': nrm(ks[7], (DEC_BATCH, D_MODEL), 1.0),
        'norm_gain': 1.0 + nrm(ks[8], (DEPTH, D_MODEL), 0.1),
        'w_ada': nrm(ks[9], (DEPTH, D_MODEL, 3 * D_MODEL), 0.5 * D_MODEL ** -0.5),
        'b_ada': nrm(ks[10], (DEPTH, 3 * D_MODEL), 0.01),
        'w_in': nrm(ks[11], (DEPTH, D_MODEL, IN_COLS), D_MODEL ** -0.5),
        'q_norm_gain': 1.0 + nrm(ks[12], (DEPTH, HEAD_DIM), 0.1),
        'k_norm_gain': 1.0 + nrm(ks[13], (DEPTH, HEAD_DIM), 0.1),
        'hgrn_lb_logits': nrm(ks[14], (DEPTH + 1, B_F), 0.5),
        'hgrn_out_norm_gain': 1.0 + nrm(ks[15], (DEPTH, B_I_HEAD), 0.1),
        'w_branch_a': nrm(ks[16], (DEPTH, A_OUT, D_MODEL), A_OUT ** -0.5),
        'w_branch_b': nrm(ks[17], (DEPTH, B_OUT, D_MODEL), B_OUT ** -0.5),
        'w_out': nrm(ks[18], (DEPTH, D_MODEL, D_MODEL), D_MODEL ** -0.5),
    }

def reference(x_prompt, x_sample, cache_kv_g0, cache_kv_g1, cache_kv_g2, state_hgrn, c_prompt, c_sample,
              norm_gain, w_ada, b_ada, w_in, q_norm_gain, k_norm_gain, hgrn_lb_logits, hgrn_out_norm_gain,
              w_branch_a, w_branch_b, w_out):
    lbs = jnp.cumsum(jax.nn.softmax(hgrn_lb_logits.astype(jnp.float32), axis=0), axis=0)
    xp, xs = x_prompt, x_sample
    kvp = ([], [], [])
    kvs = ([], [], [])
    sp, ss = [], []
    for layer in range(DEPTH):
        w = (norm_gain[layer], w_ada[layer], b_ada[layer], w_in[layer], q_norm_gain[layer],
             k_norm_gain[layer], hgrn_out_norm_gain[layer], w_branch_a[layer], w_branch_b[layer], w_out[layer])
        s0 = jnp.zeros((xp.shape[0], B_HEADS, B_F_HEAD, B_I_HEAD), jnp.float32)
        xp, kv_new, s_new = mixer_layer(xp, c_prompt, None, s0, lbs[layer], *w)
        for g in range(N_GROUPS):
            kvp[g].append(kv_new[g])
        sp.append(s_new)
        bufs = (cache_kv_g0[layer], cache_kv_g1[layer], cache_kv_g2[layer])
        xs, kv_new, s_new = mixer_layer(xs, c_sample, bufs, state_hgrn[layer], lbs[layer], *w)
        for g in range(N_GROUPS):
            kvs[g].append(kv_new[g])
        ss.append(s_new)
    return (xp, xs,
            jnp.stack(kvp[0]), jnp.stack(kvp[1]), jnp.stack(kvp[2]), jnp.stack(sp),
            jnp.stack(kvs[0]), jnp.stack(kvs[1]), jnp.stack(kvs[2]), jnp.stack(ss))


_drawn_inputs = setup_inputs


def setup_inputs(seed=0):
    import zlib

    import numpy as np

    out = dict(_drawn_inputs(seed))
    spreads = {}
    factors = {'cache_kv_g0': 8.0,
     'cache_kv_g1': 4.667,
     'cache_kv_g2': 25.456,
     'q_norm_gain': 8.0,
     'hgrn_out_norm_gain': 5.418}
    for name, (base, spread) in spreads.items():
        noise = np.random.default_rng([zlib.crc32(name.encode()), seed]).standard_normal(out[name].shape)
        drawn = base * np.exp(spread * noise) if base else spread * noise
        out[name] = __import__('jax').numpy.asarray(drawn.astype(out[name].dtype))
    for name, factor in factors.items():
        out[name] = (out[name] * factor).astype(out[name].dtype)
    return out
```

```python
from contextlib import ExitStack

import concourse.bass as bass
from concourse import mybir

ALU = mybir.AluOpType
ACT = mybir.ActivationFunctionType
F32 = mybir.dt.float32
U32 = mybir.dt.uint32
AX = mybir.AxisListType

P = 128
D = 1024
KD = D // P
SEQ = 2048
SB, ST = 8, 8
NS = SB * ST
NT = SEQ + NS
G = 3
DIL = (1, 4, 16)
PAIRS = 4
HD = 64
BLK = SEQ // P
KEYS = 13
BH = 4
EPS = 1e-6
CH = 512
NCH = SEQ // CH
ORow = 132


def block_tokens(g, i):
    if g == 0:
        return P * i, 1, i > 0
    if g == 1:
        r, b = divmod(i, 4)
        return r + 4 * P * b, 4, b > 0
    return i, 16, False


def first_signals(pool, sems):
    for sem in sems:
        pool.sem_inc(sem, 1)


def phase_input(nc, t, dr):
    with ExitStack() as ctx:
        sb = lambda name, *a: ctx.enter_context(nc.sbuf_tensor("input_" + name, *a))
        ps = lambda name, *a: ctx.enter_context(nc.psum_tensor("input_" + name, *a))
        sems = []

        def sem(name):
            sems.append(ctx.enter_context(nc.semaphore("input_" + name)))
            return sems[-1]

        c_sb = sb("c_sb", [P, KD, 9], F32)
        c_exp = sb("c_exp", [P, KD, 9], F32)
        c_rec = sb("c_rec", [P, KD, 9], F32)
        c_act = sb("c_act", [P, KD, 9], F32)
        b_sb = sb("b_sb", [P, 24], F32)
        gain_sb = sb("gain_sb", [P, KD], F32)
        ones_d = sb("ones_d", [P, P], F32)
        w_ada = [sb(f"w_ada{i}", [P, KD, CH], F32) for i in range(2)]
        x_sb = [sb(f"x_sb{i}", [P, KD, CH], F32) for i in range(2)]
        x_sq = sb("x_sq", [P, KD, CH], F32)
        log_ms = sb("log_ms", [P, CH], F32)
        rstd = sb("rstd", [P, CH], F32)
        ada_ps = ps("ada_ps", [P, 24, 9], F32)
        ss_ps = ps("ss_ps", [P, CH], F32)
        small = sem("small_loaded")
        w_in = [sem(f"w_ada_loaded{i}") for i in range(2)]
        x_in = [sem(f"x_loaded{i}") for i in range(2)]
        c_done, silu_done, ada_done, mod_done = sem("c_exp_done"), sem("silu_done"), sem("ada_done"), sem("mod_done")
        sq_done, ss_done, ms_done, r_done, xn_done, h_done = (sem(n) for n in
            ("sq_done", "ss_done", "ms_done", "r_done", "xn_done", "h_done"))
        steps = sem("vector_steps")
        hT, mod, gate = t["hT"], t["mod"], t["gate"]
        xs = dr["xT"]

        with nc.Block() as block:
            @block.gpsimd
            def _(pool):
                first_signals(pool, sems)

            @block.sync
            def _(sp):
                sp.dma_start(c_sb[:, :, :], dr["cT"]).then_inc(small, 16)
                sp.dma_start(b_sb[:, :], dr["b_ada"]).then_inc(small, 16)
                sp.dma_start(gain_sb[:, :], dr["norm_gain"]).then_inc(small, 16)
                sp.dma_start(ones_d[:, :], dr["ones_d"]).then_inc(small, 16)

                def load_x(c):
                    n = CH if c < NCH else NS
                    if c >= 2:
                        sp.wait_ge(h_done, 1 + c - 1)
                    sp.dma_start(x_sb[c % 2][:, :, 0:n], xs[:, :, c * CH:c * CH + n]).then_inc(x_in[c % 2], 16)

                load_x(0)
                load_x(1)
                with sp.Fori(0, 3) as i:
                    for j in range(2):
                        sp.wait_ge(ada_done, 1 + i * 2)
                        sp.dma_start(w_ada[j][:, :, :], dr["w_ada"][i * 2 + j]).then_inc(w_in[j], 16)
                for c in range(2, NCH + 1):
                    load_x(c)

            @block.tensor
            def _(pe):
                pe.wait_ge(silu_done, 1 + 1)
                with pe.Fori(0, 3) as i:
                    for j in range(2):
                        pe.wait_ge(w_in[j], 1 + i * 16 + 16)
                        for c in range(4):
                            for k in range(KD):
                                mm = pe.matmul(ada_ps[:, bass.ds(i * 8 + (j * 4 + c), 1), :],
                                               w_ada[j][:, k, c * P:(c + 1) * P], c_act[:, k, :],
                                               start=(k == 0), stop=(k == KD - 1))
                        mm.then_inc(ada_done, 1)

                def sums(wait_sq, wait_ms, n):
                    pe.wait_ge(sq_done, 1 + wait_sq)
                    pe.wait_ge(ms_done, 1 + wait_ms)
                    for k in range(KD):
                        mm = pe.matmul(ss_ps[:, 0:n], ones_d[:, :], x_sq[:, k, 0:n], start=(k == 0), stop=(k == KD - 1))
                    mm.then_inc(ss_done, 1)

                with pe.Fori(0, 4) as i:
                    sums(i + 1, i, CH)
                sums(5, 4, NS)

            @block.scalar
            def _(act):
                act.preload_act_table_set("natural_log_exp_and_others")
                act.wait_ge(small, 1 + 64)
                act.activation(c_exp[:, :, :], c_sb[:, :, :], ACT.Exp, scale=-1.0).then_inc(c_done, 1)

                def square(j, loaded, used, n):
                    act.wait_ge(x_in[j], 1 + loaded)
                    act.wait_ge(ss_done, 1 + used)
                    act.activation(x_sq[:, :, 0:n], x_sb[j][:, :, 0:n], ACT.Square).then_inc(sq_done, 1)

                def leave(nth, xn, n):
                    act.wait_ge(ss_done, 1 + nth)
                    act.wait_ge(xn_done, 1 + xn)
                    act.activation(log_ms[:, 0:n], ss_ps[:, 0:n], ACT.Ln, bias=t["eps"][:, 0:1]).then_inc(ms_done, 1)
                    act.wait_ge(ms_done, 1 + nth)
                    act.activation(rstd[:, 0:n], log_ms[:, 0:n], ACT.Exp, scale=-0.5).then_inc(r_done, 1)

                with act.Fori(0, 2) as i:
                    for j in range(2):
                        square(j, i * 16 + 16, i * 2 + j, CH)
                        leave(i * 2 + (j + 1), i * 2 + j, CH)
                square(0, 48, 4, NS)
                leave(5, 4, NS)

            @block.vector
            def _(dve):
                dve.wait_ge(c_done, 1 + 1)
                dve.tensor_scalar(c_rec[:, :, :], c_exp[:, :, :], 1.0, None, ALU.add).then_inc(steps, 1)
                dve.wait_ge(steps, 1 + 1)
                dve.reciprocal(c_exp[:, :, :], c_rec[:, :, :]).then_inc(steps, 1)
                dve.wait_ge(steps, 1 + 2)
                dve.tensor_tensor(c_act[:, :, :], c_exp[:, :, :], c_sb[:, :, :], ALU.mult).then_inc(silu_done, 1)
                dve.wait_ge(ada_done, 1 + 6)
                dve.tensor_tensor(mod[:, :, :], ada_ps[:, 0:16, :], b_sb[:, 0:16].unsqueeze(2).broadcast_to([P, 16, 9]),
                                  ALU.add).then_inc(steps, 1)
                dve.tensor_tensor(gate[:, :, :], ada_ps[:, 16:24, :], b_sb[:, 16:24].unsqueeze(2).broadcast_to([P, 8, 9]),
                                  ALU.add).then_inc(steps, 1)
                dve.wait_ge(steps, 1 + 4)
                dve.tensor_scalar(mod[:, 8:16, :], mod[:, 8:16, :], 1.0, None, ALU.add).then_inc(steps, 1)
                dve.wait_ge(steps, 1 + 5)
                dve.tensor_tensor(mod[:, 8:16, :], mod[:, 8:16, :], gain_sb[:, :].unsqueeze(2).broadcast_to([P, 8, 9]),
                                  ALU.mult).then_inc(mod_done, 1)
                dve.wait_ge(mod_done, 1 + 1)

                def normed(j, nth, n):
                    dve.wait_ge(r_done, 1 + nth)
                    dve.tensor_tensor(x_sb[j][:, :, 0:n], x_sb[j][:, :, 0:n],
                                      rstd[:, 0:n].unsqueeze(1).broadcast_to([P, KD, n]), ALU.mult).then_inc(xn_done, 1)
                    dve.wait_ge(xn_done, 1 + nth)

                with dve.Fori(0, 2) as i:
                    for j in range(2):
                        normed(j, i * 2 + (j + 1), CH)
                        for k in range(KD):
                            h = dve.tensor_scalar(hT[:, k, bass.ds(i * 2 * CH + j * CH, CH)], x_sb[j][:, k, :],
                                                  mod[:, 8 + k, 0:1], mod[:, k, 0:1], ALU.mult, ALU.add)
                        h.then_inc(h_done, 1)
                normed(0, 5, NS)
                per_token = lambda a: a.unsqueeze(3).broadcast_to([P, KD, SB, ST])
                split = lambda a: a.rearrange("p k (b t) -> p k b t", t=ST)
                dve.tensor_tensor(split(x_sb[0][:, :, 0:NS]), split(x_sb[0][:, :, 0:NS]), per_token(mod[:, 8:16, 1:9]),
                                  ALU.mult).then_inc(steps, 1)
                dve.wait_ge(steps, 1 + 6)
                dve.tensor_tensor(split(hT[:, :, SEQ:NT]), split(x_sb[0][:, :, 0:NS]), per_token(mod[:, 0:8, 1:9]),
                                  ALU.add).then_inc(h_done, 1)


def phase_attention(nc, t, dr):
    UNITS = 15
    with ExitStack() as ctx:
        sb = lambda name, *a: ctx.enter_context(nc.sbuf_tensor("attention_" + name, *a))
        ps = lambda name, *a: ctx.enter_context(nc.psum_tensor("attention_" + name, *a))
        sems = []

        def sem(name):
            sems.append(ctx.enter_context(nc.semaphore("attention_" + name)))
            return sems[-1]

        hT = t["hT"]
        w_sb = [sb(f"w_{x}", [P, KD, P], F32) for x in "qkv"]
        qk = [[sb(f"{x}T{g}", [P, NT], F32) for g in range(G)] for x in "qk"]
        v_sb = [sb(f"v{g}", [P, BLK + 1, 2, HD + 1], F32) for g in range(G)]
        dist = [sb(f"dist{g}", [P, 2, 2 * P], F32) for g in range(G)]
        scores = sb("scores", [P, 2, 2 * P], F32)
        probs = sb("probs", [P, 2, 2 * P], F32)
        probsT = sb("probsT", [P, 4, P], F32)
        sq = sb("sq", [P, CH], F32)
        log_ms = sb("log_ms", [P, CH], F32)
        rstd = sb("rstd", [P, CH], F32)
        o_out = sb("o_out", [P, BLK, ORow], F32)
        gains = sb("gains", [P, 2], F32)
        ident, ones_h = t["ident"], sb("ones_h", [P, P], F32)
        u_ps = [ps(f"u_ps{i}", [P, CH], F32) for i in range(2)]
        ss_ps = ps("ss_ps", [P, CH], F32)
        s_ps = [ps(f"s_ps{h}", [P, 2 * P], F32) for h in range(2)]
        t_ps = ps("t_ps", [P, 4, P], F32)
        o_ps = ps("o_ps", [P, 2, HD + 1], F32)
        const_in = sem("const_loaded")
        w_in = [sem(f"w_{x}_loaded") for x in "qkv"]
        dist_in = sem("dist_loaded")
        ones_set, gain_set = sem("ones_set"), sem("gain_set")
        unit_done, sq_done, ss_done, ms_done, r_done, evac_done = (sem(n) for n in
            ("unit_done", "sq_done", "ss_done", "ms_done", "r_done", "evac_done"))
        s_done, max_done, exp_done, t_done, copy_done, pv_done, o_done = (sem(n) for n in
            ("s_done", "max_done", "exp_done", "t_done", "copy_done", "pv_done", "o_done"))
        s_seen = sem("s_seen")
        half_out = [sem(f"o_half{i}_stored") for i in range(2)]
        kv_out = sem("kv_stored")
        KV = 16 * 5

        def project_unit(pe, g, n, i):
            kind, j = divmod(i, 5)
            if i == 0:
                pe.wait_ge(evac_done, 1 + n * UNITS)
            else:
                pe.wait_ge(evac_done, 1 + n * UNITS + (i - 1))
            if j == 0:
                pe.wait_ge(w_in[kind], 1 + n * 16 + 16)
            u = u_ps[i % 2]
            if kind < 2:
                lo, w = (j * CH, CH) if j < NCH else (SEQ, NS)
                for k in range(KD):
                    mm = pe.matmul(u[:, 0:w], w_sb[kind][:, k, :], hT[:, k, lo:lo + w], start=(k == 0), stop=(k == KD - 1))
            elif j < NCH:
                for b in range(4):
                    lo, step, _ = block_tokens(g, 4 * j + b)
                    for k in range(KD):
                        mm = pe.matmul(u[:, b * P:(b + 1) * P], hT[:, k, lo:lo + (P - 1) * step + 1:step],
                                       w_sb[2][:, k, :], start=(k == 0), stop=(k == KD - 1))
            else:
                for k in range(KD):
                    mm = pe.matmul(u[0:NS, 0:P], hT[:, k, SEQ:NT], w_sb[2][:, k, :], start=(k == 0), stop=(k == KD - 1))
            mm.then_inc(unit_done, 1)

        def head_sums(pe, n, i):
            if i >= 10:
                return
            w = CH if i % 5 < NCH else NS
            pe.wait_ge(sq_done, 1 + n * 10 + (i + 1))
            pe.wait_ge(ms_done, 1 + n * 10 + i)
            pe.matmul(ss_ps[:, 0:w], ones_h[:, :], sq[:, 0:w], start=True, stop=True).then_inc(ss_done, 1)

        def square_unit(act, n, i):
            if i >= 10:
                return
            w = CH if i % 5 < NCH else NS
            act.wait_ge(unit_done, 1 + n * UNITS + (i + 1))
            act.wait_ge(ss_done, 1 + n * 10 + i)
            act.activation(sq[:, 0:w], u_ps[i % 2][:, 0:w], ACT.Square).then_inc(sq_done, 1)

        def root(act, n, i):
            if i >= 10:
                return
            w = CH if i % 5 < NCH else NS
            act.wait_ge(ss_done, 1 + n * 10 + (i + 1))
            act.activation(log_ms[:, 0:w], ss_ps[:, 0:w], ACT.Ln, bias=t["eps"][:, 0:1]).then_inc(ms_done, 1)
            act.wait_ge(ms_done, 1 + n * 10 + (i + 1))
            act.wait_ge(evac_done, 1 + n * UNITS + i)
            act.activation(rstd[:, 0:w], log_ms[:, 0:w], ACT.Exp, scale=-0.5).then_inc(r_done, 1)

        def leave_unit(dve, g, n, i):
            kind, j = divmod(i, 5)
            u = u_ps[i % 2]
            if i == 0:
                dve.wait_ge(kv_out, 1 + (n - 1) * KV if not isinstance(n, int) or n > 1 else 0)
            if kind < 2:
                lo, w = (j * CH, CH) if j < NCH else (SEQ, NS)
                dve.wait_ge(r_done, 1 + n * 10 + (i + 1))
                dve.scalar_tensor_tensor(out=qk[kind][g][:, lo:lo + w], in0=u[:, 0:w], scalar=gains[:, kind:kind + 1],
                                         in1=rstd[:, 0:w], op0=ALU.mult, op1=ALU.mult).then_inc(evac_done, 1)
            else:
                dve.wait_ge(unit_done, 1 + n * UNITS + (i + 1))
                if j < NCH:
                    dve.tensor_copy(v_sb[g][:, 4 * j:4 * j + 4, :, 0:HD],
                                    u[:, :].rearrange("p (b h d) -> p b h d", b=4, h=2)).then_inc(evac_done, 1)
                else:
                    dve.tensor_copy(v_sb[g][0:NS, BLK, :, 0:HD],
                                    u[0:NS, 0:P].rearrange("p (h d) -> p h d", h=2)).then_inc(evac_done, 1)

        def key_range(g, i):
            lo, step, before = block_tokens(g, i)
            first = 0 if before else 1
            return lo - (0 if first else P * step), step, first

        def score(pe, g, a, i):
            if i == 0:
                pe.wait_ge(evac_done, 1 + a * UNITS + UNITS)
            pe.wait_ge(max_done, 1 + a * 32 + 2 * i)
            lo, step, _ = block_tokens(g, i)
            klo, _, first = key_range(g, i)
            nk = (2 - first) * P
            for h in range(2):
                q = qk[0][g][h * HD:(h + 1) * HD, lo:lo + (P - 1) * step + 1:step]
                k = qk[1][g][h * HD:(h + 1) * HD, klo:klo + (nk - 1) * step + 1:step]
                pe.matmul(s_ps[h][:, first * P:], q, k, start=True, stop=True).then_inc(s_done, 1)

        def turn(pe, g, a, i):
            pe.wait_ge(exp_done, 1 + a * 32 + (2 * i + 2))
            pe.wait_ge(copy_done, 1 + a * 16 + i)
            first = key_range(g, i)[2]
            for h in range(2):
                for b in range(first, 2):
                    mm = pe.transpose(t_ps[:, 2 * h + b, :], probs[:, h, b * P:(b + 1) * P], ident[:, :])
            mm.then_inc(t_done, 1)

        def weigh(pe, g, a, i):
            pe.wait_ge(copy_done, 1 + a * 16 + (i + 1))
            pe.wait_ge(o_done, 1 + a * 16 + i)
            first = key_range(g, i)[2]
            for h in range(2):
                for b in range(first, 2):
                    mm = pe.matmul(o_ps[:, h, :], probsT[:, 2 * h + b, :], v_sb[g][:, i + b - 1, h, :],
                                   start=(b == first), stop=(b == 1))
            mm.then_inc(pv_done, 1)

        def largest(dve, g, a, i):
            if i == 0:
                dve.wait_ge(dist_in, 1 + a * 16 + 16)
            if i % 8 == 0:
                dve.wait_ge(half_out[i // 8], 1 + a * 32)
            dve.wait_ge(exp_done, 1 + a * 32 + 2 * i)
            first = key_range(g, i)[2]
            for h in range(2):
                dve.wait_ge(s_done, 1 + a * 32 + (2 * i + h + 1))
                dve.sem_inc(s_seen, 1)
                dve.tensor_tensor_reduce(scores[:, h, first * P:], s_ps[h][:, first * P:], dist[g][:, h, first * P:],
                                         1.0, 3.0e38, ALU.add, ALU.min,
                                         o_out[:, i, h * 66 + 65:h * 66 + 66]).then_inc(max_done, 1)

        def weights(act, g, a, i):
            act.wait_ge(t_done, 1 + a * 16 + i)
            first = key_range(g, i)[2]
            for h in range(2):
                act.wait_ge(max_done, 1 + a * 32 + (2 * i + h + 1))
                act.activation(probs[:, h, first * P:], scores[:, h, first * P:], ACT.Exp, scale=-1.0,
                               bias=o_out[:, i, h * 66 + 65:h * 66 + 66]).then_inc(exp_done, 1)

        def copy_turned(act, g, a, i):
            act.wait_ge(t_done, 1 + a * 16 + (i + 1))
            act.wait_ge(pv_done, 1 + a * 16 + i)
            first = key_range(g, i)[2]
            view = lambda x: x[:, :, :].rearrange("p (h b) q -> p h b q", b=2)[:, :, first:, :]
            act.copy(view(probsT), view(t_ps)).then_inc(copy_done, 1)

        def leave_sums(dve, a, i):
            dve.wait_ge(pv_done, 1 + a * 16 + (i + 1))
            dve.tensor_copy(o_out[:, i, :].rearrange("p (h d) -> p h d", h=2)[:, :, 0:HD + 1], o_ps[:, :, :]).then_inc(o_done, 1)

        def pe_stage(pe, g, a, ng, n):
            for i in range(BLK):
                if a is not None:
                    score(pe, g, a, i)
                    if i:
                        weigh(pe, g, a, i - 1)
                if n is not None and 0 < i <= UNITS:
                    head_sums(pe, n, i - 1)
                if n is not None and i < UNITS:
                    project_unit(pe, ng, n, i)
                if a is not None:
                    turn(pe, g, a, i)
            if a is not None:
                weigh(pe, g, a, BLK - 1)

        def act_stage(act, g, a, ng, n):
            for i in range(BLK):
                if a is not None:
                    weights(act, g, a, i)
                if n is not None and i:
                    root(act, n, i - 1)
                if n is not None and i < UNITS:
                    square_unit(act, n, i)
                if a is not None:
                    copy_turned(act, g, a, i)

        def dve_stage(dve, g, a, ng, n):
            for i in range(BLK):
                if a is not None:
                    largest(dve, g, a, i)
                    if i:
                        leave_sums(dve, a, i - 1)
                if n is not None and 0 < i <= UNITS:
                    leave_unit(dve, ng, n, i - 1)
            if a is not None:
                leave_sums(dve, a, BLK - 1)

        def store_kv(pool, g, jp, n):
            pool.wait_ge(evac_done, 1 + n * UNITS + UNITS)
            w = (P, 512, SEQ)[g]
            kt, v = qk[1][g], v_sb[g]
            pool.dma_start(dr[f"kT_p{g}"][jp], kt[:, SEQ - w:SEQ]).then_inc(kv_out, 16)
            vb = (v[:, BLK - 1:BLK], v[:, 3:BLK:4], v[:, 0:BLK])[g]
            pool.dma_start(dr[f"v_p{g}"][jp], vb).then_inc(kv_out, 16)
            pool.dma_start(dr[f"kT_s{g}"][jp], kt[:, SEQ:NT]).then_inc(kv_out, 16)
            pool.dma_start(dr[f"v_s{g}"][jp].rearrange("t (h d) -> t h d", h=2), v[0:NS, BLK, :, 0:HD]).then_inc(kv_out, 16)
            pool.dma_start(dr["qT_s"][jp, g], qk[0][g][:, SEQ:NT]).then_inc(kv_out, 16)

        def store_sums(pool, g, jp, a, half):
            pool.wait_ge(o_done, 1 + a * 16 + 8 * (half + 1))
            rows = dr["sums"][g, jp]
            for quad in (2 * half, 2 * half + 1):
                if g == 0:
                    dst = rows.rearrange("(i p) c -> p i c", p=P)[:, 4 * quad:4 * quad + 4]
                elif g == 1:
                    dst = rows.rearrange("(b p r) c -> r p b c", p=P, r=4)[quad]
                else:
                    dst = rows.rearrange("(p i) c -> p i c", i=16)[:, 4 * quad:4 * quad + 4]
                pool.dma_start(dst, o_out[:, 4 * quad:4 * quad + 4, :]).then_inc(half_out[half], 16)

        def load_weights(sp, g, jp, kind):
            sp.dma_start(w_sb[kind][:, :, :], dr["w_qkv"][jp, g, kind]).then_inc(w_in[kind], 16)

        def load_distances(sp, g, jp):
            sp.dma_start(dist[g][:, :, :], dr["dist"][jp, g]).then_inc(dist_in, 16)

        def sp_stage(sp, g, jp, a, ng, njp, n, last):
            mg, mjp = ((ng + 1), njp) if n is not None and ng < 2 else (0, jp if n is None else njp + 1)
            load = n is not None and not last

            def load_after(kind):
                if load:
                    sp.wait_ge(unit_done, 1 + n * UNITS + 5 * (kind + 1))
                    load_weights(sp, mg, mjp, kind)

            if load:
                if a is not None:
                    sp.wait_ge(max_done, 1 + a * 32)
                load_distances(sp, mg, mjp)
            load_after(0)
            if a is not None:
                store_sums(sp, g, jp, a, 0)
            load_after(1)
            load_after(2)
            if a is not None:
                store_sums(sp, g, jp, a, 1)
            if n is not None:
                store_kv(sp, ng, njp, n)

        def stages(eng, stage):
            stage(eng, None, None, None, 0, 0, 0, False)

            def pair(jp, last):
                for g in range(G):
                    ng, njp = ((g + 1), jp) if g < 2 else (0, jp + 1)
                    n = jp * 3 + (g + 1)
                    if last and g == 2:
                        ng = njp = n = None
                    stage(eng, g, jp, jp * 3 + g, ng, njp, n, last and g == 1)

            with eng.Fori(0, PAIRS - 1) as jp:
                pair(jp, False)
            pair(PAIRS - 1, True)

        with nc.Block() as block:
            @block.sync
            def _(sp):
                sp.wait_ge(ones_set, 1 + G)
                sp.dma_start(gains[:, :], dr["qk_gain"]).then_inc(const_in, 16)
                sp.dma_start(ones_h[:, :], dr["ones_h"]).then_inc(const_in, 16)
                load_distances(sp, 0, 0)
                for kind in range(3):
                    load_weights(sp, 0, 0, kind)
                stages(sp, sp_stage)
                sp.wait_ge(kv_out, 1 + 12 * KV)
                sp.wait_ge(half_out[0], 1 + 12 * 32)
                sp.wait_ge(half_out[1], 1 + 12 * 32)

            @block.gpsimd
            def _(pool):
                first_signals(pool, sems)
                for g in range(G):
                    pool.memset(v_sb[g][:, :, :, HD:HD + 1], 1.0).then_inc(ones_set, 1)

            @block.tensor
            def _(pe):
                pe.wait_ge(const_in, 1 + 32)
                pe.wait_ge(ones_set, 1 + G)
                stages(pe, lambda e, g, jp, a, ng, njp, n, last: pe_stage(e, g, a, ng, n))

            @block.scalar
            def _(act):
                act.preload_act_table_set("natural_log_exp_and_others")
                stages(act, lambda e, g, jp, a, ng, njp, n, last: act_stage(e, g, a, ng, n))

            @block.vector
            def _(dve):
                dve.wait_ge(const_in, 1 + 32)
                dve.tensor_scalar(gains[:, 0:1], gains[:, 0:1], -(HD ** -0.5), None, ALU.mult).then_inc(gain_set, 1)
                dve.wait_ge(gain_set, 1 + 1)
                stages(dve, lambda e, g, jp, a, ng, njp, n, last: dve_stage(e, g, a, ng, n))


def phase_sample(nc, t, dr):
    COLS = 3 * CH + P + 3 * ST
    GROUP_OF_BANK = (1, 2, 2, 0)
    QJ = G * HD + 2 * ST
    with ExitStack() as ctx:
        sb = lambda name, *a: ctx.enter_context(nc.sbuf_tensor("sample_" + name, *a))
        ps = lambda name, *a: ctx.enter_context(nc.psum_tensor("sample_" + name, *a))
        sems = []

        def sem(name):
            sems.append(ctx.enter_context(nc.semaphore("sample_" + name)))
            return sems[-1]

        k_sb = [sb(f"k{c}", [P, PAIRS, CH if c < 3 else P], F32) for c in range(4)]
        v_sb = [sb(f"v{b}", [P, KEYS, CH], F32) for b in range(2)]
        v_new = [sb(f"v_new{b}", [G * ST, PAIRS, P], F32) for b in range(2)]
        q_all = sb("q_all", [P, PAIRS, G, NS], F32)
        k_all = sb("k_all", [P, PAIRS, G, NS], F32)
        q_diag = [sb(f"q_diag{b}", [P, PAIRS * QJ], F32) for b in range(2)]
        k_new = [sb(f"k_new{b}", [P, PAIRS, G, ST], F32) for b in range(2)]
        pen = sb("pen", [P, COLS], F32)
        probs = sb("probs", [P, COLS], F32)
        probsT = sb("probsT", [P, KEYS + 1, P], F32)
        least4 = sb("least4", [P, 4], F32)
        least = sb("least", [P, 1], F32)
        total = sb("total", [P, 1], F32)
        inv = sb("inv", [P, 1], F32)
        own, sel = sb("own", [P, CH], F32), sb("sel", [P, 2 * ST], F32)
        o_own = sb("o_own", [P, CH], F32)
        s_ps = [ps(f"s{c}", [P, CH], F32) for c in range(4)]
        t_ps = [ps(f"t{i}", [P, 4, P], F32) for i in range(2)]
        o_ps = ps("o", [P, CH], F32)
        ot_ps = ps("ot", [P, PAIRS, 2 * ST], F32)
        const_in = sem("const_loaded")
        k_in = [sem(f"k{c}_loaded") for c in range(4)]
        v_in = [sem(f"v{b}_loaded") for b in range(2)]
        vn_in = [sem(f"v_new{b}_loaded") for b in range(2)]
        zeroed, q_ready = sem("zeroed"), sem("q_ready")
        bank_done = [sem(f"bank{c}_done") for c in range(4)]
        max_done, least_done, exp_done, inv_done = (sem(n) for n in ("max_done", "least_done", "exp_done", "inv_done"))
        seen = sem("seen")
        t_done, copy_done, pv_done, own_done, ot_done, out_done = (sem(n) for n in
            ("t_done", "copy_done", "pv_done", "own_done", "ot_done", "out_done"))
        bank = lambda c: slice(c * CH, min((c + 1) * CH, COLS))

        with nc.Block() as block:
            @block.gpsimd
            def _(pool):
                first_signals(pool, sems)

            @block.sync
            def _(sp):
                for g in range(G):
                    sp.dma_start(k_all[:, :, g, :], dr[f"kT_s{g}"].rearrange("j p t -> p j t")).then_inc(const_in, 16)
                for j in range(PAIRS):
                    sp.dma_start(q_all[:, j], dr["qT_s"][j].rearrange("g p t -> p g t")).then_inc(const_in, 16)
                sp.dma_start(pen[:, :], dr["pen_s"]).then_inc(const_in, 16)
                sp.dma_start(own[:, :], dr["own_s"]).then_inc(const_in, 16)
                sp.dma_start(sel[:, :], dr["sel_s"]).then_inc(const_in, 16)
                with sp.Fori(0, SB // 2) as i:
                    for b in range(2):
                        for c in range(4):
                            sp.wait_ge(bank_done[c], 1 + i * 2 + b)
                            w = CH if c < 3 else P
                            sp.dma_start(k_sb[c][:, :, :], dr["kT_c"][i * 2 + b, :, :, c * CH:c * CH + w]).then_inc(k_in[c], 16)
                    for b in range(2):
                        sp.wait_ge(pv_done, 1 + i)
                        sp.dma_start(v_sb[b][:, :, :], dr["v_c"][i * 2 + b]).then_inc(v_in[b], 16)
                        for g in range(G):
                            rows = dr[f"v_s{g}"].rearrange("j (b t) c -> b t j c", t=ST)
                            sp.dma_start(v_new[b][g * ST:(g + 1) * ST], rows[i * 2 + b]).then_inc(vn_in[b], 16)

            @block.tensor
            def _(pe):
                with pe.Fori(0, SB // 2) as i:
                    for b in range(2):
                        rows = slice(64 * b, 64 * b + 64)
                        pe.wait_ge(q_ready, 1 + i * 2 + (b + 1))
                        pe.wait_ge(max_done, 1 + i * 4)
                        for c in range(4):
                            g = GROUP_OF_BANK[c]
                            pe.wait_ge(k_in[c], 1 + i * 32 + 16 * (b + 1))
                            w = CH if c < 3 else P
                            for j in range(PAIRS):
                                lhsT = q_diag[b][:, j * G * HD + g * HD:j * G * HD + (g + 1) * HD]
                                mm = pe.matmul(s_ps[c][rows, 0:w], lhsT, k_sb[c][:, j, :], start=(j == 0), stop=(j == PAIRS - 1))
                            if c == 3:
                                for g in range(G):
                                    for j in range(PAIRS):
                                        lhsT = q_diag[b][:, j * G * HD + g * HD:j * G * HD + (g + 1) * HD]
                                        mm = pe.matmul(s_ps[3][rows, P + g * ST:P + (g + 1) * ST], lhsT, k_new[b][:, j, g, :],
                                                       start=(j == 0), stop=(j == PAIRS - 1))
                            mm.then_inc(bank_done[c], 1)
                    pe.wait_ge(exp_done, 1 + i + 1)
                    for r in range(4):
                        pe.wait_ge(copy_done, 1 + i * 4 + max(r - 1, 0))
                        for m in range(4 * r, min(4 * r + 4, KEYS + 1)):
                            n = P if m < KEYS else G * ST
                            mm = pe.transpose(t_ps[r % 2][0:n, m % 4, :], probs[:, m * P:m * P + n], t["ident"][:, :])
                        mm.then_inc(t_done, 1)
                    pe.wait_ge(copy_done, 1 + i * 4 + 4)
                    pe.wait_ge(own_done, 1 + i)
                    for b in range(2):
                        rows = slice(64 * b, 64 * b + 64)
                        pe.wait_ge(v_in[b], 1 + i * 16 + 16)
                        for m in range(KEYS):
                            pe.matmul(o_ps[rows, :], probsT[:, m, rows], v_sb[b][:, m, :], start=(m == 0), stop=False)
                        pe.wait_ge(vn_in[b], 1 + i * 48 + 48)
                        mm = pe.matmul(o_ps[rows, :], probsT[0:G * ST, KEYS, rows],
                                       v_new[b][:, :, :].rearrange("p j c -> p (j c)"), start=False, stop=True)
                    mm.then_inc(pv_done, 1)
                    pe.wait_ge(own_done, 1 + i + 1)
                    pe.wait_ge(out_done, 1 + i)
                    for j in range(PAIRS):
                        mm = pe.matmul(ot_ps[:, j, :], o_own[:, j * P:(j + 1) * P], sel[:, :], start=True, stop=True)
                    mm.then_inc(ot_done, 1)

            @block.scalar
            def _(act):
                act.preload_act_table_set("natural_log_exp_and_others")
                with act.Fori(0, SB // 2) as i:
                    act.wait_ge(least_done, 1 + i + 1)
                    act.wait_ge(inv_done, 1 + i)
                    act.activation(probs[:, :], probs[:, :], ACT.Exp, scale=-1.0, bias=least[:, 0:1],
                                   accum_out=total[:, 0:1]).then_inc(exp_done, 1)
                    for r in range(4):
                        act.wait_ge(t_done, 1 + i * 4 + (r + 1))
                        act.wait_ge(pv_done, 1 + i)
                        n = 4 if r < 3 else 1
                        act.copy(probsT[:, 4 * r:4 * r + n, :], t_ps[r % 2][:, 0:n, :]).then_inc(copy_done, 1) if r < 3 else \
                            act.copy(probsT[:, 12:13, :], t_ps[1][:, 0:1, :])
                    act.copy(probsT[0:G * ST, KEYS, :], t_ps[1][0:G * ST, 1, :]).then_inc(copy_done, 1)

            @block.vector
            def _(dve):
                for b in range(2):
                    dve.memset(q_diag[b][:, :], 0.0).then_inc(zeroed, 1)
                dve.wait_ge(zeroed, 1 + 2)
                dve.wait_ge(const_in, 1 + 16 * (G + PAIRS + 3))
                with dve.Fori(0, SB // 2) as i:
                    for b in range(2):
                        dve.wait_ge(bank_done[3], 1 + i * 2)
                        new = bass.ds(i * 2 * ST + b * ST, ST)
                        for h in range(2):
                            rows = slice(HD * h, HD * (h + 1))
                            dst = q_diag[b][rows, :].rearrange("p (j x) -> p j x", x=QJ)[:, :, 0:G * HD]
                            dst = dst.rearrange("p j (g y) -> p j g y", y=HD)[:, :, :, h * ST:(h + 1) * ST]
                            dve.tensor_copy(dst, q_all[rows, :, :, new])
                        dve.tensor_copy(k_new[b][:, :, :, :], k_all[:, :, :, new]).then_inc(q_ready, 1)
                    dve.wait_ge(t_done, 1 + i * 4)
                    for c in range(4):
                        dve.wait_ge(bank_done[c], 1 + i * 2 + 2)
                        dve.sem_inc(seen, 1)
                        n = bank(c).stop - bank(c).start
                        dve.tensor_tensor_reduce(probs[:, bank(c)], s_ps[c][:, 0:n], pen[:, bank(c)], 1.0, 3.0e38,
                                                 ALU.add, ALU.min, least4[:, c:c + 1]).then_inc(max_done, 1)
                    dve.wait_ge(max_done, 1 + i * 4 + 4)
                    dve.tensor_reduce(least[:, :], least4[:, :], AX.X, ALU.min).then_inc(least_done, 1)
                    dve.wait_ge(exp_done, 1 + i + 1)
                    dve.reciprocal(inv[:, :], total[:, :]).then_inc(inv_done, 1)
                    dve.wait_ge(inv_done, 1 + i + 1)
                    dve.wait_ge(pv_done, 1 + i + 1)
                    dve.scalar_tensor_tensor(out=o_own[:, :], in0=o_ps[:, :], scalar=inv[:, 0:1], in1=own[:, :],
                                             op0=ALU.mult, op1=ALU.mult).then_inc(own_done, 1)
                    dve.wait_ge(ot_done, 1 + i + 1)
                    dve.tensor_copy(t["oT_s"][:, :, bass.ds(i * 2 * ST, 2 * ST)], ot_ps[:, :, :]).then_inc(out_done, 1)


def phase_hgrn(nc, t, dr):
    with ExitStack() as ctx:
        sb = lambda name, *a: ctx.enter_context(nc.sbuf_tensor("hgrn_" + name, *a))
        ps = lambda name, *a: ctx.enter_context(nc.psum_tensor("hgrn_" + name, *a))
        sems = []

        def sem(name):
            sems.append(ctx.enter_context(nc.semaphore("hgrn_" + name)))
            return sems[-1]

        hT = t["hT"]
        w_sb = [sb(f"w{k}", [P, KD, P], F32) for k in range(3)]
        q_neg = sb("q_neg", [P, NT], F32)
        f_sb = sb("f", [P, NT], F32)
        v_sb = sb("v", [P, BLK + 1, P], F32)
        e_u = [sb(f"e_u{k}", [P, CH], F32) for k in range(2)]
        log_f, b_sum, e_b, q_in = (sb(n, [P, CH], F32) for n in ("log_f", "b_sum", "e_b", "q_in"))
        d_sb = [sb(f"d{i}", [P, CH], F32) for i in range(2)]
        x_sb = [sb(f"x{i}", [P, CH], F32) for i in range(2)]
        keys, k_out = sb("keys", [P, CH], F32), sb("k_out", [P, CH], F32)
        k_turned = sb("k_turned", [P, 4, P], F32)
        att = sb("att", [P, 4, P], F32)
        state = sb("state", [P, 5, P], F32)
        state_o = sb("state_o", [P, P], F32)
        s0 = sb("s0", [P, SB, P], F32)
        s_new = sb("s_new", [P, SB, P], F32)
        v_seq = sb("v_seq", [NS, SB, P], F32)
        sq, log_ms, rstd = sb("sq", [P, CH], F32), sb("log_ms", [P, CH], F32), sb("rstd", [P, CH], F32)
        level = sb("level", [P, 8, P], U32)
        seq = sb("seq", [NS, SB], F32)
        ones_i, ones = sb("ones_i", [P, P], F32), sb("ones", [P, P], F32)
        o_gain = sb("o_gain", [P, 1], F32)
        lb2, lb_e = sb("lb2", [P, 2, BH], F32), sb("lb_e", [P, 2, BH], F32)
        lb_s, lb, lb1 = (sb(n, [P, BH], F32) for n in ("lb_s", "lb", "lb1"))
        u_ps = [ps(f"u{k}", [P, CH], F32) for k in range(3)]
        l_ps = [ps(f"l{i}", [P, 4, P], F32) for i in range(2)]
        kd_ps = ps("kd", [P, 4, P], F32)
        o_ps = ps("o", [P, CH], F32)
        ss_ps = ps("ss", [P, CH], F32)
        const_in = sem("const_loaded")
        w_in = [sem(f"w{k}_loaded") for k in range(3)]
        s0_in, state_out, s_new_out = sem("s0_loaded"), sem("state_stored"), sem("s_new_stored")
        names = ("lb_steps unit_done eu_done min_done log1_done max_done sig_done evac_done logf_done b_done eb_done qin_done d_done e_done "
                 "x_done xk_done l_done pred_done kt_done kcopy_done ds_done chain_done carry_done o_done sq_done ss_done "
                 "log_done r_done out_done seen vseq_done dss_done snew_half snew_done stateo_done ones_set").split()
        s = {n: sem(n) for n in names}

        def at(h, j, quad, sample, k):
            return h * (4 * quad + sample) + (j * quad + k)

        width = lambda j: CH if j < 4 else NS
        cols = lambda j: slice(j * CH, j * CH + width(j))
        span = lambda j: (4, P) if j < 4 else (SB, ST)
        levels = lambda j: 7 if j < 4 else 3
        RND, XS, LV = (8, 4), (8, 4), (8, 4)

        def project(pe, h, j, kind):
            if j or not isinstance(h, int):
                pe.wait_ge(s["evac_done"], 1 + at(h, j, 3, 3, kind - 2))
            pe.wait_ge(w_in[kind], 1 + h * 16 + 16)
            u = u_ps[kind]
            if kind < 2:
                for k in range(KD):
                    mm = pe.matmul(u[:, 0:width(j)], w_sb[kind][:, k, :], hT[:, k, cols(j)], start=(k == 0), stop=(k == KD - 1))
            else:
                for b in range(4 if j < 4 else 1):
                    n = P if j < 4 else NS
                    lo = j * CH + b * P
                    for k in range(KD):
                        mm = pe.matmul(u[0:n, b * P:(b + 1) * P], hT[:, k, lo:lo + n], w_sb[2][:, k, :],
                                       start=(k == 0), stop=(k == KD - 1))
            mm.then_inc(s["unit_done"], 1)

        def gate_on_act(act, h, j, kind, part):
            n = width(j)
            e = e_u[kind][:, 0:n]
            if part == 0:
                act.wait_ge(s["unit_done"], 1 + at(h, j, 3, 3, kind + 1))
                act.wait_ge(s["evac_done"], 1 + at(h, j, 3, 3, 0))
                act.activation(e, u_ps[kind][:, 0:n], ACT.Exp, scale=-1.0).then_inc(s["eu_done"], 1)
            elif part == 1:
                act.wait_ge(s["min_done"], 1 + at(h, j, 2, 2, kind + 1))
                act.activation(e, e, ACT.Ln, bias=1.0).then_inc(s["log1_done"], 1)
            else:
                act.wait_ge(s["max_done"], 1 + at(h, j, 2, 2, kind + 1))
                act.activation(e, e, ACT.Exp, scale=-1.0).then_inc(s["sig_done"], 1)

        def gate_on_dve(dve, h, j, kind, part):
            n = width(j)
            e = e_u[kind][:, 0:n]
            if part == 0:
                dve.wait_ge(s["eu_done"], 1 + at(h, j, 2, 2, kind + 1))
                dve.tensor_scalar(e, e, 1.0e18, None, ALU.min).then_inc(s["min_done"], 1)
            elif part == 1:
                dve.wait_ge(s["log1_done"], 1 + at(h, j, 2, 2, kind + 1))
                dve.scalar_tensor_tensor(out=e, in0=u_ps[kind][:, 0:n], scalar=-1.0, in1=e,
                                         op0=ALU.mult, op1=ALU.max).then_inc(s["max_done"], 1)
            elif kind == 0:
                dve.wait_ge(s["sig_done"], 1 + at(h, j, 2, 2, 1))
                dve.scalar_tensor_tensor(out=q_neg[:, cols(j)], in0=u_ps[0][:, 0:n], scalar=-1.0, in1=e,
                                         op0=ALU.mult, op1=ALU.mult).then_inc(s["evac_done"], 1)
            else:
                dve.wait_ge(s["sig_done"], 1 + at(h, j, 2, 2, 2))
                dve.tensor_scalar(f_sb[:, cols(j)], e, col(lb1, h), col(lb, h), ALU.mult, ALU.add).then_inc(s["evac_done"], 1)

        def evacuate_values(dve, h, j):
            dve.wait_ge(s["unit_done"], 1 + at(h, j, 3, 3, 3))
            if j < 4:
                dve.tensor_copy(v_sb[:, 4 * j:4 * j + 4, :], u_ps[2][:, :].rearrange("p (b c) -> p b c", b=4)) \
                   .then_inc(s["evac_done"], 1)
            else:
                dve.tensor_copy(v_sb[0:NS, BLK, :], u_ps[2][0:NS, 0:P]).then_inc(s["evac_done"], 1)

        ACT_PARTS = {2: ((0, 0),), 3: ((0, 1),), 4: ((0, 2),), 5: ((1, 0),), 6: ((1, 1),), 7: ((1, 2),)}
        ACT_PARTS_S = {2: ((0, 0),), 3: ((0, 1), (0, 2), (1, 0), (1, 1), (1, 2))}
        DVE_PARTS = {2: ((0, 0),), 3: ((0, 1),), 5: ((0, 2), (1, 0)), 6: ((1, 1),)}
        DVE_PARTS_S = {2: ((0, 0),), 3: ((0, 1),)}
        DVE_LAST, DVE_LAST_S = ((1, 2),), ((0, 2), (1, 0), (1, 1), (1, 2))

        def col(x, h):
            return x[:, h:h + 1] if isinstance(h, int) else x[:, bass.ds(h, 1)]

        def halves(x, j, l):
            v = x[:, 0:width(j)].rearrange("p (n w) -> p n w", w=1 << l)
            return v[:, :, 0:1 << (l - 1)], v[:, :, 1 << (l - 1):]

        def difference(dve, h, j, r):
            d = d_sb[r % 2]
            dve.wait_ge(s["x_done"], 1 + at(h, j, *XS, r - 1 if r > 1 else 0))
            dve.wait_ge(s["xk_done"], 1 + at(h, j, *RND, r - 1 if r > 1 else 0))
            if r == 0:
                n, w = span(j)
                v = b_sum[:, 0:width(j)].rearrange("p (n w) -> p n w", w=w)
                dve.tensor_tensor(d[:, 0:width(j)].rearrange("p (n w) -> p n w", w=w),
                                  v[:, :, w - 1:w].broadcast_to([P, n, w]), v, ALU.subtract).then_inc(s["d_done"], 1)
                return
            (d1, d2), (b1, b2) = halves(d, j, r), halves(b_sum, j, r)
            n, w = width(j) >> r, 1 << (r - 1)
            mid = b1[:, :, w - 1:w].broadcast_to([P, n, w])
            dve.tensor_tensor(d1, mid, b1, ALU.subtract)
            dve.tensor_tensor(d2, b2, mid, ALU.subtract).then_inc(s["d_done"], 1)

        def exponent(act, h, j, r):
            d = d_sb[r % 2][:, 0:width(j)]
            act.wait_ge(s["d_done"], 1 + at(h, j, *RND, r + 1))
            act.activation(d, d, ACT.Exp).then_inc(s["e_done"], 1)

        def scaled_keys(pool, h, j, r):
            pool.wait_ge(s["e_done"], 1 + at(h, j, *RND, r + 1))
            if r == 0:
                out, k, d = (x[:, 0:width(j)] for x in (k_out, keys, d_sb[0]))
                pool.wait_ge(s["x_done"], 1 + at(h, j, *XS, 1))
                pool.wait_ge(s["kt_done"], 1 + at(h, j, 1, 1, 0))
            else:
                out, k, d = (halves(x, j, r)[0] for x in (x_sb[r % 2], keys, d_sb[r % 2]))
                pool.wait_ge(s["l_done"], 1 + at(h, j, *LV, r - 1))
            pool.tensor_tensor(out, k, d, ALU.mult).then_inc(s["xk_done"], 1)

        def scaled_queries(dve, h, j, r):
            dve.wait_ge(s["e_done"], 1 + at(h, j, *RND, r + 1))
            dve.wait_ge(s["l_done"], 1 + at(h, j, *LV, r - 1))
            x2, d2, q2 = (halves(v, j, r)[1] for v in (x_sb[r % 2], d_sb[r % 2], q_neg[:, cols(j)]))
            dve.tensor_tensor(x2, q2, d2, ALU.mult).then_inc(s["x_done"], 1)

        def level_product(pe, h, j, l):
            pe.wait_ge(s["x_done"], 1 + at(h, j, *XS, l + 1))
            if l:
                pe.wait_ge(s["xk_done"], 1 + at(h, j, *RND, l + 1))
            if l == 0 and j == 0:
                pe.wait_ge(s["snew_done"], 1 + h)
            pe.wait_ge(s["pred_done"], 1 + at(h, j, *LV, max(l - 1, 0)))
            n = 4 if j < 4 else 1
            w = P if j < 4 else NS
            for c in range(n):
                x = (x_sb[l % 2] if l else keys)[:, c * w:(c + 1) * w]
                y = x if l else q_neg[:, j * CH + c * w:j * CH + (c + 1) * w]
                mm = pe.matmul(l_ps[l % 2][0:w, c, 0:w], x, y, start=True, stop=True)
            mm.then_inc(s["l_done"], 1)

        def take_level(dve, h, j, l):
            dve.wait_ge(s["l_done"], 1 + at(h, j, *LV, l + 1))
            n, w = (4, P) if j < 4 else (1, NS)
            src, dst = l_ps[l % 2][0:w, 0:n, 0:w], att[0:w, 0:n, 0:w]
            if l == 0:
                dve.wait_ge(s["o_done"], 1 + at(h, j, 1, 1, 0))
                dve.tensor_tensor(dst, src, t["ident"][0:w, 0:w].unsqueeze(1).broadcast_to([w, n, w]), ALU.mult) \
                   .then_inc(s["pred_done"], 1)
            else:
                dve.wait_ge(s["pred_done"], 1 + at(h, j, *LV, l))
                dve.sem_inc(s["seen"], 1)
                dve.copy_predicated(dst, level[0:w, l:l + 1, 0:w].broadcast_to([w, n, w]), src).then_inc(s["pred_done"], 1)

        def turn_keys(pe, h, j):
            pe.wait_ge(s["xk_done"], 1 + at(h, j, *RND, 1))
            pe.wait_ge(s["chain_done"], 1 + at(h, j, 4, 0, 0))
            pe.wait_ge(s["kcopy_done"], 1 + at(h, j, 1, 1, 0))
            for c in range(4 if j < 4 else 1):
                mm = pe.transpose(kd_ps[:, c, :], k_out[:, c * P:(c + 1) * P], t["ident"][:, :])
            mm.then_inc(s["kt_done"], 1)

        def increments(pe, h, j):
            pe.wait_ge(s["kcopy_done"], 1 + at(h, j, 1, 1, 1))
            if j < 4:
                for c in range(4):
                    mm = pe.matmul(kd_ps[:, c, :], k_turned[:, c, :], v_sb[:, 4 * j + c, :], start=True, stop=True)
            else:
                pe.wait_ge(s["vseq_done"], 1 + h + 1)
                pe.wait_ge(s["pred_done"], 1 + at(h, j, *LV, 4))
                for b in range(2):
                    mm = pe.matmul(l_ps[b][:, :, :], k_turned[0:NS, 0, :],
                                   v_seq[:, 4 * b:4 * b + 4, :], start=True, stop=True)
            mm.then_inc(s["ds_done"], 1)

        def outputs(pe, h, j):
            pe.wait_ge(s["pred_done"], 1 + at(h, j, *LV, LV[j == 4]))
            pe.wait_ge(s["qin_done"], 1 + at(h, j, 1, 1, 1))
            pe.wait_ge(s["out_done"], 1 + at(h, j, 1, 1, 0))
            if j < 4:
                pe.wait_ge(s["chain_done"], 1 + at(h, j, 4, 0, 3))
                for c in range(4):
                    o = o_ps[:, c * P:(c + 1) * P]
                    pe.matmul(o, v_sb[:, 4 * j + c, :], att[:, c, :], start=True, stop=False)
                    mm = pe.matmul(o, state[:, c, :], q_in[:, c * P:(c + 1) * P], start=False, stop=True)
            else:
                pe.wait_ge(s0_in, 1 + h * 16 + 16)
                pe.matmul(o_ps[:, 0:NS], v_sb[0:NS, BLK, :], att[0:NS, 0, 0:NS], start=True, stop=True,
                          skip_group_check=True)
                for b in range(SB):
                    mm = pe.matmul(o_ps[:, b * ST:(b + 1) * ST], s0[:, b, :], q_in[:, b * ST:(b + 1) * ST],
                                   start=False, stop=True, skip_group_check=True)
            mm.then_inc(s["o_done"], 1)

        def pe_step(pe, h, j, hp, jp):
            if h is None:
                for kind in range(3):
                    project(pe, hp, jp, kind)
                return
            L = levels(j)
            level_at = {2: (0, 1), 3: (2, 3, 4), 4: (5, 6), 5: (7,)} if j < 4 else {2: (0, 1), 3: (2,), 4: (), 5: (3,)}
            if hp is not None:
                project(pe, hp, jp, 0)
            level_product(pe, h, j, 0)
            turn_keys(pe, h, j)
            level_product(pe, h, j, 1)
            if hp is not None:
                project(pe, hp, jp, 1)
            for l in level_at[3]:
                level_product(pe, h, j, l)
            if j < 4:
                increments(pe, h, j)
            for l in level_at[4]:
                level_product(pe, h, j, l)
            if hp is not None:
                project(pe, hp, jp, 2)
            for l in level_at[5]:
                level_product(pe, h, j, l)
            if j == 4:
                increments(pe, h, j)
            outputs(pe, h, j)
            pe.wait_ge(s["sq_done"], 1 + at(h, j, 1, 1, 1))
            pe.wait_ge(s["log_done"], 1 + at(h, j, 1, 1, 0))
            pe.matmul(ss_ps[:, 0:width(j)], ones_i[:, :], sq[:, 0:width(j)], start=True, stop=True).then_inc(s["ss_done"], 1)

        def act_step(act, h, j, hp, jp):
            if h is None:
                for kind in range(2):
                    for part in range(3):
                        gate_on_act(act, hp, jp, kind, part)
                return
            n = width(j)
            act.wait_ge(s["evac_done"], 1 + at(h, j, 3, 3, 2))
            act.wait_ge(s["b_done"], 1 + at(h, j, 1, 1, 0))
            act.activation(log_f[:, 0:n], f_sb[:, cols(j)], ACT.Ln).then_inc(s["logf_done"], 1)
            act.wait_ge(s["b_done"], 1 + at(h, j, 1, 1, 1))
            act.wait_ge(s["chain_done"], 1 + at(h, j, 4, 0, 0))
            act.wait_ge(s["snew_half"], 1 + h)
            act.activation(e_b[:, 0:n], b_sum[:, 0:n], ACT.Exp).then_inc(s["eb_done"], 1)
            exponent(act, h, j, 0)
            L = levels(j)
            for r in range(1, L + 1):
                exponent(act, h, j, r)
                if r == 1:
                    act.wait_ge(s["kt_done"], 1 + at(h, j, 1, 1, 1))
                    if j < 4:
                        act.copy(k_turned[:, :, :], kd_ps[:, :, :]).then_inc(s["kcopy_done"], 1)
                    else:
                        act.copy(k_turned[0:NS, 0, :], kd_ps[0:NS, 0, :]).then_inc(s["kcopy_done"], 1)
                for kind, part in (ACT_PARTS if j < 4 else ACT_PARTS_S).get(r, ()) if hp is not None else ():
                    gate_on_act(act, hp, jp, kind, part)
            act.wait_ge(s["o_done"], 1 + at(h, j, 1, 1, 1))
            act.activation(sq[:, 0:n], o_ps[:, 0:n], ACT.Square).then_inc(s["sq_done"], 1)
            act.wait_ge(s["ss_done"], 1 + at(h, j, 1, 1, 1))
            act.activation(log_ms[:, 0:n], ss_ps[:, 0:n], ACT.Ln, bias=t["eps"][:, 0:1]).then_inc(s["log_done"], 1)
            act.wait_ge(s["log_done"], 1 + at(h, j, 1, 1, 1))
            act.wait_ge(s["out_done"], 1 + at(h, j, 1, 1, 0))
            act.activation(rstd[:, 0:n], log_ms[:, 0:n], ACT.Exp, scale=-0.5).then_inc(s["r_done"], 1)

        def write_output(dve, h, j):
            dve.wait_ge(s["r_done"], 1 + at(h, j, 1, 1, 1))
            n = width(j)
            dst = t["oT_b"][:, h, cols(j)] if isinstance(h, int) else \
                t["oT_b"][:, bass.ds(h, 1), cols(j)].rearrange("p a c -> p (a c)")
            dve.scalar_tensor_tensor(out=dst, in0=o_ps[:, 0:n], scalar=o_gain[:, 0:1], in1=rstd[:, 0:n],
                                     op0=ALU.mult, op1=ALU.mult).then_inc(s["out_done"], 1)

        def dve_step(dve, h, j, hp, jp):
            if h is None:
                for kind in range(2):
                    for part in range(3):
                        gate_on_dve(dve, hp, jp, kind, part)
                evacuate_values(dve, hp, jp)
                return
            n = width(j)
            L = levels(j)
            dve.wait_ge(s["logf_done"], 1 + at(h, j, 1, 1, 1))
            dve.wait_ge(s["d_done"], 1 + at(h, j, *RND, 0))
            nch, w = span(j)
            for c in range(nch):
                scan = dve.tensor_tensor_scan(b_sum[:, c * w:(c + 1) * w], ones[:, 0:w], log_f[:, c * w:(c + 1) * w], 0.0,
                                              ALU.mult, ALU.add)
            scan.then_inc(s["b_done"], 1)
            dve.wait_ge(s["b_done"], 1 + at(h, j, 1, 1, 1))
            difference(dve, h, j, 0)
            difference(dve, h, j, 1)
            dve.tensor_scalar(keys[:, 0:n], f_sb[:, cols(j)], -1.0, None, ALU.add).then_inc(s["x_done"], 1)
            difference(dve, h, j, 2)
            dve.wait_ge(s["eb_done"], 1 + at(h, j, 1, 1, 1))
            if j < 4:
                dve.tensor_tensor(q_in[:, 0:n], q_neg[:, cols(j)], e_b[:, 0:n], ALU.mult).then_inc(s["qin_done"], 1)
            else:
                dve.scalar_tensor_tensor(out=q_in[:, 0:n], in0=q_neg[:, cols(j)], scalar=-1.0, in1=e_b[:, 0:n],
                                         op0=ALU.mult, op1=ALU.mult).then_inc(s["qin_done"], 1)
            for r in range(1, L + 1):
                scaled_queries(dve, h, j, r)
                take_level(dve, h, j, r - 1)
                if r + 2 <= L:
                    difference(dve, h, j, r + 2)
                for kind, part in (DVE_PARTS if j < 4 else DVE_PARTS_S).get(r, ()) if hp is not None else ():
                    gate_on_dve(dve, hp, jp, kind, part)
                if r == 4:
                    chain(dve, h, j)
            if j == 4:
                dve.wait_ge(s["o_done"], 1 + at(h, j, 1, 1, 0))
                dve.tensor_tensor(v_seq[:, :, :], v_sb[0:NS, BLK, :].unsqueeze(1).broadcast_to([NS, SB, P]),
                                  seq[:, :].unsqueeze(2).broadcast_to([NS, SB, P]), ALU.mult).then_inc(s["vseq_done"], 1)
            take_level(dve, h, j, L)
            if hp is not None:
                for kind, part in DVE_LAST if j < 4 else DVE_LAST_S:
                    gate_on_dve(dve, hp, jp, kind, part)
                evacuate_values(dve, hp, jp)
            if j == 4:
                new_states(dve, h)
            write_output(dve, h, j)
            if j < 4:
                dve.tensor_copy(state[:, 0, :], state[:, 4, :]).then_inc(s["carry_done"], 1)
                dve.wait_ge(s["carry_done"], 1 + h * 5 + (j + 1))
            if j == 3:
                dve.wait_ge(state_out, 1 + h * 16)
                dve.tensor_scalar(state_o[:, :], state[:, 4, :], -1.0, None, ALU.mult).then_inc(s["stateo_done"], 1)
            if j == 4:
                dve.memset(state[:, 0, :], 0.0).then_inc(s["carry_done"], 1)
                dve.wait_ge(s["carry_done"], 1 + h * 5 + 5)

        def pool_step(pool, h, j, hp, jp):
            for r in range(levels(j) + 1 if h is not None else 0):
                scaled_keys(pool, h, j, r)

        def chain(dve, h, j):
            if j == 4:
                return
            dve.wait_ge(s["ds_done"], 1 + at(h, j, 1, 1, 1))
            for c in range(4):
                dve.scalar_tensor_tensor(out=state[:, c + 1, :], in0=state[:, c, :], scalar=e_b[:, c * P + P - 1:c * P + P],
                                         in1=kd_ps[:, c, :], op0=ALU.mult, op1=ALU.add).then_inc(s["chain_done"], 1)
                dve.wait_ge(s["chain_done"], 1 + at(h, j, 4, 0, c + 1))

        def new_states(dve, h):
            dve.wait_ge(s0_in, 1 + h * 16 + 16)
            dve.wait_ge(s_new_out, 1 + h * 16)
            decay = e_b[:, ST - 1:NS:ST].unsqueeze(2).broadcast_to([P, SB, P])
            dve.tensor_tensor(s_new[:, :, :], s0[:, :, :], decay, ALU.mult).then_inc(s["snew_half"], 1)
            dve.wait_ge(s["snew_half"], 1 + h + 1)
            dve.wait_ge(s["ds_done"], 1 + at(h, 4, 1, 1, 1))
            for b in range(2):
                part = s_new[:, 4 * b:4 * b + 4, :]
                last = dve.tensor_tensor(part, part, l_ps[b][:, :, :], ALU.subtract)
            last.then_inc(s["snew_done"], 1)

        def sp_step(sp, h, j, hp, jp):
            if h is None:
                return
            if j == 0:
                for kind in range(3):
                    if hp is not None and h is not LAST:
                        sp.wait_ge(s["unit_done"], 1 + at(h, 4, 3, 3, kind + 1))
                        sp.dma_start(w_sb[kind][:, :, :], dr["w_b"][h + 1, kind]).then_inc(w_in[kind], 16)
                sp.wait_ge(s["out_done"], 1 + at(h, 0, 1, 1, 0))
                sp.dma_start(s0[:, :, :], dr["state"][h]).then_inc(s0_in, 16)
            if j == 3:
                sp.wait_ge(s["stateo_done"], 1 + h + 1)
                sp.dma_start(dr["state_p"][h], state_o[:, :]).then_inc(state_out, 16)
            if j == 4:
                sp.wait_ge(s["snew_done"], 1 + h + 1)
                sp.dma_start(dr["state_s"][h], s_new[:, :, :]).then_inc(s_new_out, 16)

        LAST = BH - 1

        def heads(eng, step):
            for j in range(4):
                step(eng, None, None, 0, j)

            def head(h):
                step(eng, h, 0, h, 4)
                for j in range(1, 5):
                    step(eng, h, j, *((h + 1, j - 1) if h is not LAST else (None, None)))

            with eng.Fori(0, LAST) as h:
                head(h)
            head(LAST)

        with nc.Block() as block:
            @block.gpsimd
            def _(pool):
                first_signals(pool, sems)
                heads(pool, pool_step)

            @block.sync
            def _(sp):
                for dst, src in ((level[:, :, :], "level"), (seq[:, :], "seq_s"), (ones_i[:, :], "ones_i"),
                                 (o_gain[:, :], "o_gain"), (lb2[:, :, :], "lb")):
                    sp.dma_start(dst, dr[src]).then_inc(const_in, 16)
                for kind in range(3):
                    sp.dma_start(w_sb[kind][:, :, :], dr["w_b"][0, kind]).then_inc(w_in[kind], 16)
                heads(sp, sp_step)
                sp.wait_ge(state_out, 1 + 16 * BH)
                sp.wait_ge(s_new_out, 1 + 16 * BH)

            @block.tensor
            def _(pe):
                pe.wait_ge(const_in, 1 + 80)
                heads(pe, pe_step)

            @block.scalar
            def _(act):
                act.preload_act_table_set("natural_log_exp_and_others")
                act.wait_ge(s["lb_steps"], 1 + 2)
                act.activation(lb_e[:, :, :], lb2[:, :, :], ACT.Exp).then_inc(s["lb_steps"], 1)
                heads(act, act_step)

            @block.vector
            def _(dve):
                dve.memset(ones[:, :], 1.0).then_inc(s["ones_set"], 1)
                dve.memset(state[:, 0, :], 0.0).then_inc(s["ones_set"], 1)
                dve.wait_ge(s["ones_set"], 1 + 2)
                dve.wait_ge(const_in, 1 + 80)
                dve.tensor_tensor(lb_s[:, :], lb2[:, 0, :], lb2[:, 1, :], ALU.max).then_inc(s["lb_steps"], 1)
                dve.wait_ge(s["lb_steps"], 1 + 1)
                dve.tensor_tensor(lb2[:, :, :], lb2[:, :, :], lb_s[:, :].unsqueeze(1).broadcast_to([P, 2, BH]),
                                  ALU.subtract).then_inc(s["lb_steps"], 1)
                dve.wait_ge(s["lb_steps"], 1 + 3)
                dve.tensor_tensor(lb_s[:, :], lb_e[:, 0, :], lb_e[:, 1, :], ALU.add).then_inc(s["lb_steps"], 1)
                dve.wait_ge(s["lb_steps"], 1 + 4)
                dve.reciprocal(lb_s[:, :], lb_s[:, :]).then_inc(s["lb_steps"], 1)
                dve.wait_ge(s["lb_steps"], 1 + 5)
                dve.tensor_tensor(lb[:, :], lb_e[:, 0, :], lb_s[:, :], ALU.mult).then_inc(s["lb_steps"], 1)
                dve.wait_ge(s["lb_steps"], 1 + 6)
                dve.tensor_scalar(lb1[:, :], lb[:, :], -1.0, 1.0, ALU.mult, ALU.add).then_inc(s["lb_steps"], 1)
                dve.wait_ge(s["lb_steps"], 1 + 7)
                heads(dve, dve_step)


def phase_join(nc, t, dr):
    UNITS = 10
    UNITS_OF_STEP = ((0,), (1,), (2,), (3, 4), (5,), (6,), (7,), (8, 9))
    SMALL, STEPS = 7, 5
    with ExitStack() as ctx:
        sb = lambda name, *a: ctx.enter_context(nc.sbuf_tensor("join_" + name, *a))
        ps = lambda name, *a: ctx.enter_context(nc.psum_tensor("join_" + name, *a))
        sems = []

        def sem(name):
            sems.append(ctx.enter_context(nc.semaphore("join_" + name)))
            return sems[-1]

        hT, oT_a, oT_b = t["hT"], t["oT_a"], t["oT_b"]
        rows = [sb(f"rows{i}", [P, G * 8, HD + 2], F32) for i in range(2)]
        w_z = [sb(f"w_z{i}", [P, KD, P], F32) for i in range(2)]
        least, den, inv = sb("least", [P, 8], F32), sb("den", [P, G * 8], F32), sb("inv", [P, 8], F32)
        wgt = sb("wgt", [P, G * 8], F32)
        joined = [sb(f"joined{i}", [P, 8, HD], F32) for i in range(2)]
        part = sb("part", [P, 8, HD], F32)
        gate_buf, silu = sb("gate_buf", [P, CH], F32), sb("silu", [P, CH], F32)
        z_ps = [ps(f"z{i}", [P, CH], F32) for i in range(2)]
        t_ps = [ps(f"t{i}", [P, 4, P], F32) for i in range(2)]
        rows_in = [sem(f"rows{i}_loaded") for i in range(2)]
        w_in = [sem(f"w{i}_loaded") for i in range(2)]
        diff_done, e_done, small, sums, t_done, copy_done, s_copied = (sem(n) for n in
            ("diff_done", "e_done", "small", "sums", "t_done", "copy_done", "s_copied"))
        z_done, eu_done, one_done, rec_done, silu_done, z_used = (sem(n) for n in
            ("z_done", "eu_done", "one_done", "rec_done", "silu_done", "z_used"))

        def cols(u):
            c = u % 5
            return slice(c * CH, c * CH + (CH if c < NCH else NS))

        def width(u):
            return CH if u % 5 < NCH else NS

        def project_z(pe, n0, i, u, loaded):
            pe.wait_ge(z_used, 1 + i * UNITS + (n0 + max(u - 1, 0)))
            if u % 5 == 0:
                pe.wait_ge(w_in[u // 5], 1 + i * 16 + loaded)
            for k in range(KD):
                mm = pe.matmul(z_ps[u % 2][:, 0:width(u)], w_z[u // 5][:, k, :], hT[:, k, cols(u)],
                               start=(k == 0), stop=(k == KD - 1))
            mm.then_inc(z_done, 1)

        def exp_z(act, n0, i, u):
            act.wait_ge(z_done, 1 + i * UNITS + (n0 + u + 1))
            act.wait_ge(z_used, 1 + i * UNITS + (n0 + u))
            act.activation(gate_buf[:, 0:width(u)], z_ps[u % 2][:, 0:width(u)], ACT.Exp, scale=-1.0).then_inc(eu_done, 1)

        def apply_z(dve, n0, i, u, x):
            nth, w = i * UNITS + (n0 + u + 1), width(u)
            e = gate_buf[:, 0:w]
            dve.wait_ge(eu_done, 1 + nth)
            dve.tensor_scalar(e, e, 1.0, None, ALU.add).then_inc(one_done, 1)
            dve.wait_ge(one_done, 1 + nth)
            dve.reciprocal(e, e).then_inc(rec_done, 1)
            dve.wait_ge(rec_done, 1 + nth)
            dve.tensor_tensor(silu[:, 0:w], z_ps[u % 2][:, 0:w], e, ALU.mult).then_inc(silu_done, 1)
            dve.wait_ge(silu_done, 1 + nth)
            dst = x[:, bass.ds(i * 2 + u // 5, 1), cols(u)].rearrange("p a c -> p (a c)")
            dve.tensor_tensor(dst, dst, silu[:, 0:w], ALU.mult).then_inc(z_used, 1)

        def join(dve, i, j):
            r, out = rows[j % 2], joined[j % 2]
            of = lambda x, g: x[:, 8 * g:8 * g + 8]
            neg_max, den_of = r[:, :, HD + 1], r[:, :, HD]
            n = [0]

            def then_wait(ins, sem, per_block):
                n[0] += 1
                ins.then_inc(sem, 1)
                dve.wait_ge(sem, 1 + i * 8 * per_block + (j * per_block + n[0]))

            dve.wait_ge(rows_in[j % 2], 1 + i * 64 + 16 * (j // 2 + 1))
            then_wait(dve.tensor_tensor(least[:, :], of(neg_max, 0), of(neg_max, 1), ALU.min), small, SMALL)
            then_wait(dve.tensor_tensor(least[:, :], least[:, :], of(neg_max, 2), ALU.min), small, SMALL)
            dve.tensor_tensor(wgt[:, :].rearrange("p (g s) -> p g s", g=G), least[:, :].unsqueeze(1).broadcast_to([P, G, 8]),
                              neg_max.rearrange("p (g s) -> p g s", g=G), ALU.subtract).then_inc(diff_done, 1)
            dve.wait_ge(e_done, 1 + i * 8 + (j + 1))
            then_wait(dve.tensor_tensor(den[:, :], wgt[:, :], den_of, ALU.mult), small, SMALL)
            then_wait(dve.tensor_tensor(of(den, 0), of(den, 0), of(den, 1), ALU.add), small, SMALL)
            then_wait(dve.tensor_tensor(of(den, 0), of(den, 0), of(den, 2), ALU.add), small, SMALL)
            then_wait(dve.reciprocal(inv[:, :], of(den, 0)), small, SMALL)
            w3 = wgt[:, :].rearrange("p (g s) -> p g s", g=G)
            then_wait(dve.tensor_tensor(w3, w3, inv[:, :].unsqueeze(1).broadcast_to([P, G, 8]), ALU.mult), small, SMALL)
            dve.wait_ge(t_done, 1 + i * 8 + max(j - 1, 0))
            n[0] = 0
            w = lambda g: of(wgt, g).unsqueeze(2).broadcast_to([P, 8, HD])
            then_wait(dve.tensor_tensor(out[:, :, :], r[:, 0:8, 0:HD], w(0), ALU.mult), sums, STEPS)
            for g in (1, 2):
                then_wait(dve.tensor_tensor(part[:, :, :], r[:, 8 * g:8 * g + 8, 0:HD], w(g), ALU.mult), sums, STEPS)
                then_wait(dve.tensor_tensor(out[:, :, :], out[:, :, :], part[:, :, :], ALU.add), sums, STEPS)

        def turn(pe, i, j):
            pe.wait_ge(sums, 1 + i * 8 * STEPS + STEPS * (j + 1))
            pe.wait_ge(copy_done, 1 + i * 8 + max(j - 1, 0))
            flat = joined[j % 2][:, :, :].rearrange("p h d -> p (h d)")
            for m in range(PAIRS):
                mm = pe.transpose(t_ps[j % 2][:, m, :], flat[:, m * P:(m + 1) * P], t["ident"][:, :])
            mm.then_inc(t_done, 1)

        with nc.Block() as block:
            @block.gpsimd
            def _(pool):
                first_signals(pool, sems)

            @block.sync
            def _(sp):
                w_of = lambda n: dr["w_b"][n, 3] if n < BH else dr["w_za"][n - BH]
                src = dr["sums"].rearrange("g j (b p) c -> b p (g j) c", p=P)
                sp.dma_start(w_z[0][:, :, :], w_of(0)).then_inc(w_in[0], 16)
                sp.dma_start(w_z[1][:, :, :], w_of(1)).then_inc(w_in[1], 16)
                for b in range(BLK):
                    if b >= 2:
                        sp.wait_ge(sums, 1 + STEPS * (b - 1))
                    sp.dma_start(rows[b % 2][:, :, :].rearrange("p (a h) c -> p a (h c)", h=2), src[b]).then_inc(rows_in[b % 2], 16)
                    if b in (5, 9):
                        n = b // 4 + 1
                        sp.wait_ge(z_done, 1 + 5 * (n - 1))
                        sp.dma_start(w_z[n % 2][:, :, :], w_of(n)).then_inc(w_in[n % 2], 16)
                for n in range(4, 8):
                    sp.wait_ge(z_done, 1 + 5 * (n - 1))
                    sp.dma_start(w_z[n % 2][:, :, :], w_of(n)).then_inc(w_in[n % 2], 16)

            @block.tensor
            def _(pe):
                with pe.Fori(0, 2) as i:
                    for j in range(8):
                        for u in UNITS_OF_STEP[j]:
                            project_z(pe, 0, i, u, 16)
                        turn(pe, i, j)
                with pe.Fori(0, 2) as i:
                    for u in range(UNITS):
                        project_z(pe, 2 * UNITS, i, u, 48)

            @block.scalar
            def _(act):
                act.preload_act_table_set("natural_log_exp_and_others")
                with act.Fori(0, 2) as i:
                    for j in range(8):
                        act.wait_ge(diff_done, 1 + i * 8 + (j + 1))
                        act.activation(wgt[:, :], wgt[:, :], ACT.Exp).then_inc(e_done, 1)
                        for u in UNITS_OF_STEP[j]:
                            exp_z(act, 0, i, u)
                        act.wait_ge(t_done, 1 + i * 8 + (j + 1))
                        act.copy(oT_a[:, :, bass.ds(i * 8 * P + j * P, P)], t_ps[j % 2][:, :, :]).then_inc(copy_done, 1)
                with act.Fori(0, 2) as i:
                    for u in range(UNITS):
                        exp_z(act, 2 * UNITS, i, u)

            @block.vector
            def _(dve):
                dve.tensor_copy(oT_a[:, :, SEQ:NT], t["oT_s"][:, :, :]).then_inc(s_copied, 1)
                with dve.Fori(0, 2) as i:
                    for j in range(8):
                        join(dve, i, j)
                        for u in UNITS_OF_STEP[j]:
                            apply_z(dve, 0, i, u, oT_b)
                dve.wait_ge(copy_done, 1 + BLK)
                dve.wait_ge(s_copied, 1 + 1)
                with dve.Fori(0, 2) as i:
                    for u in range(UNITS):
                        apply_z(dve, 2 * UNITS, i, u, oT_a)


def phase_merge(nc, t, dr):
    UNITS = 10
    with ExitStack() as ctx:
        sb = lambda name, *a: ctx.enter_context(nc.sbuf_tensor("merge_" + name, *a))
        ps = lambda name, *a: ctx.enter_context(nc.psum_tensor("merge_" + name, *a))
        sems = []

        def sem(name):
            sems.append(ctx.enter_context(nc.semaphore("merge_" + name)))
            return sems[-1]

        hT = t["hT"]
        branch = (t["oT_a"], t["oT_b"])
        w_g = [sb(f"w_g{i}", [P, 2, KD, P], F32) for i in range(2)]
        w_br = [sb(f"w_br{i}", [P, 2, 4, P], F32) for i in range(2)]
        gates, prod = sb("gates", [P, 2, CH], F32), sb("prod", [P, 2, CH], F32)
        out = [sb(f"out{i}", [P, CH], F32) for i in range(2)]
        banks = [ps(f"banks{i}", [P, 4, CH], F32) for i in range(2)]
        w_in = [sem(f"w{i}_loaded") for i in range(2)]
        stored = [sem(f"out{i}_stored") for i in range(2)]
        g_done, br_done, e_done, one_done, rec_done, prod_done, m_done = (sem(n) for n in
            ("g_done", "br_done", "e_done", "one_done", "rec_done", "prod_done", "m_done"))
        cols = lambda u: slice(u % 5 * CH, u % 5 * CH + width(u))
        width = lambda u: CH if u % 5 < NCH else NS

        def load(sp, tile, b):
            sp.dma_start(w_g[b][:, :, :, :], dr["w_g"][tile].rearrange("a p k c -> p a k c")).then_inc(w_in[b], 16)
            sp.dma_start(w_br[b][:, :, :, :], dr["w_br"][tile].rearrange("a p k c -> p a k c")).then_inc(w_in[b], 16)

        with nc.Block() as block:
            @block.gpsimd
            def _(pool):
                first_signals(pool, sems)

            @block.sync
            def _(sp):
                load(sp, 0, 0)
                load(sp, 1, 1)

                def iteration(i, last):
                    for u in range(UNITS):
                        sp.wait_ge(m_done, 1 + i * UNITS + (u + 1))
                        sp.dma_start(dr["merged"][i * 2 + u // 5, :, cols(u)], out[u % 2][:, 0:width(u)]) \
                          .then_inc(stored[u % 2], 16)
                        if u % 5 == 4 and not last:
                            load(sp, i * 2 + (u // 5 + 2), u // 5)

                with sp.Fori(0, 3) as i:
                    iteration(i, False)
                iteration(3, True)
                for b in range(2):
                    sp.wait_ge(stored[b], 1 + 4 * 5 * 16)

            @block.tensor
            def _(pe):
                with pe.Fori(0, 4) as i:
                    for u in range(UNITS):
                        pe.wait_ge(m_done, 1 + i * UNITS + max(u - 1, 0))
                        if u % 5 == 0:
                            pe.wait_ge(w_in[u // 5], 1 + i * 32 + 32)
                        for a in range(2):
                            for k in range(KD):
                                mm = pe.matmul(banks[u % 2][:, a, 0:width(u)], w_g[u // 5][:, a, k, :], hT[:, k, cols(u)],
                                               start=(k == 0), stop=(k == KD - 1))
                        mm.then_inc(g_done, 1)
                        for a in range(2):
                            for k in range(4):
                                mm = pe.matmul(banks[u % 2][:, 2 + a, 0:width(u)], w_br[u // 5][:, a, k, :],
                                               branch[a][:, k, cols(u)], start=(k == 0), stop=(k == 3))
                        mm.then_inc(br_done, 1)

            @block.scalar
            def _(act):
                act.preload_act_table_set("natural_log_exp_and_others")
                with act.Fori(0, 4) as i:
                    for u in range(UNITS):
                        act.wait_ge(g_done, 1 + i * UNITS + (u + 1))
                        act.wait_ge(prod_done, 1 + i * UNITS + u)
                        act.activation(gates[:, :, 0:width(u)], banks[u % 2][:, 0:2, 0:width(u)], ACT.Exp, scale=-1.0) \
                            .then_inc(e_done, 1)

            @block.vector
            def _(dve):
                with dve.Fori(0, 4) as i:
                    for u in range(UNITS):
                        nth, w = i * UNITS + (u + 1), width(u)
                        g = gates[:, :, 0:w]
                        dve.wait_ge(e_done, 1 + nth)
                        dve.tensor_scalar(g, g, 1.0, None, ALU.add).then_inc(one_done, 1)
                        dve.wait_ge(one_done, 1 + nth)
                        dve.reciprocal(g, g).then_inc(rec_done, 1)
                        dve.wait_ge(rec_done, 1 + nth)
                        dve.wait_ge(br_done, 1 + nth)
                        dve.tensor_tensor(prod[:, :, 0:w], banks[u % 2][:, 2:4, 0:w], g, ALU.mult).then_inc(prod_done, 1)
                        dve.wait_ge(prod_done, 1 + nth)
                        dve.wait_ge(stored[u % 2], 1 + i * 80 + 16 * (u // 2))
                        dve.tensor_tensor(out[u % 2][:, 0:w], prod[:, 0, 0:w], prod[:, 1, 0:w], ALU.add).then_inc(m_done, 1)


def phase_output(nc, t, dr):
    UNITS = 10
    with ExitStack() as ctx:
        sb = lambda name, *a: ctx.enter_context(nc.sbuf_tensor("output_" + name, *a))
        ps = lambda name, *a: ctx.enter_context(nc.psum_tensor("output_" + name, *a))
        sems = []

        def sem(name):
            sems.append(ctx.enter_context(nc.semaphore("output_" + name)))
            return sems[-1]

        gate = t["gate"]
        merged = sb("merged", [P, KD, NT], F32)
        w_o = [sb(f"w_o{i}", [P, KD, P], F32) for i in range(2)]
        x_sb = [sb(f"x{i}", [P, NT], F32) for i in range(2)]
        y_sb = [sb(f"y{i}", [P, NT], F32) for i in range(2)]
        gated = sb("gated", [P, NS], F32)
        gate_c = sb("gate_c", [P, 9], F32)
        banks = [ps(f"bank{i}", [P, CH], F32) for i in range(2)]
        m_in = [sem(f"merged{c}_loaded") for c in range(5)]
        w_in = [sem(f"w{i}_loaded") for i in range(2)]
        x_in = [sem(f"x{i}_loaded") for i in range(2)]
        stored = [sem(f"y{i}_stored") for i in range(2)]
        mm_done, y_done, gc_done, g_done = sem("mm_done"), sem("y_done"), sem("gc_done"), sem("g_done")
        cols = lambda u: slice(u % 5 * CH, u % 5 * CH + width(u))
        width = lambda u: CH if u % 5 < NCH else NS

        with nc.Block() as block:
            @block.gpsimd
            def _(pool):
                first_signals(pool, sems)

            @block.sync
            def _(sp):
                def load(tile, b):
                    sp.dma_start(w_o[b][:, :, :], dr["w_o"][tile]).then_inc(w_in[b], 16)
                    sp.dma_start(x_sb[b][:, :], dr["xT"][:, tile, :]).then_inc(x_in[b], 16)

                load(0, 0)
                for c in range(5):
                    sp.dma_start(merged[:, :, cols(c)], dr["merged"].rearrange("k p t -> p k t")[:, :, cols(c)]).then_inc(m_in[c], 16)
                load(1, 1)
                with sp.Fori(0, 3) as i:
                    for b in range(2):
                        sp.wait_ge(y_done, 1 + i * UNITS + 5 * (b + 1))
                        load(i * 2 + (b + 2), b)

            @block.tensor
            def _(pe):
                with pe.Fori(0, 4) as i:
                    for u in range(UNITS):
                        pe.wait_ge(y_done, 1 + i * UNITS + max(u - 1, 0))
                        if u < 5:
                            pe.wait_ge(m_in[u], 1 + 16)
                        if u % 5 == 0:
                            pe.wait_ge(w_in[u // 5], 1 + i * 16 + 16)
                        for k in range(KD):
                            mm = pe.matmul(banks[u % 2][:, 0:width(u)], w_o[u // 5][:, k, :], merged[:, k, cols(u)],
                                           start=(k == 0), stop=(k == KD - 1))
                        mm.then_inc(mm_done, 1)

            @block.vector
            def _(dve):
                with dve.Fori(0, 4) as i:
                    for u in range(UNITS):
                        b, n = u // 5, width(u)
                        if u % 5 == 0:
                            dve.wait_ge(x_in[b], 1 + i * 16 + 16)
                            dve.wait_ge(stored[b], 1 + i * 16)
                            dve.tensor_copy(gate_c[:, :], gate[:, bass.ds(i * 2 + b, 1), :].rearrange("p a c -> p (a c)")) \
                               .then_inc(gc_done, 1)
                            dve.wait_ge(gc_done, 1 + i * 2 + (b + 1))
                        dve.wait_ge(mm_done, 1 + i * UNITS + (u + 1))
                        if n == CH:
                            dve.scalar_tensor_tensor(out=y_sb[b][:, cols(u)], in0=banks[u % 2][:, :], scalar=gate_c[:, 0:1],
                                                     in1=x_sb[b][:, cols(u)], op0=ALU.mult, op1=ALU.add).then_inc(y_done, 1)
                        else:
                            dve.tensor_tensor(gated[:, :].rearrange("p (b t) -> p b t", t=ST),
                                              banks[u % 2][:, 0:NS].rearrange("p (b t) -> p b t", t=ST),
                                              gate_c[:, 1:9].unsqueeze(2).broadcast_to([P, SB, ST]), ALU.mult).then_inc(g_done, 1)
                            dve.wait_ge(g_done, 1 + i * 2 + (b + 1))
                            dve.tensor_tensor(y_sb[b][:, cols(u)], gated[:, :], x_sb[b][:, cols(u)], ALU.add).then_inc(y_done, 1)

            @block.scalar
            def _(act):
                act.preload_act_table_set("natural_log_exp_and_others")
                with act.Fori(0, 4) as i:
                    for b in range(2):
                        act.wait_ge(y_done, 1 + i * UNITS + 5 * (b + 1))
                        act.dma_start(dr["yT"][i * 2 + b], y_sb[b][:, :]).then_inc(stored[b], 16)
                for b in range(2):
                    act.wait_ge(stored[b], 1 + 64)


def decoder_step(nc, dr):
    with ExitStack() as whole:
        t = {}

        def keep(ctx, name, shape):
            t[name] = ctx.enter_context(nc.sbuf_tensor(name, shape, F32))

        keep(whole, "ident", [P, P])
        keep(whole, "eps", [P, 1])
        keep(whole, "gate", [P, 8, 9])
        const_in = whole.enter_context(nc.semaphore("const_loaded"))
        with nc.Block() as block:
            @block.sync
            def _(sp):
                sp.dma_start(t["ident"][:, :], dr["ident"]).then_inc(const_in, 16)
                sp.dma_start(t["eps"][:, :], dr["eps"]).then_inc(const_in, 16)
                sp.wait_ge(const_in, 32)
        with ExitStack() as ctx:
            keep(ctx, "mod", [P, 16, 9])
            keep(ctx, "oT_s", [P, PAIRS, NS])
            keep(ctx, "hT", [P, KD, NT])
            phase_input(nc, t, dr)
            phase_attention(nc, t, dr)
            phase_sample(nc, t, dr)
            keep(ctx, "oT_b", [P, BH, NT])
            phase_hgrn(nc, t, dr)
            keep(ctx, "oT_a", [P, PAIRS, NT])
            phase_join(nc, t, dr)
            phase_merge(nc, t, dr)
        phase_output(nc, t, dr)


BIG = 1.0e30


def _tables(np):
    c = {}
    c["ident"] = np.eye(P, dtype=np.float32)
    c["eps"] = np.full((P, 1), EPS, np.float32)
    c["ones_d"] = np.full((P, P), 1.0 / D, np.float32)
    half = np.arange(P) // HD
    c["ones_h"] = (half[:, None] == half[None, :]).astype(np.float32) / HD
    c["ones_i"] = np.full((P, P), 1.0 / P, np.float32)
    slopes = (2.0 ** (-8.0 * (np.arange(24) + 1) / 24)).astype(np.float32).reshape(G, 8)
    delta = np.arange(P)[:, None] + P - np.arange(2 * P)[None, :]
    dist = np.empty((PAIRS, G, P, 2, 2 * P), np.float32)
    for g in range(G):
        for s in range(8):
            dist[s // 2, g, :, s % 2] = np.where((delta >= 0) & (delta <= P),
                                                 slopes[g, s] * (delta * DIL[g]).astype(np.float32), np.float32(BIG))
    c["dist"] = dist
    pen = np.full((2, 8, ST, 4 * CH), BIG, np.float32)
    pos = np.arange(P)
    for s in range(8):
        for q in range(ST):
            def put(col, g, d):
                ok = (d >= 0) & (d <= DIL[g] * P) & (d % DIL[g] == 0)
                pen[:, s, q, col:col + len(d)] = np.where(ok, slopes[g, s] * d.astype(np.float32), np.float32(BIG))
            for r in range(4):
                put(r * P, 1, 512 + q - (4 * pos + r))
            for r in range(8):
                put(CH + r * P, 2, 2048 + q - (16 * pos + r))
            put(3 * CH, 0, P + q - pos)
            for g in range(G):
                put(3 * CH + P + 8 * g, g, q - np.arange(ST))
    c["pen_s"] = pen.reshape(P, 4 * CH)[:, :3 * CH + P + 24].copy()
    row = np.arange(P)
    c["own_s"] = (((row % 64) // 8)[:, None] == (np.arange(CH) // HD)[None, :]).astype(np.float32)
    c["sel_s"] = ((row // 64 * 8 + row % 8)[:, None] == np.arange(16)[None, :]).astype(np.float32)
    keep = np.ones(NT, np.float32)
    keep[0:SEQ:P] = 0
    keep[SEQ::ST] = 0
    c["keep"] = np.broadcast_to(keep, (P, NT)).copy()
    s_, t_ = np.arange(P)[:, None], np.arange(P)[None, :]
    lev = np.zeros((P, 8, P), np.uint32)
    lev[:, 0] = s_ == t_
    for l in range(1, 8):
        B = 1 << l
        lev[:, l] = (s_ // B == t_ // B) & (s_ % B < B // 2) & (t_ % B >= B // 2)
    c["level"] = lev
    c["seq_s"] = ((np.arange(NS) // ST)[:, None] == np.arange(SB)[None, :]).astype(np.float32)
    return c


def kernel(x_prompt, x_sample, cache_kv_g0, cache_kv_g1, cache_kv_g2, state_hgrn, c_prompt, c_sample,
           norm_gain, w_ada, b_ada, w_in, q_norm_gain, k_norm_gain, hgrn_lb_logits, hgrn_out_norm_gain,
           w_branch_a, w_branch_b, w_out):
    import numpy as np
    import concourse.bacc as bacc
    from concourse.bass_utils import run_bass_kernel_spmd as run

    A = np.asarray
    tiles = lambda w: A(w).reshape(-1, P, w.shape[-1] // P, P).transpose(2, 1, 0, 3)
    x = np.concatenate([A(x_prompt)[0], A(x_sample).reshape(NS, D)])
    c = np.concatenate([A(c_prompt), A(c_sample)])
    w = tiles(A(w_in)[0])
    kv = [A(cache_kv_g0)[0], A(cache_kv_g1)[0], A(cache_kv_g2)[0]]
    keys = []
    keys.append(kv[1].reshape(SB, P, 4, 2, CH).transpose(0, 2, 1, 3, 4))
    keys.append(kv[2].reshape(SB, P, 16, 2, CH)[:, :, :8].transpose(0, 2, 1, 3, 4))
    keys.append(kv[0].reshape(SB, 1, P, 2, CH))
    keys = np.concatenate(keys, axis=1)
    ins = {
        "xT": x.T.reshape(KD, P, NT).transpose(1, 0, 2),
        "cT": c.T.reshape(KD, P, 9).transpose(1, 0, 2),
        "w_ada": A(w_ada)[0].reshape(KD, P, 6, CH).transpose(2, 1, 0, 3),
        "b_ada": A(b_ada)[0].reshape(24, P).T,
        "norm_gain": A(norm_gain)[0].reshape(KD, P).T,
        "w_qkv": w[0:36].reshape(3, G, PAIRS, P, KD, P).transpose(2, 1, 0, 3, 4, 5),
        "w_za": w[36:40],
        "w_b": w[40:56].reshape(4, BH, P, KD, P).transpose(1, 0, 2, 3, 4),
        "w_g": w[56:72].reshape(2, 8, P, KD, P).transpose(1, 0, 2, 3, 4),
        "w_br": np.stack([tiles(A(w_branch_a)[0]), tiles(A(w_branch_b)[0])], axis=1),
        "w_o": tiles(A(w_out)[0]),
        "qk_gain": np.stack([np.tile(A(q_norm_gain)[0], 2), np.tile(A(k_norm_gain)[0], 2)], axis=1),
        "lb": A(hgrn_lb_logits).reshape(2, BH, P).transpose(2, 0, 1),
        "o_gain": A(hgrn_out_norm_gain)[0].reshape(P, 1),
        "kT_c": keys[:, :, :, 0].reshape(SB, KEYS * P, 4, P).transpose(0, 3, 2, 1),
        "v_c": keys[:, :, :, 1].transpose(0, 2, 1, 3),
        "state": A(state_hgrn)[0].transpose(1, 2, 0, 3),
    }
    ins.update(_tables(np))
    outs = {
        "yT": (8, P, NT), "kT_p0": (4, P, P), "kT_p1": (4, P, 512), "kT_p2": (4, P, SEQ),
        "v_p0": (4, P, 1, 2, 65), "v_p1": (4, P, 4, 2, 65), "v_p2": (4, P, 16, 2, 65),
        "kT_s0": (4, P, NS), "kT_s1": (4, P, NS), "kT_s2": (4, P, NS),
        "v_s0": (4, NS, P), "v_s1": (4, NS, P), "v_s2": (4, NS, P),
        "state_p": (BH, P, P), "state_s": (BH, P, SB, P),
    }
    scratch = {"sums": (G, PAIRS, SEQ, ORow), "qT_s": (PAIRS, G, P, NS), "merged": (8, P, NT)}

    nc = bacc.Bacc("TRN2", target_bir_lowering=False, num_devices=1)
    arrays, dr = {}, {}
    for name, a in ins.items():
        arrays["in_" + name] = np.ascontiguousarray(a)
        dr[name] = nc.dram_tensor("in_" + name, a.shape, mybir.dt.from_np(a.dtype), kind="ExternalInput").ap()
    for name, shape in outs.items():
        dr[name] = nc.dram_tensor("out_" + name, shape, F32, kind="ExternalOutput").ap()
    for name, shape in scratch.items():
        dr[name] = nc.dram_tensor("scratch_" + name, shape, F32).ap()
    decoder_step(nc, dr)
    r = run(nc, [arrays], core_ids=[0]).results[0]
    o = {name: r["out_" + name] for name in outs}

    y = o["yT"].transpose(2, 0, 1).reshape(NT, D)
    head = lambda a: a.reshape(1, -1, 8, HD)
    kv_p, kv_s = [], []
    for g, W in enumerate((P, 512, SEQ)):
        k = o[f"kT_p{g}"].transpose(2, 0, 1).reshape(W, CH)
        v = o[f"v_p{g}"][..., :HD]
        v = v.transpose(1, 2, 0, 3, 4).reshape(W, CH)
        kv_p.append(np.stack([k.reshape(1, 1, W, 8, HD), v.reshape(1, 1, W, 8, HD)], axis=3))
        k = o[f"kT_s{g}"].transpose(2, 0, 1).reshape(1, SB, ST, 8, HD)
        v = o[f"v_s{g}"].transpose(1, 0, 2).reshape(1, SB, ST, 8, HD)
        kv_s.append(np.stack([k, v], axis=3))
    return (y[:SEQ].reshape(1, SEQ, D), y[SEQ:].reshape(SB, ST, D), *kv_p,
            o["state_p"].reshape(1, 1, BH, P, P), *kv_s, o["state_s"].transpose(2, 0, 1, 3).reshape(1, SB, BH, P, P))
```

```python
from contextlib import ExitStack

import concourse.bass as bass
from concourse import mybir

ALU = mybir.AluOpType
ACT = mybir.ActivationFunctionType
F32 = mybir.dt.float32
F32R = mybir.dt.float32r
U32 = mybir.dt.uint32
AX = mybir.AxisListType

P = 128
D = 1024
KD = D // P
SEQ = 2048
SB, ST = 8, 8
NS = SB * ST
NT = SEQ + NS
G = 3
DIL = (1, 4, 16)
PAIRS = 4
HD = 64
BLK = SEQ // P
KEYS = 13
BH = 4
EPS = 1e-6
CH = 512
NCH = SEQ // CH
ORow = 132


def block_tokens(g, i):
    if g == 0:
        return P * i, 1, i > 0
    if g == 1:
        r, b = divmod(i, 4)
        return r + 4 * P * b, 4, b > 0
    return i, 16, False


def first_signals(pool, sems):
    for sem in sems:
        pool.sem_inc(sem, 1)


def phase_input(nc, t, dr):
    DVE_KD = 5
    with ExitStack() as ctx:
        sb = lambda name, *a: ctx.enter_context(nc.sbuf_tensor("input_" + name, *a))
        ps = lambda name, *a: ctx.enter_context(nc.psum_tensor("input_" + name, *a))
        sems = []

        def sem(name):
            sems.append(nc.alloc_semaphore(name="input_" + name))
            return sems[-1]

        c_sb = sb("c_sb", [P, KD, 9], F32)
        c_exp = sb("c_exp", [P, KD, 9], F32)
        c_rec = sb("c_rec", [P, KD, 9], F32)
        c_act = sb("c_act", [P, KD, 9], F32)
        b_sb = sb("b_sb", [P, 24], F32)
        gain_sb = sb("gain_sb", [P, KD], F32)
        ones_d = sb("ones_d", [P, P], F32)
        w_ada = [sb(f"w_ada{i}", [P, KD, CH], F32) for i in range(2)]
        x_sb = [sb(f"x_sb{i}", [P, KD, CH], F32) for i in range(2)]
        x_sq = sb("x_sq", [P, KD, CH], F32)
        log_ms = sb("log_ms", [P, CH], F32)
        rstd = sb("rstd", [P, CH], F32)
        ada_ps, gate_ps = ps("ada_ps", [P, 56, 9], F32), ps("gate_ps", [P, 56, 9], F32)
        ss_ps = ps("ss_ps", [P, CH], F32)
        small = sem("small_loaded")
        w_in = [sem(f"w_ada_loaded{i}") for i in range(2)]
        x_in = [sem(f"x_loaded{i}") for i in range(2)]
        c_done, silu_done, ada_done, mod_done = sem("c_exp_done"), sem("silu_done"), sem("ada_done"), sem("mod_done")
        sq_done, ss_done, ms_done, r_done, xn_done, h_done = (sem(n) for n in
            ("sq_done", "ss_done", "ms_done", "r_done", "xn_done", "h_done"))
        steps = sem("vector_steps")
        hT, mod, gate = t["hT"], t["mod"], t["gate"]
        xs = dr["xT"]

        with nc.Block() as block:
            @block.gpsimd
            def _(pool):
                first_signals(pool, sems)

            @block.sync
            def _(sp):
                sp.dma_start(c_sb[:, :, :], dr["cT"]).then_inc(small, 16)
                sp.dma_start(b_sb[:, :], dr["b_ada"]).then_inc(small, 16)
                sp.dma_start(gain_sb[:, :], dr["norm_gain"]).then_inc(small, 16)
                sp.dma_start(ones_d[:, :], dr["ones_d"]).then_inc(small, 16)

                def load_x(c):
                    n = CH if c < NCH else NS
                    if c >= 2:
                        sp.wait_ge(xn_done, 1 + c - 1)
                    sp.dma_start(x_sb[c % 2][:, :, 0:n], xs[:, :, c * CH:c * CH + n]).then_inc(x_in[c % 2], 16)

                def load_w(c):
                    if c >= 2:
                        sp.wait_ge(ada_done, 1 + c - 1)
                    sp.dma_start(w_ada[c % 2][:, :, :], dr["w_ada"][c]).then_inc(w_in[c % 2], 16)

                for c in range(NCH + 1):
                    load_x(c)
                    load_w(c)
                load_w(5)

            @block.tensor
            def _(pe):
                def sums(c):
                    n = CH if c < NCH else NS
                    pe.wait_ge(sq_done, 1 + c + 1)
                    pe.wait_ge(ms_done, 1 + c)
                    for k in range(KD):
                        mm = pe.matmul(ss_ps[:, 0:n], ones_d[:, :], x_sq[:, k, 0:n], start=(k == 0), stop=(k == KD - 1))
                    mm.then_inc(ss_done, 1)

                def vectors(c):
                    pe.wait_ge(w_in[c % 2], 1 + 16 * (c // 2 + 1))
                    for f in range(4):
                        for k in range(KD):
                            mm = pe.matmul((ada_ps if c < 4 else gate_ps)[:, 4 * (c % 4) + f, :], w_ada[c % 2][:, k, f * P:(f + 1) * P], c_act[:, k, :],
                                           start=(k == 0), stop=(k == KD - 1))
                    mm.then_inc(ada_done, 1)

                pe.wait_ge(silu_done, 1 + 1)
                for c in range(NCH + 1):
                    sums(c)
                    vectors(c)
                vectors(5)

            @block.scalar
            def _(act):
                act.preload_act_table_set("natural_log_exp_and_others")
                act.wait_ge(small, 1 + 64)
                act.activation(c_exp[:, :, :], c_sb[:, :, :], ACT.Exp, scale=-1.0).then_inc(c_done, 1)

                def square(j, loaded, used, n):
                    act.wait_ge(x_in[j], 1 + loaded)
                    act.wait_ge(ss_done, 1 + used)
                    act.activation(x_sq[:, :, 0:n], x_sb[j][:, :, 0:n], ACT.Square).then_inc(sq_done, 1)

                def leave(nth, xn, n):
                    act.wait_ge(ss_done, 1 + nth)
                    act.wait_ge(xn_done, 1 + xn)
                    act.activation(log_ms[:, 0:n], ss_ps[:, 0:n], ACT.Ln, bias=t["eps"][:, 0:1]).then_inc(ms_done, 1)
                    act.wait_ge(ms_done, 1 + nth)
                    act.activation(rstd[:, 0:n], log_ms[:, 0:n], ACT.Exp, scale=-0.5).then_inc(r_done, 1)

                for c in range(NCH + 1):
                    n = CH if c < NCH else NS
                    square(c % 2, 16 * (c // 2 + 1), c, n)
                    leave(c + 1, c, n)
                act.wait_ge(mod_done, 1 + 1)
                act.wait_ge(xn_done, 1 + NCH + 1)
                for k in range(DVE_KD, KD):
                    act.activation(hT[:, k, 0:SEQ], hT[:, k, 0:SEQ], ACT.Identity, scale=mod[:, 8 + k, 0:1],
                                   bias=mod[:, k, 0:1]).then_inc(h_done, 1)

            @block.vector
            def _(dve):
                dve.wait_ge(c_done, 1 + 1)
                dve.tensor_scalar(c_rec[:, :, :], c_exp[:, :, :], 1.0, None, ALU.add).then_inc(steps, 1)
                dve.wait_ge(steps, 1 + 1)
                dve.reciprocal(c_exp[:, :, :], c_rec[:, :, :]).then_inc(steps, 1)
                dve.wait_ge(steps, 1 + 2)
                dve.tensor_tensor(c_act[:, :, :], c_exp[:, :, :], c_sb[:, :, :], ALU.mult).then_inc(silu_done, 1)
                def normed(c):
                    n = CH if c < NCH else NS
                    dve.wait_ge(r_done, 1 + c + 1)
                    dve.tensor_tensor(hT[:, :, c * CH:c * CH + n], x_sb[c % 2][:, :, 0:n],
                                      rstd[:, 0:n].unsqueeze(1).broadcast_to([P, KD, n]), ALU.mult).then_inc(xn_done, 1)

                for c in range(NCH):
                    normed(c)
                dve.wait_ge(ada_done, 1 + 4)
                dve.tensor_tensor(mod[:, :, :], ada_ps[:, 0:16, :], b_sb[:, 0:16].unsqueeze(2).broadcast_to([P, 16, 9]),
                                  ALU.add).then_inc(steps, 1)
                dve.wait_ge(steps, 1 + 3)
                dve.tensor_scalar(mod[:, 8:16, :], mod[:, 8:16, :], 1.0, None, ALU.add).then_inc(steps, 1)
                dve.wait_ge(steps, 1 + 4)
                dve.tensor_tensor(mod[:, 8:16, :], mod[:, 8:16, :], gain_sb[:, :].unsqueeze(2).broadcast_to([P, 8, 9]),
                                  ALU.mult).then_inc(mod_done, 1)
                dve.wait_ge(mod_done, 1 + 1)

                normed(NCH)
                dve.wait_ge(xn_done, 1 + NCH + 1)
                for k in range(DVE_KD):
                    dve.tensor_scalar(hT[:, k, 0:SEQ], hT[:, k, 0:SEQ], mod[:, 8 + k, 0:1], mod[:, k, 0:1],
                                      ALU.mult, ALU.add).then_inc(h_done, 1)
                per_token = lambda a: a.unsqueeze(3).broadcast_to([P, KD, SB, ST])
                split = lambda a: a.rearrange("p k (b t) -> p k b t", t=ST)
                dve.tensor_tensor(split(x_sb[0][:, :, 0:NS]), split(hT[:, :, SEQ:NT]), per_token(mod[:, 8:16, 1:9]),
                                  ALU.mult).then_inc(steps, 1)
                dve.wait_ge(steps, 1 + 5)
                dve.tensor_tensor(split(hT[:, :, SEQ:NT]), split(x_sb[0][:, :, 0:NS]), per_token(mod[:, 0:8, 1:9]),
                                  ALU.add).then_inc(h_done, 1)
                dve.wait_ge(ada_done, 1 + 6)
                dve.tensor_tensor(gate[:, :, :], gate_ps[:, 0:8, :], b_sb[:, 16:24].unsqueeze(2).broadcast_to([P, 8, 9]),
                                  ALU.add).then_inc(steps, 1)

        with nc.Block() as block:
            @block.gpsimd
            def _(pool):
                nc.clear_and_free_semaphores(sems)


def phase_gates(nc, t, dr):
    TILES = 16
    with ExitStack() as ctx:
        sb = lambda name, *a: ctx.enter_context(nc.sbuf_tensor("gates_" + name, *a))
        ps = lambda name, *a: ctx.enter_context(nc.psum_tensor("gates_" + name, *a))
        sems = []

        def sem(name):
            sems.append(nc.alloc_semaphore(name="gates_" + name))
            return sems[-1]

        hT = t["hT"]
        WIDTHS = ((CH, CH), (CH, CH, NS))
        LO, COLS = (0, SEQ // 2), (SEQ // 2, SEQ // 2 + NS)
        h_high, h_low = sb("h_high", [P, KD, COLS[1]], F32R), sb("h_low", [P, KD, COLS[1]], F32R)
        w_raw = [sb(f"w_raw{i}", [P, KD, P], F32) for i in range(2)]
        w_high = [sb(f"w_high{i}", [P, KD, P], F32R) for i in range(2)]
        w_low = [sb(f"w_low{i}", [P, KD, P], F32R) for i in range(2)]
        out = [sb(f"out{i}", [P, COLS[1]], F32) for i in range(2)]
        banks = [[ps(f"bank{i}_{u}", [P, CH], F32) for u in range(3)] for i in range(2)]
        w_in = [sem(f"w_raw{i}_loaded") for i in range(2)]
        stored = [sem(f"out{i}_stored") for i in range(2)]
        h_high_done, h_low_done, w_high_done, w_low_done, unit_done, e_done, one_done, sig_done = (sem(n) for n in
            ("h_high_done", "h_low_done", "w_high_done", "w_low_done", "unit_done", "e_done", "one_done", "sig_done"))

        def units(half, n):
            return n * 2 if half == 0 else (n - TILES) * 3 + 2 * TILES

        def all_tiles(eng, tile):
            def pair(half, i, first=False, last=False):
                for b in range(2):
                    tile(eng, half, i, b, first and b == 0, last and b == 1)

            pair(0, 0, first=True)
            with eng.Fori(1, TILES // 2) as i:
                pair(0, i)
            with eng.Fori(TILES // 2, TILES - 1) as i:
                pair(1, i)
            pair(1, TILES - 1, last=True)

        def split_w_high(act, half, n, b, nth):
            act.wait_ge(w_in[b], 1 + nth * 16 + 16)
            if not isinstance(n, int) or n >= 2:
                act.wait_ge(unit_done, 1 + units(half, n - 1))
            act.copy(w_high[b][:, :, :], w_raw[b][:, :, :]).then_inc(w_high_done, 1)

        def split_w_low(dve, n, b):
            dve.wait_ge(w_high_done, 1 + n + 1)
            dve.tensor_tensor(w_low[b][:, :, :], w_raw[b][:, :, :], w_high[b][:, :, :], ALU.subtract).then_inc(w_low_done, 1)

        def pe_tile(pe, half, i, b, first, last):
            n = i * 2 + b
            pe.wait_ge(w_low_done, 1 + n + 1)
            if not first:
                pe.wait_ge(e_done, 1 + units(half, n - 1) + (half == 1 and b == 0))
            for u, w in enumerate(WIDTHS[half]):
                pe.wait_ge(h_low_done, 1 + 2 * half + (u + 1))
                bank, c = banks[b][u][:, 0:w], slice(u * CH, u * CH + w)
                for k in range(KD):
                    pe.matmul(bank, w_high[b][:, k, :], h_high[:, k, c], start=(k == 0), stop=False)
                    pe.matmul(bank, w_high[b][:, k, :], h_low[:, k, c], start=False, stop=False)
                    mm = pe.matmul(bank, w_low[b][:, k, :], h_high[:, k, c], start=False, stop=(k == KD - 1))
                mm.then_inc(unit_done, 1)

        def act_tile(act, half, i, b, first, last):
            n = i * 2 + b
            if not last:
                split_w_high(act, half, n + 1, 1 - b, i + b)
            act.wait_ge(stored[b], 1 + i * 16)
            for u, w in enumerate(WIDTHS[half]):
                act.wait_ge(unit_done, 1 + units(half, n) + (u + 1))
                act.activation(out[b][:, u * CH:u * CH + w], banks[b][u][:, 0:w], ACT.Exp, scale=-1.0).then_inc(e_done, 1)

        def dve_tile(dve, half, i, b, first, last):
            n = i * 2 + b
            if not last:
                split_w_low(dve, n + 1, 1 - b)
            for u, w in enumerate(WIDTHS[half]):
                nth, e = units(half, n) + (u + 1), out[b][:, u * CH:u * CH + w]
                dve.wait_ge(e_done, 1 + nth)
                dve.tensor_scalar(e, e, 1.0, None, ALU.add).then_inc(one_done, 1)
                dve.wait_ge(one_done, 1 + nth)
                dve.reciprocal(e, e).then_inc(sig_done, 1)

        def split_h_high(act, half):
            for u, w in enumerate(WIDTHS[half]):
                if half:
                    act.wait_ge(unit_done, 1 + 2 * TILES)
                act.copy(h_high[:, :, u * CH:u * CH + w], hT[:, :, LO[half] + u * CH:LO[half] + u * CH + w]) \
                   .then_inc(h_high_done, 1)

        def split_h_low(dve, half):
            for u, w in enumerate(WIDTHS[half]):
                dve.wait_ge(h_high_done, 1 + 2 * half + (u + 1))
                c = slice(u * CH, u * CH + w)
                dve.tensor_tensor(h_low[:, :, c], hT[:, :, LO[half] + u * CH:LO[half] + u * CH + w], h_high[:, :, c],
                                  ALU.subtract).then_inc(h_low_done, 1)

        def with_h(eng, split, tile):
            def pair(half, i, last=False):
                for b in range(2):
                    tile(eng, half, i, b, False, last and b == 1)

            split(eng, 0)
            pair(0, 0)
            with eng.Fori(1, TILES // 2) as i:
                pair(0, i)
            split(eng, 1)
            with eng.Fori(TILES // 2, TILES - 1) as i:
                pair(1, i)
            pair(1, TILES - 1, last=True)

        def load(sp, tile, n, b):
            if not isinstance(n, int) or n >= 2:
                sp.wait_ge(w_low_done, 1 + n - 1)
            sp.dma_start(w_raw[b][:, :, :], dr["w_g"][tile, b]).then_inc(w_in[b], 16)

        def store(sp, half, tile, n, b):
            sp.wait_ge(sig_done, 1 + units(half, n + 1))
            sp.dma_start(dr["gates"][b, tile, :, LO[half]:LO[half] + COLS[half]], out[b][:, 0:COLS[half]]).then_inc(stored[b], 16)

        with nc.Block() as block:
            @block.gpsimd
            def _(pool):
                first_signals(pool, sems[::-1])

            @block.sync
            def _(sp):
                for b in range(2):
                    load(sp, 0, b, b)
                for half in range(2):
                    with sp.Fori(0, TILES // 2 - 1) as i:
                        for b in range(2):
                            load(sp, i + 1, i * 2 + (half * TILES + 2 + b), b)
                        for b in range(2):
                            store(sp, half, i, i * 2 + (half * TILES + b), b)
                    if half == 0:
                        for b in range(2):
                            load(sp, 0, TILES + b, b)
                    for b in range(2):
                        store(sp, half, TILES // 2 - 1, half * TILES + TILES - 2 + b, b)
                for b in range(2):
                    sp.wait_ge(stored[b], 1 + 16 * TILES)

            @block.tensor
            def _(pe):
                all_tiles(pe, pe_tile)

            @block.scalar
            def _(act):
                act.preload_act_table_set("natural_log_exp_and_others")
                split_w_high(act, 0, 0, 0, 0)
                with_h(act, split_h_high, act_tile)

            @block.vector
            def _(dve):
                split_w_low(dve, 0, 0)
                with_h(dve, split_h_low, dve_tile)

        with nc.Block() as block:
            @block.gpsimd
            def _(pool):
                nc.clear_and_free_semaphores(sems)


def phase_attention(nc, t, dr):
    UNITS = 15
    with ExitStack() as ctx:
        sb = lambda name, *a: ctx.enter_context(nc.sbuf_tensor("attention_" + name, *a))
        ps = lambda name, *a: ctx.enter_context(nc.psum_tensor("attention_" + name, *a))
        sems = []

        def sem(name):
            sems.append(ctx.enter_context(nc.semaphore("attention_" + name)))
            return sems[-1]

        hT = t["hT"]
        w_sb = [sb(f"w_{x}", [P, KD, P], F32) for x in "qkv"]
        qk = [[sb(f"{x}T{g}", [P, NT], F32) for g in range(G)] for x in "qk"]
        v_sb = [sb(f"v{g}", [P, BLK + 1, 2, HD + 1], F32) for g in range(G)]
        dist = [sb(f"dist{g}", [P, 2, 2 * P], F32) for g in range(G)]
        scores = sb("scores", [P, 2, 2 * P], F32)
        probs = sb("probs", [P, 2, 2 * P], F32)
        probsT = sb("probsT", [P, 4, P], F32)
        sq = sb("sq", [P, CH], F32)
        log_ms = sb("log_ms", [P, CH], F32)
        rstd = sb("rstd", [P, CH], F32)
        o_out = sb("o_out", [P, BLK, ORow], F32)
        gains = sb("gains", [P, 2], F32)
        ident, ones_h = t["ident"], sb("ones_h", [P, P], F32)
        u_ps = [ps(f"u_ps{i}", [P, CH], F32) for i in range(3)]
        ss_ps = ps("ss_ps", [P, CH], F32)
        s_ps = [ps(f"s_ps{h}", [P, 2 * P], F32) for h in range(2)]
        t_ps = ps("t_ps", [P, 4, P], F32)
        o_ps = ps("o_ps", [P, 2, HD + 1], F32)
        const_in = sem("const_loaded")
        w_in = [sem(f"w_{x}_loaded") for x in "qkv"]
        dist_in = sem("dist_loaded")
        ones_set, gain_set = sem("ones_set"), sem("gain_set")
        unit_done, sq_done, ss_done, ms_done, r_done, evac_done = (sem(n) for n in
            ("unit_done", "sq_done", "ss_done", "ms_done", "r_done", "evac_done"))
        s_done, max_done, exp_done, t_done, copy_done, pv_done, o_done = (sem(n) for n in
            ("s_done", "max_done", "exp_done", "t_done", "copy_done", "pv_done", "o_done"))
        s_seen = sem("s_seen")
        half_out = [sem(f"o_half{i}_stored") for i in range(2)]
        kv_out = sem("kv_stored")
        KV = 16 * 5

        def project_unit(pe, g, n, i):
            kind, j = divmod(i, 5)
            if i == 0:
                pe.wait_ge(evac_done, 1 + n * UNITS)
            elif i >= 3:
                pe.wait_ge(evac_done, 1 + n * UNITS + (i - 2))
            if j == 0:
                pe.wait_ge(w_in[kind], 1 + n * 16 + 16)
            u = u_ps[i % 3]
            if kind < 2:
                lo, w = (j * CH, CH) if j < NCH else (SEQ, NS)
                for k in range(KD):
                    mm = pe.matmul(u[:, 0:w], w_sb[kind][:, k, :], hT[:, k, lo:lo + w], start=(k == 0), stop=(k == KD - 1))
            elif j < NCH:
                for b in range(4):
                    lo, step, _ = block_tokens(g, 4 * j + b)
                    for k in range(KD):
                        mm = pe.matmul(u[:, b * P:(b + 1) * P], hT[:, k, lo:lo + (P - 1) * step + 1:step],
                                       w_sb[2][:, k, :], start=(k == 0), stop=(k == KD - 1))
            else:
                for k in range(KD):
                    mm = pe.matmul(u[0:NS, 0:P], hT[:, k, SEQ:NT], w_sb[2][:, k, :], start=(k == 0), stop=(k == KD - 1))
            mm.then_inc(unit_done, 1)

        def head_sums(pe, n, i):
            if i >= 10:
                return
            w = CH if i % 5 < NCH else NS
            pe.wait_ge(sq_done, 1 + n * 10 + (i + 1))
            pe.wait_ge(ms_done, 1 + n * 10 + i)
            pe.matmul(ss_ps[:, 0:w], ones_h[:, :], sq[:, 0:w], start=True, stop=True).then_inc(ss_done, 1)

        def square_unit(act, n, i):
            if i >= 10:
                return
            w = CH if i % 5 < NCH else NS
            act.wait_ge(unit_done, 1 + n * UNITS + (i + 1))
            act.wait_ge(ss_done, 1 + n * 10 + i)
            act.activation(sq[:, 0:w], u_ps[i % 3][:, 0:w], ACT.Square).then_inc(sq_done, 1)

        def root(act, n, i):
            if i >= 10:
                return
            w = CH if i % 5 < NCH else NS
            act.wait_ge(ss_done, 1 + n * 10 + (i + 1))
            act.activation(log_ms[:, 0:w], ss_ps[:, 0:w], ACT.Ln, bias=t["eps"][:, 0:1]).then_inc(ms_done, 1)
            act.wait_ge(ms_done, 1 + n * 10 + (i + 1))
            act.wait_ge(evac_done, 1 + n * UNITS + i)
            act.activation(rstd[:, 0:w], log_ms[:, 0:w], ACT.Exp, scale=-0.5).then_inc(r_done, 1)

        def leave_unit(dve, g, n, i):
            kind, j = divmod(i, 5)
            u = u_ps[i % 3]
            if i == 0:
                dve.wait_ge(kv_out, 1 + (n - 1) * KV if not isinstance(n, int) or n > 1 else 0)
            if kind < 2:
                lo, w = (j * CH, CH) if j < NCH else (SEQ, NS)
                dve.wait_ge(r_done, 1 + n * 10 + (i + 1))
                dve.scalar_tensor_tensor(out=qk[kind][g][:, lo:lo + w], in0=u[:, 0:w], scalar=gains[:, kind:kind + 1],
                                         in1=rstd[:, 0:w], op0=ALU.mult, op1=ALU.mult).then_inc(evac_done, 1)
            else:
                dve.wait_ge(unit_done, 1 + n * UNITS + (i + 1))
                if j < NCH:
                    dve.tensor_copy(v_sb[g][:, 4 * j:4 * j + 4, :, 0:HD],
                                    u[:, :].rearrange("p (b h d) -> p b h d", b=4, h=2)).then_inc(evac_done, 1)
                else:
                    dve.tensor_copy(v_sb[g][0:NS, BLK, :, 0:HD],
                                    u[0:NS, 0:P].rearrange("p (h d) -> p h d", h=2)).then_inc(evac_done, 1)

        def key_range(g, i):
            lo, step, before = block_tokens(g, i)
            first = 0 if before else 1
            return lo - (0 if first else P * step), step, first

        def score(pe, g, a, i):
            if i == 0:
                pe.wait_ge(evac_done, 1 + a * UNITS + UNITS)
            pe.wait_ge(max_done, 1 + a * 32 + 2 * i)
            lo, step, _ = block_tokens(g, i)
            klo, _, first = key_range(g, i)
            nk = (2 - first) * P
            for h in range(2):
                q = qk[0][g][h * HD:(h + 1) * HD, lo:lo + (P - 1) * step + 1:step]
                k = qk[1][g][h * HD:(h + 1) * HD, klo:klo + (nk - 1) * step + 1:step]
                pe.matmul(s_ps[h][:, first * P:], q, k, start=True, stop=True).then_inc(s_done, 1)

        def turn(pe, g, a, i):
            pe.wait_ge(exp_done, 1 + a * 32 + (2 * i + 2))
            pe.wait_ge(copy_done, 1 + a * 16 + i)
            first = key_range(g, i)[2]
            for h in range(2):
                for b in range(first, 2):
                    mm = pe.transpose(t_ps[:, 2 * h + b, :], probs[:, h, b * P:(b + 1) * P], ident[:, :])
            mm.then_inc(t_done, 1)

        def weigh(pe, g, a, i):
            pe.wait_ge(copy_done, 1 + a * 16 + (i + 1))
            pe.wait_ge(o_done, 1 + a * 16 + i)
            first = key_range(g, i)[2]
            for h in range(2):
                for b in range(first, 2):
                    mm = pe.matmul(o_ps[:, h, :], probsT[:, 2 * h + b, :], v_sb[g][:, i + b - 1, h, :],
                                   start=(b == first), stop=(b == 1))
            mm.then_inc(pv_done, 1)

        def largest(dve, g, a, i):
            if i == 0:
                dve.wait_ge(dist_in, 1 + a * 16 + 16)
            if i % 8 == 0:
                dve.wait_ge(half_out[i // 8], 1 + a * 32)
            dve.wait_ge(exp_done, 1 + a * 32 + 2 * i)
            first = key_range(g, i)[2]
            for h in range(2):
                dve.wait_ge(s_done, 1 + a * 32 + (2 * i + h + 1))
                dve.sem_inc(s_seen, 1)
                dve.tensor_tensor_reduce(scores[:, h, first * P:], s_ps[h][:, first * P:], dist[g][:, h, first * P:],
                                         1.0, 3.0e38, ALU.add, ALU.min,
                                         o_out[:, i, h * 66 + 65:h * 66 + 66]).then_inc(max_done, 1)

        def weights(act, g, a, i):
            act.wait_ge(t_done, 1 + a * 16 + i)
            first = key_range(g, i)[2]
            for h in range(2):
                act.wait_ge(max_done, 1 + a * 32 + (2 * i + h + 1))
                act.activation(probs[:, h, first * P:], scores[:, h, first * P:], ACT.Exp, scale=-1.0,
                               bias=o_out[:, i, h * 66 + 65:h * 66 + 66]).then_inc(exp_done, 1)

        def copy_turned(act, g, a, i):
            act.wait_ge(t_done, 1 + a * 16 + (i + 1))
            act.wait_ge(pv_done, 1 + a * 16 + i)
            first = key_range(g, i)[2]
            view = lambda x: x[:, :, :].rearrange("p (h b) q -> p h b q", b=2)[:, :, first:, :]
            act.copy(view(probsT), view(t_ps)).then_inc(copy_done, 1)

        def leave_sums(dve, a, i):
            dve.wait_ge(pv_done, 1 + a * 16 + (i + 1))
            dve.tensor_copy(o_out[:, i, :].rearrange("p (h d) -> p h d", h=2)[:, :, 0:HD + 1], o_ps[:, :, :]).then_inc(o_done, 1)

        def pe_stage(pe, g, a, ng, n):
            for i in range(BLK):
                if a is not None:
                    score(pe, g, a, i)
                    if i:
                        weigh(pe, g, a, i - 1)
                if n is not None and 0 < i <= UNITS:
                    head_sums(pe, n, i - 1)
                if n is not None and i < UNITS:
                    project_unit(pe, ng, n, i)
                if a is not None:
                    turn(pe, g, a, i)
            if a is not None:
                weigh(pe, g, a, BLK - 1)

        def act_stage(act, g, a, ng, n):
            for i in range(BLK):
                if a is not None:
                    weights(act, g, a, i)
                if n is not None and i:
                    root(act, n, i - 1)
                if n is not None and i < UNITS:
                    square_unit(act, n, i)
                if a is not None:
                    copy_turned(act, g, a, i)

        def dve_stage(dve, g, a, ng, n):
            for i in range(BLK):
                if a is not None:
                    largest(dve, g, a, i)
                    if i:
                        leave_sums(dve, a, i - 1)
                if n is not None and 0 < i <= UNITS:
                    leave_unit(dve, ng, n, i - 1)
            if a is not None:
                leave_sums(dve, a, BLK - 1)

        def store_kv(pool, g, jp, n):
            pool.wait_ge(evac_done, 1 + n * UNITS + UNITS)
            w = (P, 512, SEQ)[g]
            kt, v = qk[1][g], v_sb[g]
            pool.dma_start(dr[f"kT_p{g}"][jp], kt[:, SEQ - w:SEQ]).then_inc(kv_out, 16)
            vb = (v[:, BLK - 1:BLK], v[:, 3:BLK:4], v[:, 0:BLK])[g]
            pool.dma_start(dr[f"v_p{g}"][jp], vb).then_inc(kv_out, 16)
            pool.dma_start(dr[f"kT_s{g}"][jp], kt[:, SEQ:NT]).then_inc(kv_out, 16)
            pool.dma_start(dr[f"v_s{g}"][jp].rearrange("t (h d) -> t h d", h=2), v[0:NS, BLK, :, 0:HD]).then_inc(kv_out, 16)
            pool.dma_start(dr["qT_s"][jp, g], qk[0][g][:, SEQ:NT]).then_inc(kv_out, 16)

        def store_sums(pool, g, jp, a, half):
            pool.wait_ge(o_done, 1 + a * 16 + 8 * (half + 1))
            rows = dr["sums"][g, jp]
            for quad in (2 * half, 2 * half + 1):
                if g == 0:
                    dst = rows.rearrange("(i p) c -> p i c", p=P)[:, 4 * quad:4 * quad + 4]
                elif g == 1:
                    dst = rows.rearrange("(b p r) c -> r p b c", p=P, r=4)[quad]
                else:
                    dst = rows.rearrange("(p i) c -> p i c", i=16)[:, 4 * quad:4 * quad + 4]
                pool.dma_start(dst, o_out[:, 4 * quad:4 * quad + 4, :]).then_inc(half_out[half], 16)

        def load_weights(sp, g, jp, kind):
            sp.dma_start(w_sb[kind][:, :, :], dr["w_qkv"][jp, g, kind]).then_inc(w_in[kind], 16)

        def load_distances(sp, g, jp):
            sp.dma_start(dist[g][:, :, :], dr["dist"][jp, g]).then_inc(dist_in, 16)

        def sp_stage(sp, g, jp, a, ng, njp, n, last):
            mg, mjp = ((ng + 1), njp) if n is not None and ng < 2 else (0, jp if n is None else njp + 1)
            load = n is not None and not last

            def load_after(kind):
                if load:
                    sp.wait_ge(unit_done, 1 + n * UNITS + 5 * (kind + 1))
                    load_weights(sp, mg, mjp, kind)

            if load:
                if a is not None:
                    sp.wait_ge(max_done, 1 + a * 32)
                load_distances(sp, mg, mjp)
            load_after(0)
            if a is not None:
                store_sums(sp, g, jp, a, 0)
            load_after(1)
            load_after(2)
            if a is not None:
                store_sums(sp, g, jp, a, 1)
            if n is not None:
                store_kv(sp, ng, njp, n)

        def stages(eng, stage):
            stage(eng, None, None, None, 0, 0, 0, False)

            def pair(jp, last):
                for g in range(G):
                    ng, njp = ((g + 1), jp) if g < 2 else (0, jp + 1)
                    n = jp * 3 + (g + 1)
                    if last and g == 2:
                        ng = njp = n = None
                    stage(eng, g, jp, jp * 3 + g, ng, njp, n, last and g == 1)

            with eng.Fori(0, PAIRS - 1) as jp:
                pair(jp, False)
            pair(PAIRS - 1, True)

        with nc.Block() as block:
            @block.sync
            def _(sp):
                sp.wait_ge(ones_set, 1 + G)
                sp.dma_start(gains[:, :], dr["qk_gain"]).then_inc(const_in, 16)
                sp.dma_start(ones_h[:, :], dr["ones_h"]).then_inc(const_in, 16)
                load_distances(sp, 0, 0)
                for kind in range(3):
                    load_weights(sp, 0, 0, kind)
                stages(sp, sp_stage)
                sp.wait_ge(kv_out, 1 + 12 * KV)
                sp.wait_ge(half_out[0], 1 + 12 * 32)
                sp.wait_ge(half_out[1], 1 + 12 * 32)

            @block.gpsimd
            def _(pool):
                first_signals(pool, sems)
                for g in range(G):
                    pool.memset(v_sb[g][:, :, :, HD:HD + 1], 1.0).then_inc(ones_set, 1)

            @block.tensor
            def _(pe):
                pe.wait_ge(const_in, 1 + 32)
                pe.wait_ge(ones_set, 1 + G)
                stages(pe, lambda e, g, jp, a, ng, njp, n, last: pe_stage(e, g, a, ng, n))

            @block.scalar
            def _(act):
                act.preload_act_table_set("natural_log_exp_and_others")
                stages(act, lambda e, g, jp, a, ng, njp, n, last: act_stage(e, g, a, ng, n))

            @block.vector
            def _(dve):
                dve.wait_ge(const_in, 1 + 32)
                dve.tensor_scalar(gains[:, 0:1], gains[:, 0:1], -(HD ** -0.5), None, ALU.mult).then_inc(gain_set, 1)
                dve.wait_ge(gain_set, 1 + 1)
                stages(dve, lambda e, g, jp, a, ng, njp, n, last: dve_stage(e, g, a, ng, n))


def phase_sample(nc, t, dr):
    COLS = 3 * CH + P + 3 * ST
    GROUP_OF_BANK = (1, 2, 2, 0)
    QJ = G * HD + 2 * ST
    with ExitStack() as ctx:
        sb = lambda name, *a: ctx.enter_context(nc.sbuf_tensor("sample_" + name, *a))
        ps = lambda name, *a: ctx.enter_context(nc.psum_tensor("sample_" + name, *a))
        sems = []

        def sem(name):
            sems.append(ctx.enter_context(nc.semaphore("sample_" + name)))
            return sems[-1]

        k_sb = [sb(f"k{c}", [P, PAIRS, CH if c < 3 else P], F32) for c in range(4)]
        v_sb = [sb(f"v{b}", [P, KEYS, CH], F32) for b in range(2)]
        v_new = [sb(f"v_new{b}", [G * ST, PAIRS, P], F32) for b in range(2)]
        q_all = sb("q_all", [P, PAIRS, G, NS], F32)
        k_all = sb("k_all", [P, PAIRS, G, NS], F32)
        q_diag = [sb(f"q_diag{b}", [P, PAIRS * QJ], F32) for b in range(2)]
        k_new = [sb(f"k_new{b}", [P, PAIRS, G, ST], F32) for b in range(2)]
        pen = sb("pen", [P, COLS], F32)
        probs = sb("probs", [P, COLS], F32)
        probsT = sb("probsT", [P, KEYS + 1, P], F32)
        least4 = sb("least4", [P, 4], F32)
        least = sb("least", [P, 1], F32)
        total = sb("total", [P, 1], F32)
        inv = sb("inv", [P, 1], F32)
        own, sel = sb("own", [P, CH], F32), sb("sel", [P, 2 * ST], F32)
        o_own = sb("o_own", [P, CH], F32)
        s_ps = [ps(f"s{c}", [P, CH], F32) for c in range(4)]
        t_ps = [ps(f"t{i}", [P, 4, P], F32) for i in range(2)]
        o_ps = ps("o", [P, CH], F32)
        ot_ps = ps("ot", [P, PAIRS, 2 * ST], F32)
        const_in = sem("const_loaded")
        k_in = [sem(f"k{c}_loaded") for c in range(4)]
        v_in = [sem(f"v{b}_loaded") for b in range(2)]
        vn_in = [sem(f"v_new{b}_loaded") for b in range(2)]
        zeroed, q_ready = sem("zeroed"), sem("q_ready")
        bank_done = [sem(f"bank{c}_done") for c in range(4)]
        max_done, least_done, exp_done, inv_done = (sem(n) for n in ("max_done", "least_done", "exp_done", "inv_done"))
        seen = sem("seen")
        t_done, copy_done, pv_done, own_done, ot_done, out_done = (sem(n) for n in
            ("t_done", "copy_done", "pv_done", "own_done", "ot_done", "out_done"))
        bank = lambda c: slice(c * CH, min((c + 1) * CH, COLS))

        with nc.Block() as block:
            @block.gpsimd
            def _(pool):
                first_signals(pool, sems)

            @block.sync
            def _(sp):
                for g in range(G):
                    sp.dma_start(k_all[:, :, g, :], dr[f"kT_s{g}"].rearrange("j p t -> p j t")).then_inc(const_in, 16)
                for j in range(PAIRS):
                    sp.dma_start(q_all[:, j], dr["qT_s"][j].rearrange("g p t -> p g t")).then_inc(const_in, 16)
                sp.dma_start(pen[:, :], dr["pen_s"]).then_inc(const_in, 16)
                sp.dma_start(own[:, :], dr["own_s"]).then_inc(const_in, 16)
                sp.dma_start(sel[:, :], dr["sel_s"]).then_inc(const_in, 16)
                with sp.Fori(0, SB // 2) as i:
                    for b in range(2):
                        for c in range(4):
                            sp.wait_ge(bank_done[c], 1 + i * 2 + b)
                            w = CH if c < 3 else P
                            sp.dma_start(k_sb[c][:, :, :], dr["kT_c"][i * 2 + b, :, :, c * CH:c * CH + w]).then_inc(k_in[c], 16)
                    for b in range(2):
                        sp.wait_ge(pv_done, 1 + i)
                        sp.dma_start(v_sb[b][:, :, :], dr["v_c"][i * 2 + b]).then_inc(v_in[b], 16)
                        for g in range(G):
                            rows = dr[f"v_s{g}"].rearrange("j (b t) c -> b t j c", t=ST)
                            sp.dma_start(v_new[b][g * ST:(g + 1) * ST], rows[i * 2 + b]).then_inc(vn_in[b], 16)

            @block.tensor
            def _(pe):
                with pe.Fori(0, SB // 2) as i:
                    for b in range(2):
                        rows = slice(64 * b, 64 * b + 64)
                        pe.wait_ge(q_ready, 1 + i * 2 + (b + 1))
                        pe.wait_ge(max_done, 1 + i * 4)
                        for c in range(4):
                            g = GROUP_OF_BANK[c]
                            pe.wait_ge(k_in[c], 1 + i * 32 + 16 * (b + 1))
                            w = CH if c < 3 else P
                            for j in range(PAIRS):
                                lhsT = q_diag[b][:, j * G * HD + g * HD:j * G * HD + (g + 1) * HD]
                                mm = pe.matmul(s_ps[c][rows, 0:w], lhsT, k_sb[c][:, j, :], start=(j == 0), stop=(j == PAIRS - 1))
                            if c == 3:
                                for g in range(G):
                                    for j in range(PAIRS):
                                        lhsT = q_diag[b][:, j * G * HD + g * HD:j * G * HD + (g + 1) * HD]
                                        mm = pe.matmul(s_ps[3][rows, P + g * ST:P + (g + 1) * ST], lhsT, k_new[b][:, j, g, :],
                                                       start=(j == 0), stop=(j == PAIRS - 1))
                            mm.then_inc(bank_done[c], 1)
                    pe.wait_ge(exp_done, 1 + i + 1)
                    for r in range(4):
                        pe.wait_ge(copy_done, 1 + i * 4 + max(r - 1, 0))
                        for m in range(4 * r, min(4 * r + 4, KEYS + 1)):
                            n = P if m < KEYS else G * ST
                            mm = pe.transpose(t_ps[r % 2][0:n, m % 4, :], probs[:, m * P:m * P + n], t["ident"][:, :])
                        mm.then_inc(t_done, 1)
                    pe.wait_ge(copy_done, 1 + i * 4 + 4)
                    pe.wait_ge(own_done, 1 + i)
                    for b in range(2):
                        rows = slice(64 * b, 64 * b + 64)
                        pe.wait_ge(v_in[b], 1 + i * 16 + 16)
                        for m in range(KEYS):
                            pe.matmul(o_ps[rows, :], probsT[:, m, rows], v_sb[b][:, m, :], start=(m == 0), stop=False)
                        pe.wait_ge(vn_in[b], 1 + i * 48 + 48)
                        mm = pe.matmul(o_ps[rows, :], probsT[0:G * ST, KEYS, rows],
                                       v_new[b][:, :, :].rearrange("p j c -> p (j c)"), start=False, stop=True)
                    mm.then_inc(pv_done, 1)
                    pe.wait_ge(own_done, 1 + i + 1)
                    pe.wait_ge(out_done, 1 + i)
                    for j in range(PAIRS):
                        mm = pe.matmul(ot_ps[:, j, :], o_own[:, j * P:(j + 1) * P], sel[:, :], start=True, stop=True)
                    mm.then_inc(ot_done, 1)

            @block.scalar
            def _(act):
                act.preload_act_table_set("natural_log_exp_and_others")
                with act.Fori(0, SB // 2) as i:
                    act.wait_ge(least_done, 1 + i + 1)
                    act.wait_ge(inv_done, 1 + i)
                    act.activation(probs[:, :], probs[:, :], ACT.Exp, scale=-1.0, bias=least[:, 0:1],
                                   accum_out=total[:, 0:1]).then_inc(exp_done, 1)
                    for r in range(4):
                        act.wait_ge(t_done, 1 + i * 4 + (r + 1))
                        act.wait_ge(pv_done, 1 + i)
                        n = 4 if r < 3 else 1
                        act.copy(probsT[:, 4 * r:4 * r + n, :], t_ps[r % 2][:, 0:n, :]).then_inc(copy_done, 1) if r < 3 else \
                            act.copy(probsT[:, 12:13, :], t_ps[1][:, 0:1, :])
                    act.copy(probsT[0:G * ST, KEYS, :], t_ps[1][0:G * ST, 1, :]).then_inc(copy_done, 1)

            @block.vector
            def _(dve):
                for b in range(2):
                    dve.memset(q_diag[b][:, :], 0.0).then_inc(zeroed, 1)
                dve.wait_ge(zeroed, 1 + 2)
                dve.wait_ge(const_in, 1 + 16 * (G + PAIRS + 3))
                with dve.Fori(0, SB // 2) as i:
                    for b in range(2):
                        dve.wait_ge(bank_done[3], 1 + i * 2)
                        new = bass.ds(i * 2 * ST + b * ST, ST)
                        for h in range(2):
                            rows = slice(HD * h, HD * (h + 1))
                            dst = q_diag[b][rows, :].rearrange("p (j x) -> p j x", x=QJ)[:, :, 0:G * HD]
                            dst = dst.rearrange("p j (g y) -> p j g y", y=HD)[:, :, :, h * ST:(h + 1) * ST]
                            dve.tensor_copy(dst, q_all[rows, :, :, new])
                        dve.tensor_copy(k_new[b][:, :, :, :], k_all[:, :, :, new]).then_inc(q_ready, 1)
                    dve.wait_ge(t_done, 1 + i * 4)
                    for c in range(4):
                        dve.wait_ge(bank_done[c], 1 + i * 2 + 2)
                        dve.sem_inc(seen, 1)
                        n = bank(c).stop - bank(c).start
                        dve.tensor_tensor_reduce(probs[:, bank(c)], s_ps[c][:, 0:n], pen[:, bank(c)], 1.0, 3.0e38,
                                                 ALU.add, ALU.min, least4[:, c:c + 1]).then_inc(max_done, 1)
                    dve.wait_ge(max_done, 1 + i * 4 + 4)
                    dve.tensor_reduce(least[:, :], least4[:, :], AX.X, ALU.min).then_inc(least_done, 1)
                    dve.wait_ge(exp_done, 1 + i + 1)
                    dve.reciprocal(inv[:, :], total[:, :]).then_inc(inv_done, 1)
                    dve.wait_ge(inv_done, 1 + i + 1)
                    dve.wait_ge(pv_done, 1 + i + 1)
                    dve.scalar_tensor_tensor(out=o_own[:, :], in0=o_ps[:, :], scalar=inv[:, 0:1], in1=own[:, :],
                                             op0=ALU.mult, op1=ALU.mult).then_inc(own_done, 1)
                    dve.wait_ge(ot_done, 1 + i + 1)
                    dve.tensor_copy(t["oT_s"][:, :, bass.ds(i * 2 * ST, 2 * ST)], ot_ps[:, :, :]).then_inc(out_done, 1)


def phase_hgrn(nc, t, dr):
    with ExitStack() as ctx:
        sb = lambda name, *a: ctx.enter_context(nc.sbuf_tensor("hgrn_" + name, *a))
        ps = lambda name, *a: ctx.enter_context(nc.psum_tensor("hgrn_" + name, *a))
        sems = []

        def sem(name):
            sems.append(ctx.enter_context(nc.semaphore("hgrn_" + name)))
            return sems[-1]

        hT = t["hT"]
        w_sb = [sb(f"w{k}", [P, KD, P], F32) for k in range(3)]
        q_neg = sb("q_neg", [P, NT], F32)
        f_sb = sb("f", [P, NT], F32)
        v_sb = sb("v", [P, BLK + 1, P], F32)
        e_u = [sb(f"e_u{k}", [P, CH], F32) for k in range(2)]
        log_f, b_sum, e_b, q_in = (sb(n, [P, CH], F32) for n in ("log_f", "b_sum", "e_b", "q_in"))
        d_sb = [sb(f"d{i}", [P, CH], F32) for i in range(2)]
        x_sb = [sb(f"x{i}", [P, CH], F32) for i in range(2)]
        keys, k_out = sb("keys", [P, CH], F32), sb("k_out", [P, CH], F32)
        k_turned = sb("k_turned", [P, 4, P], F32)
        att = sb("att", [P, 4, P], F32)
        state = sb("state", [P, 5, P], F32)
        state_o = sb("state_o", [P, P], F32)
        s0 = sb("s0", [P, SB, P], F32)
        s_new = sb("s_new", [P, SB, P], F32)
        v_seq = sb("v_seq", [NS, SB, P], F32)
        sq, log_ms, rstd = sb("sq", [P, CH], F32), sb("log_ms", [P, CH], F32), sb("rstd", [P, CH], F32)
        level = sb("level", [P, 8, P], U32)
        seq = sb("seq", [NS, SB], F32)
        ones_i, ones = sb("ones_i", [P, P], F32), sb("ones", [P, P], F32)
        o_gain = sb("o_gain", [P, 1], F32)
        lb2, lb_e = sb("lb2", [P, 2, BH], F32), sb("lb_e", [P, 2, BH], F32)
        lb_s, lb, lb1 = (sb(n, [P, BH], F32) for n in ("lb_s", "lb", "lb1"))
        u_ps = [ps(f"u{k}", [P, CH], F32) for k in range(3)]
        l_ps = [ps(f"l{i}", [P, 4, P], F32) for i in range(2)]
        kd_ps = ps("kd", [P, 4, P], F32)
        o_ps = ps("o", [P, CH], F32)
        ss_ps = ps("ss", [P, CH], F32)
        const_in = sem("const_loaded")
        w_in = [sem(f"w{k}_loaded") for k in range(3)]
        s0_in, state_out, s_new_out = sem("s0_loaded"), sem("state_stored"), sem("s_new_stored")
        names = ("lb_steps unit_done eu_done min_done log1_done max_done sig_done evac_done logf_done b_done eb_done qin_done d_done e_done "
                 "x_done xk_done l_done pred_done kt_done kcopy_done ds_done chain_done carry_done o_done sq_done ss_done "
                 "log_done r_done out_done seen vseq_done snew_half snew_done stateo_done ones_set").split()
        s = {n: sem(n) for n in names}

        def at(h, j, quad, sample, k):
            return h * (4 * quad + sample) + (j * quad + k)

        width = lambda j: CH if j < 4 else NS
        cols = lambda j: slice(j * CH, j * CH + width(j))
        span = lambda j: (4, P) if j < 4 else (SB, ST)
        levels = lambda j: 7 if j < 4 else 3
        RND, XS, LV = (8, 4), (8, 4), (8, 4)

        def project(pe, h, j, kind, part=(0, 8)):
            if h is None:
                return
            if part[0] == 0:
                if j or not isinstance(h, int):
                    pe.wait_ge(s["evac_done"], 1 + at(h, j, 3, 3, kind - 2))
                pe.wait_ge(w_in[kind], 1 + h * 16 + 16)
            u = u_ps[kind]
            if kind < 2:
                for k in range(*part):
                    mm = pe.matmul(u[:, 0:width(j)], w_sb[kind][:, k, :], hT[:, k, cols(j)], start=(k == 0), stop=(k == KD - 1))
            else:
                for b in range(part[0] // 2, part[1] // 2) if j < 4 else (0,) if part[1] == 8 else ():
                    n = P if j < 4 else NS
                    lo = j * CH + b * P
                    for k in range(KD):
                        mm = pe.matmul(u[0:n, b * P:(b + 1) * P], hT[:, k, lo:lo + n], w_sb[2][:, k, :],
                                       start=(k == 0), stop=(k == KD - 1))
            if part[1] == 8:
                mm.then_inc(s["unit_done"], 1)

        def gate_on_act(act, h, j, kind, part):
            n = width(j)
            e = e_u[kind][:, 0:n]
            if part == 0:
                act.wait_ge(s["unit_done"], 1 + at(h, j, 3, 3, kind + 1))
                act.wait_ge(s["evac_done"], 1 + at(h, j, 3, 3, 0))
                act.activation(e, u_ps[kind][:, 0:n], ACT.Exp, scale=-1.0).then_inc(s["eu_done"], 1)
            elif part == 1:
                act.wait_ge(s["min_done"], 1 + at(h, j, 2, 2, kind + 1))
                act.activation(e, e, ACT.Ln, bias=1.0).then_inc(s["log1_done"], 1)
            else:
                act.wait_ge(s["max_done"], 1 + at(h, j, 2, 2, kind + 1))
                act.activation(e, e, ACT.Exp, scale=-1.0).then_inc(s["sig_done"], 1)

        def gate_on_dve(dve, h, j, kind, part):
            n = width(j)
            e = e_u[kind][:, 0:n]
            if part == 0:
                dve.wait_ge(s["eu_done"], 1 + at(h, j, 2, 2, kind + 1))
                dve.tensor_scalar(e, e, 1.0e18, None, ALU.min).then_inc(s["min_done"], 1)
            elif part == 1:
                dve.wait_ge(s["log1_done"], 1 + at(h, j, 2, 2, kind + 1))
                dve.scalar_tensor_tensor(out=e, in0=u_ps[kind][:, 0:n], scalar=-1.0, in1=e,
                                         op0=ALU.mult, op1=ALU.max).then_inc(s["max_done"], 1)
            elif kind == 0:
                dve.wait_ge(s["sig_done"], 1 + at(h, j, 2, 2, 1))
                dve.scalar_tensor_tensor(out=q_neg[:, cols(j)], in0=u_ps[0][:, 0:n], scalar=-1.0, in1=e,
                                         op0=ALU.mult, op1=ALU.mult).then_inc(s["evac_done"], 1)
            else:
                dve.wait_ge(s["sig_done"], 1 + at(h, j, 2, 2, 2))
                dve.tensor_scalar(f_sb[:, cols(j)], e, col(lb1, h), col(lb, h), ALU.mult, ALU.add).then_inc(s["evac_done"], 1)

        def evacuate_values(dve, h, j):
            dve.wait_ge(s["unit_done"], 1 + at(h, j, 3, 3, 3))
            if j < 4:
                dve.tensor_copy(v_sb[:, 4 * j:4 * j + 4, :], u_ps[2][:, :].rearrange("p (b c) -> p b c", b=4)) \
                   .then_inc(s["evac_done"], 1)
            else:
                dve.tensor_copy(v_sb[0:NS, BLK, :], u_ps[2][0:NS, 0:P]).then_inc(s["evac_done"], 1)

        ACT_PARTS = {2: ((0, 0),), 3: ((0, 1),), 4: ((0, 2),), 5: ((1, 0),), 6: ((1, 1),), 7: ((1, 2),)}
        ACT_PARTS_S = {2: ((0, 0),), 3: ((0, 1), (0, 2), (1, 0), (1, 1), (1, 2))}
        DVE_PARTS = {2: ((0, 0),), 3: ((0, 1),), 5: ((0, 2), (1, 0)), 6: ((1, 1),)}
        DVE_PARTS_S = {2: ((0, 0),), 3: ((0, 1),)}
        DVE_LAST, DVE_LAST_S = ((1, 2),), ((0, 2), (1, 0), (1, 1), (1, 2))

        def col(x, h):
            return x[:, h:h + 1] if isinstance(h, int) else x[:, bass.ds(h, 1)]

        def halves(x, j, l):
            v = x[:, 0:width(j)].rearrange("p (n w) -> p n w", w=1 << l)
            return v[:, :, 0:1 << (l - 1)], v[:, :, 1 << (l - 1):]

        def difference(dve, h, j, r):
            d = d_sb[r % 2]
            dve.wait_ge(s["x_done"], 1 + at(h, j, *XS, r - 1 if r > 1 else 0))
            dve.wait_ge(s["xk_done"], 1 + at(h, j, *RND, r - 1 if r > 1 else 0))
            if r == 0:
                n, w = span(j)
                v = b_sum[:, 0:width(j)].rearrange("p (n w) -> p n w", w=w)
                dve.tensor_tensor(d[:, 0:width(j)].rearrange("p (n w) -> p n w", w=w),
                                  v[:, :, w - 1:w].broadcast_to([P, n, w]), v, ALU.subtract).then_inc(s["d_done"], 1)
                return
            (d1, d2), (b1, b2) = halves(d, j, r), halves(b_sum, j, r)
            n, w = width(j) >> r, 1 << (r - 1)
            mid = b1[:, :, w - 1:w].broadcast_to([P, n, w])
            dve.tensor_tensor(d1, mid, b1, ALU.subtract)
            dve.tensor_tensor(d2, b2, mid, ALU.subtract).then_inc(s["d_done"], 1)

        def exponent(act, h, j, r):
            d = d_sb[r % 2][:, 0:width(j)]
            act.wait_ge(s["d_done"], 1 + at(h, j, *RND, r + 1))
            act.activation(d, d, ACT.Exp).then_inc(s["e_done"], 1)

        def scaled_keys(pool, h, j, r):
            pool.wait_ge(s["e_done"], 1 + at(h, j, *RND, r + 1))
            if r == 0:
                out, k, d = (x[:, 0:width(j)] for x in (k_out, keys, d_sb[0]))
                pool.wait_ge(s["x_done"], 1 + at(h, j, *XS, 1))
                pool.wait_ge(s["kt_done"], 1 + at(h, j, 1, 1, 0))
            else:
                out, k, d = (halves(x, j, r)[0] for x in (x_sb[r % 2], keys, d_sb[r % 2]))
                pool.wait_ge(s["l_done"], 1 + at(h, j, *LV, r - 1))
            pool.tensor_tensor(out, k, d, ALU.mult).then_inc(s["xk_done"], 1)

        def scaled_queries(dve, h, j, r):
            dve.wait_ge(s["e_done"], 1 + at(h, j, *RND, r + 1))
            dve.wait_ge(s["l_done"], 1 + at(h, j, *LV, r - 1))
            x2, d2, q2 = (halves(v, j, r)[1] for v in (x_sb[r % 2], d_sb[r % 2], q_neg[:, cols(j)]))
            dve.tensor_tensor(x2, q2, d2, ALU.mult).then_inc(s["x_done"], 1)

        def level_product(pe, h, j, l):
            pe.wait_ge(s["x_done"], 1 + at(h, j, *XS, l + 1))
            if l:
                pe.wait_ge(s["xk_done"], 1 + at(h, j, *RND, l + 1))
            if l == 0 and j == 0:
                pe.wait_ge(s["snew_done"], 1 + h)
            pe.wait_ge(s["pred_done"], 1 + at(h, j, *LV, max(l - 1, 0)))
            n = 4 if j < 4 else 1
            w = P if j < 4 else NS
            for c in range(n):
                x = (x_sb[l % 2] if l else keys)[:, c * w:(c + 1) * w]
                y = x if l else q_neg[:, j * CH + c * w:j * CH + (c + 1) * w]
                mm = pe.matmul(l_ps[l % 2][0:w, c, 0:w], x, y, start=True, stop=True)
            mm.then_inc(s["l_done"], 1)

        def take_level(dve, h, j, l):
            dve.wait_ge(s["l_done"], 1 + at(h, j, *LV, l + 1))
            n, w = (4, P) if j < 4 else (1, NS)
            src, dst = l_ps[l % 2][0:w, 0:n, 0:w], att[0:w, 0:n, 0:w]
            if l == 0:
                dve.wait_ge(s["o_done"], 1 + at(h, j, 1, 1, 0))
                dve.tensor_tensor(dst, src, t["ident"][0:w, 0:w].unsqueeze(1).broadcast_to([w, n, w]), ALU.mult) \
                   .then_inc(s["pred_done"], 1)
            else:
                dve.wait_ge(s["pred_done"], 1 + at(h, j, *LV, l))
                dve.sem_inc(s["seen"], 1)
                dve.copy_predicated(dst, level[0:w, l:l + 1, 0:w].broadcast_to([w, n, w]), src).then_inc(s["pred_done"], 1)

        def turn_keys(pe, h, j):
            pe.wait_ge(s["xk_done"], 1 + at(h, j, *RND, 1))
            pe.wait_ge(s["chain_done"], 1 + at(h, j, 4, 0, 0))
            pe.wait_ge(s["kcopy_done"], 1 + at(h, j, 1, 1, 0))
            for c in range(4 if j < 4 else 1):
                mm = pe.transpose(kd_ps[:, c, :], k_out[:, c * P:(c + 1) * P], t["ident"][:, :])
            mm.then_inc(s["kt_done"], 1)

        def increments(pe, h, j):
            pe.wait_ge(s["kcopy_done"], 1 + at(h, j, 1, 1, 1))
            if j < 4:
                for c in range(4):
                    mm = pe.matmul(kd_ps[:, c, :], k_turned[:, c, :], v_sb[:, 4 * j + c, :], start=True, stop=True)
            else:
                pe.wait_ge(s["vseq_done"], 1 + h + 1)
                pe.wait_ge(s["pred_done"], 1 + at(h, j, *LV, 4))
                for b in range(2):
                    mm = pe.matmul(l_ps[b][:, :, :], k_turned[0:NS, 0, :],
                                   v_seq[:, 4 * b:4 * b + 4, :], start=True, stop=True)
            mm.then_inc(s["ds_done"], 1)

        def outputs(pe, h, j):
            pe.wait_ge(s["pred_done"], 1 + at(h, j, *LV, LV[j == 4]))
            pe.wait_ge(s["qin_done"], 1 + at(h, j, 1, 1, 1))
            pe.wait_ge(s["out_done"], 1 + at(h, j, 1, 1, 0))
            if j < 4:
                pe.wait_ge(s["chain_done"], 1 + at(h, j, 4, 0, 3))
                for c in range(4):
                    o = o_ps[:, c * P:(c + 1) * P]
                    pe.matmul(o, v_sb[:, 4 * j + c, :], att[:, c, :], start=True, stop=False)
                    mm = pe.matmul(o, state[:, c, :], q_in[:, c * P:(c + 1) * P], start=False, stop=True)
            else:
                pe.wait_ge(s0_in, 1 + h * 16 + 16)
                pe.matmul(o_ps[:, 0:NS], v_sb[0:NS, BLK, :], att[0:NS, 0, 0:NS], start=True, stop=True,
                          skip_group_check=True)
                for b in range(SB):
                    mm = pe.matmul(o_ps[:, b * ST:(b + 1) * ST], s0[:, b, :], q_in[:, b * ST:(b + 1) * ST],
                                   start=False, stop=True, skip_group_check=True)
            mm.then_inc(s["o_done"], 1)

        def pe_step(pe, h, j, hp, jp):
            if h is None:
                for kind in range(3):
                    project(pe, hp, jp, kind)
                return
            project(pe, hp, jp, 0)
            level_product(pe, h, j, 0)
            turn_keys(pe, h, j)
            level_product(pe, h, j, 1)
            if j < 4:
                for l, kind, part in ((2, 1, (0, 3)), (3, 1, (3, 6)), (4, 1, (6, 8)), (5, 2, (0, 2)), (6, 2, (2, 4)), (7, 2, (4, 8))):
                    project(pe, hp, jp, kind, part)
                    level_product(pe, h, j, l)
                    if l == 4:
                        increments(pe, h, j)
            else:
                project(pe, hp, jp, 1)
                level_product(pe, h, j, 2)
                project(pe, hp, jp, 2)
                level_product(pe, h, j, 3)
                increments(pe, h, j)
            outputs(pe, h, j)
            pe.wait_ge(s["sq_done"], 1 + at(h, j, 1, 1, 1))
            pe.wait_ge(s["log_done"], 1 + at(h, j, 1, 1, 0))
            pe.matmul(ss_ps[:, 0:width(j)], ones_i[:, :], sq[:, 0:width(j)], start=True, stop=True).then_inc(s["ss_done"], 1)

        def act_step(act, h, j, hp, jp):
            if h is None:
                for kind in range(2):
                    for part in range(3):
                        gate_on_act(act, hp, jp, kind, part)
                return
            n = width(j)
            act.wait_ge(s["evac_done"], 1 + at(h, j, 3, 3, 2))
            act.wait_ge(s["b_done"], 1 + at(h, j, 1, 1, 0))
            act.activation(log_f[:, 0:n], f_sb[:, cols(j)], ACT.Ln).then_inc(s["logf_done"], 1)
            act.wait_ge(s["b_done"], 1 + at(h, j, 1, 1, 1))
            act.wait_ge(s["chain_done"], 1 + at(h, j, 4, 0, 0))
            act.wait_ge(s["snew_half"], 1 + h)
            act.activation(e_b[:, 0:n], b_sum[:, 0:n], ACT.Exp).then_inc(s["eb_done"], 1)
            exponent(act, h, j, 0)
            L = levels(j)
            for r in range(1, L + 1):
                exponent(act, h, j, r)
                if r == 1:
                    act.wait_ge(s["kt_done"], 1 + at(h, j, 1, 1, 1))
                    if j < 4:
                        act.copy(k_turned[:, :, :], kd_ps[:, :, :]).then_inc(s["kcopy_done"], 1)
                    else:
                        act.copy(k_turned[0:NS, 0, :], kd_ps[0:NS, 0, :]).then_inc(s["kcopy_done"], 1)
                for kind, part in (ACT_PARTS if j < 4 else ACT_PARTS_S).get(r, ()) if hp is not None else ():
                    gate_on_act(act, hp, jp, kind, part)
            act.wait_ge(s["o_done"], 1 + at(h, j, 1, 1, 1))
            act.activation(sq[:, 0:n], o_ps[:, 0:n], ACT.Square).then_inc(s["sq_done"], 1)
            act.wait_ge(s["ss_done"], 1 + at(h, j, 1, 1, 1))
            act.activation(log_ms[:, 0:n], ss_ps[:, 0:n], ACT.Ln, bias=t["eps"][:, 0:1]).then_inc(s["log_done"], 1)
            act.wait_ge(s["log_done"], 1 + at(h, j, 1, 1, 1))
            act.wait_ge(s["out_done"], 1 + at(h, j, 1, 1, 0))
            act.activation(rstd[:, 0:n], log_ms[:, 0:n], ACT.Exp, scale=-0.5).then_inc(s["r_done"], 1)

        def write_output(dve, h, j):
            dve.wait_ge(s["r_done"], 1 + at(h, j, 1, 1, 1))
            n = width(j)
            dst = t["oT_b"][:, h, cols(j)] if isinstance(h, int) else \
                t["oT_b"][:, bass.ds(h, 1), cols(j)].rearrange("p a c -> p (a c)")
            dve.scalar_tensor_tensor(out=dst, in0=o_ps[:, 0:n], scalar=o_gain[:, 0:1], in1=rstd[:, 0:n],
                                     op0=ALU.mult, op1=ALU.mult).then_inc(s["out_done"], 1)

        def dve_step(dve, h, j, hp, jp):
            if h is None:
                for kind in range(2):
                    for part in range(3):
                        gate_on_dve(dve, hp, jp, kind, part)
                evacuate_values(dve, hp, jp)
                return
            n = width(j)
            L = levels(j)
            dve.wait_ge(s["logf_done"], 1 + at(h, j, 1, 1, 1))
            dve.wait_ge(s["d_done"], 1 + at(h, j, *RND, 0))
            nch, w = span(j)
            for c in range(nch):
                scan = dve.tensor_tensor_scan(b_sum[:, c * w:(c + 1) * w], ones[:, 0:w], log_f[:, c * w:(c + 1) * w], 0.0,
                                              ALU.mult, ALU.add)
            scan.then_inc(s["b_done"], 1)
            dve.wait_ge(s["b_done"], 1 + at(h, j, 1, 1, 1))
            difference(dve, h, j, 0)
            difference(dve, h, j, 1)
            dve.tensor_scalar(keys[:, 0:n], f_sb[:, cols(j)], -1.0, None, ALU.add).then_inc(s["x_done"], 1)
            difference(dve, h, j, 2)
            dve.wait_ge(s["eb_done"], 1 + at(h, j, 1, 1, 1))
            if j < 4:
                dve.tensor_tensor(q_in[:, 0:n], q_neg[:, cols(j)], e_b[:, 0:n], ALU.mult).then_inc(s["qin_done"], 1)
            else:
                dve.scalar_tensor_tensor(out=q_in[:, 0:n], in0=q_neg[:, cols(j)], scalar=-1.0, in1=e_b[:, 0:n],
                                         op0=ALU.mult, op1=ALU.mult).then_inc(s["qin_done"], 1)
            for r in range(1, L + 1):
                scaled_queries(dve, h, j, r)
                take_level(dve, h, j, r - 1)
                if r + 2 <= L:
                    difference(dve, h, j, r + 2)
                for kind, part in (DVE_PARTS if j < 4 else DVE_PARTS_S).get(r, ()) if hp is not None else ():
                    gate_on_dve(dve, hp, jp, kind, part)
                if r == 4:
                    chain(dve, h, j)
            if j == 4:
                dve.wait_ge(s["o_done"], 1 + at(h, j, 1, 1, 0))
                dve.tensor_tensor(v_seq[:, :, :], v_sb[0:NS, BLK, :].unsqueeze(1).broadcast_to([NS, SB, P]),
                                  seq[:, :].unsqueeze(2).broadcast_to([NS, SB, P]), ALU.mult).then_inc(s["vseq_done"], 1)
            take_level(dve, h, j, L)
            if hp is not None:
                for kind, part in DVE_LAST if j < 4 else DVE_LAST_S:
                    gate_on_dve(dve, hp, jp, kind, part)
                evacuate_values(dve, hp, jp)
            if j == 4:
                new_states(dve, h)
            write_output(dve, h, j)
            if j < 4:
                dve.tensor_copy(state[:, 0, :], state[:, 4, :]).then_inc(s["carry_done"], 1)
                dve.wait_ge(s["carry_done"], 1 + h * 5 + (j + 1))
            if j == 3:
                dve.wait_ge(state_out, 1 + h * 16)
                dve.tensor_scalar(state_o[:, :], state[:, 4, :], -1.0, None, ALU.mult).then_inc(s["stateo_done"], 1)
            if j == 4:
                dve.memset(state[:, 0, :], 0.0).then_inc(s["carry_done"], 1)
                dve.wait_ge(s["carry_done"], 1 + h * 5 + 5)

        def pool_step(pool, h, j, hp, jp):
            for r in range(levels(j) + 1 if h is not None else 0):
                scaled_keys(pool, h, j, r)

        def chain(dve, h, j):
            if j == 4:
                return
            dve.wait_ge(s["ds_done"], 1 + at(h, j, 1, 1, 1))
            for c in range(4):
                dve.scalar_tensor_tensor(out=state[:, c + 1, :], in0=state[:, c, :], scalar=e_b[:, c * P + P - 1:c * P + P],
                                         in1=kd_ps[:, c, :], op0=ALU.mult, op1=ALU.add).then_inc(s["chain_done"], 1)
                dve.wait_ge(s["chain_done"], 1 + at(h, j, 4, 0, c + 1))

        def new_states(dve, h):
            dve.wait_ge(s0_in, 1 + h * 16 + 16)
            dve.wait_ge(s_new_out, 1 + h * 16)
            decay = e_b[:, ST - 1:NS:ST].unsqueeze(2).broadcast_to([P, SB, P])
            dve.tensor_tensor(s_new[:, :, :], s0[:, :, :], decay, ALU.mult).then_inc(s["snew_half"], 1)
            dve.wait_ge(s["snew_half"], 1 + h + 1)
            dve.wait_ge(s["ds_done"], 1 + at(h, 4, 1, 1, 1))
            for b in range(2):
                part = s_new[:, 4 * b:4 * b + 4, :]
                last = dve.tensor_tensor(part, part, l_ps[b][:, :, :], ALU.subtract)
            last.then_inc(s["snew_done"], 1)

        def sp_step(sp, h, j, hp, jp):
            if h is None:
                return
            if j == 0:
                for kind in range(3):
                    if hp is not None and h is not LAST:
                        sp.wait_ge(s["unit_done"], 1 + at(h, 4, 3, 3, kind + 1))
                        sp.dma_start(w_sb[kind][:, :, :], dr["w_b"][h + 1, kind]).then_inc(w_in[kind], 16)
                sp.wait_ge(s["out_done"], 1 + at(h, 0, 1, 1, 0))
                sp.dma_start(s0[:, :, :], dr["state"][h]).then_inc(s0_in, 16)
            if j == 3:
                sp.wait_ge(s["stateo_done"], 1 + h + 1)
                sp.dma_start(dr["state_p"][h], state_o[:, :]).then_inc(state_out, 16)
            if j == 4:
                sp.wait_ge(s["snew_done"], 1 + h + 1)
                sp.dma_start(dr["state_s"][h], s_new[:, :, :]).then_inc(s_new_out, 16)

        LAST = BH - 1

        def heads(eng, step):
            for j in range(4):
                step(eng, None, None, 0, j)

            def head(h):
                step(eng, h, 0, h, 4)
                for j in range(1, 5):
                    step(eng, h, j, *((h + 1, j - 1) if h is not LAST else (None, None)))

            with eng.Fori(0, LAST) as h:
                head(h)
            head(LAST)

        with nc.Block() as block:
            @block.gpsimd
            def _(pool):
                first_signals(pool, sems)
                heads(pool, pool_step)

            @block.sync
            def _(sp):
                for dst, src in ((level[:, :, :], "level"), (seq[:, :], "seq_s"), (ones_i[:, :], "ones_i"),
                                 (o_gain[:, :], "o_gain"), (lb2[:, :, :], "lb")):
                    sp.dma_start(dst, dr[src]).then_inc(const_in, 16)
                for kind in range(3):
                    sp.dma_start(w_sb[kind][:, :, :], dr["w_b"][0, kind]).then_inc(w_in[kind], 16)
                heads(sp, sp_step)
                sp.wait_ge(state_out, 1 + 16 * BH)
                sp.wait_ge(s_new_out, 1 + 16 * BH)

            @block.tensor
            def _(pe):
                pe.wait_ge(const_in, 1 + 80)
                heads(pe, pe_step)

            @block.scalar
            def _(act):
                act.preload_act_table_set("natural_log_exp_and_others")
                act.wait_ge(s["lb_steps"], 1 + 2)
                act.activation(lb_e[:, :, :], lb2[:, :, :], ACT.Exp).then_inc(s["lb_steps"], 1)
                heads(act, act_step)

            @block.vector
            def _(dve):
                dve.memset(ones[:, :], 1.0).then_inc(s["ones_set"], 1)
                dve.memset(state[:, 0, :], 0.0).then_inc(s["ones_set"], 1)
                dve.wait_ge(s["ones_set"], 1 + 2)
                dve.wait_ge(const_in, 1 + 80)
                dve.tensor_tensor(lb_s[:, :], lb2[:, 0, :], lb2[:, 1, :], ALU.max).then_inc(s["lb_steps"], 1)
                dve.wait_ge(s["lb_steps"], 1 + 1)
                dve.tensor_tensor(lb2[:, :, :], lb2[:, :, :], lb_s[:, :].unsqueeze(1).broadcast_to([P, 2, BH]),
                                  ALU.subtract).then_inc(s["lb_steps"], 1)
                dve.wait_ge(s["lb_steps"], 1 + 3)
                dve.tensor_tensor(lb_s[:, :], lb_e[:, 0, :], lb_e[:, 1, :], ALU.add).then_inc(s["lb_steps"], 1)
                dve.wait_ge(s["lb_steps"], 1 + 4)
                dve.reciprocal(lb_s[:, :], lb_s[:, :]).then_inc(s["lb_steps"], 1)
                dve.wait_ge(s["lb_steps"], 1 + 5)
                dve.tensor_tensor(lb[:, :], lb_e[:, 0, :], lb_s[:, :], ALU.mult).then_inc(s["lb_steps"], 1)
                dve.wait_ge(s["lb_steps"], 1 + 6)
                dve.tensor_scalar(lb1[:, :], lb[:, :], -1.0, 1.0, ALU.mult, ALU.add).then_inc(s["lb_steps"], 1)
                dve.wait_ge(s["lb_steps"], 1 + 7)
                heads(dve, dve_step)


def phase_join(nc, t, dr):
    UNITS = 10
    UNITS_OF_STEP = ((0,), (1,), (2,), (3, 4), (5,), (6,), (7,), (8, 9))
    SMALL, STEPS = 7, 5
    with ExitStack() as ctx:
        sb = lambda name, *a: ctx.enter_context(nc.sbuf_tensor("join_" + name, *a))
        ps = lambda name, *a: ctx.enter_context(nc.psum_tensor("join_" + name, *a))
        sems = []

        def sem(name):
            sems.append(ctx.enter_context(nc.semaphore("join_" + name)))
            return sems[-1]

        hT, oT_a, oT_b = t["hT"], t["oT_a"], t["oT_b"]
        rows = [sb(f"rows{i}", [P, G * 8, HD + 2], F32) for i in range(2)]
        w_z = [sb(f"w_z{i}", [P, KD, P], F32) for i in range(2)]
        least, den, inv = sb("least", [P, 8], F32), sb("den", [P, G * 8], F32), sb("inv", [P, 8], F32)
        wgt = sb("wgt", [P, G * 8], F32)
        joined = [sb(f"joined{i}", [P, 8, HD], F32) for i in range(2)]
        part = sb("part", [P, 8, HD], F32)
        gate_buf = [sb(f"gate_buf{i}", [P, CH], F32) for i in range(2)]
        silu = [sb(f"silu{i}", [P, CH], F32) for i in range(2)]
        z_ps = [ps(f"z{i}", [P, CH], F32) for i in range(5)]
        t_ps = [ps(f"t{i}", [P, 4, P], F32) for i in range(2)]
        rows_in = [sem(f"rows{i}_loaded") for i in range(2)]
        w_in = [sem(f"w{i}_loaded") for i in range(2)]
        diff_done, e_done, small, sums, t_done, copy_done, s_copied = (sem(n) for n in
            ("diff_done", "e_done", "small", "sums", "t_done", "copy_done", "s_copied"))
        z_done, clamp_done, eu_done, log_done, max_done, sig_done, silu_done, x_done = (sem(n) for n in
            ("z_done", "clamp_done", "eu_done", "log_done", "max_done", "sig_done", "silu_done", "x_done"))

        def cols(u):
            c = u % 5
            return slice(c * CH, c * CH + (CH if c < NCH else NS))

        def width(u):
            return CH if u % 5 < NCH else NS

        def project_z(pe, n0, i, u, loaded):
            pe.wait_ge(silu_done, 1 + i * UNITS + (n0 + max(u - 4, 0)))
            if u % 5 == 0:
                pe.wait_ge(w_in[u // 5], 1 + i * 16 + loaded)
            for k in range(KD):
                mm = pe.matmul(z_ps[u % 5][:, 0:width(u)], w_z[u // 5][:, k, :], hT[:, k, cols(u)],
                               start=(k == 0), stop=(k == KD - 1))
            mm.then_inc(z_done, 1)

        def clamp_z(dve, n0, i, u):
            nth = i * UNITS + (n0 + u)
            dve.wait_ge(z_done, 1 + nth + 1)
            dve.wait_ge(silu_done, 1 + i * UNITS + (n0 + max(u - 1, 0)))
            dve.tensor_scalar(gate_buf[u % 2][:, 0:width(u)], z_ps[u % 5][:, 0:width(u)], -40.0, None, ALU.max) \
               .then_inc(clamp_done, 1)

        def log_z(act, n0, i, u):
            nth = i * UNITS + (n0 + u + 1)
            e = gate_buf[u % 2][:, 0:width(u)]
            act.wait_ge(clamp_done, 1 + nth)
            act.activation(e, e, ACT.Exp, scale=-1.0).then_inc(eu_done, 1)
            act.wait_ge(eu_done, 1 + nth)
            act.activation(e, e, ACT.Ln, bias=1.0).then_inc(log_done, 1)

        def larger_z(dve, n0, i, u):
            nth = i * UNITS + (n0 + u + 1)
            e = gate_buf[u % 2][:, 0:width(u)]
            dve.wait_ge(log_done, 1 + nth)
            dve.scalar_tensor_tensor(out=e, in0=z_ps[u % 5][:, 0:width(u)], scalar=-1.0, in1=e,
                                     op0=ALU.mult, op1=ALU.max).then_inc(max_done, 1)

        def sigmoid_z(act, n0, i, u):
            nth = i * UNITS + (n0 + u + 1)
            e = gate_buf[u % 2][:, 0:width(u)]
            act.wait_ge(max_done, 1 + nth)
            act.activation(e, e, ACT.Exp, scale=-1.0).then_inc(sig_done, 1)

        def silu_z(dve, n0, i, u):
            nth = i * UNITS + (n0 + u + 1)
            dve.wait_ge(sig_done, 1 + nth)
            dve.wait_ge(x_done, 1 + i * UNITS + (n0 + max(u - 1, 0)))
            dve.tensor_tensor(silu[u % 2][:, 0:width(u)], z_ps[u % 5][:, 0:width(u)], gate_buf[u % 2][:, 0:width(u)],
                              ALU.mult).then_inc(silu_done, 1)

        def apply_z(pool, n0, i, u, x):
            pool.wait_ge(silu_done, 1 + i * UNITS + (n0 + u + 1))
            dst = x[:, bass.ds(i * 2 + u // 5, 1), cols(u)].rearrange("p a c -> p (a c)")
            pool.tensor_tensor(dst, dst, silu[u % 2][:, 0:width(u)], ALU.mult).then_inc(x_done, 1)

        def join(dve, i, j, between):
            r, out = rows[j % 2], joined[j % 2]
            of = lambda x, g: x[:, 8 * g:8 * g + 8]
            neg_max, den_of = r[:, :, HD + 1], r[:, :, HD]
            n = [0]

            def then_wait(ins, sem, per_block):
                n[0] += 1
                ins.then_inc(sem, 1)
                dve.wait_ge(sem, 1 + i * 8 * per_block + (j * per_block + n[0]))

            dve.wait_ge(rows_in[j % 2], 1 + i * 64 + 16 * (j // 2 + 1))
            then_wait(dve.tensor_tensor(least[:, :], of(neg_max, 0), of(neg_max, 1), ALU.min), small, SMALL)
            then_wait(dve.tensor_tensor(least[:, :], least[:, :], of(neg_max, 2), ALU.min), small, SMALL)
            dve.tensor_tensor(wgt[:, :].rearrange("p (g s) -> p g s", g=G), least[:, :].unsqueeze(1).broadcast_to([P, G, 8]),
                              neg_max.rearrange("p (g s) -> p g s", g=G), ALU.subtract).then_inc(diff_done, 1)
            dve.wait_ge(e_done, 1 + i * 8 + (j + 1))
            then_wait(dve.tensor_tensor(den[:, :], wgt[:, :], den_of, ALU.mult), small, SMALL)
            then_wait(dve.tensor_tensor(of(den, 0), of(den, 0), of(den, 1), ALU.add), small, SMALL)
            then_wait(dve.tensor_tensor(of(den, 0), of(den, 0), of(den, 2), ALU.add), small, SMALL)
            then_wait(dve.reciprocal(inv[:, :], of(den, 0)), small, SMALL)
            w3 = wgt[:, :].rearrange("p (g s) -> p g s", g=G)
            then_wait(dve.tensor_tensor(w3, w3, inv[:, :].unsqueeze(1).broadcast_to([P, G, 8]), ALU.mult), small, SMALL)
            between()
            dve.wait_ge(t_done, 1 + i * 8 + max(j - 1, 0))
            n[0] = 0
            w = lambda g: of(wgt, g).unsqueeze(2).broadcast_to([P, 8, HD])
            then_wait(dve.tensor_tensor(out[:, :, :], r[:, 0:8, 0:HD], w(0), ALU.mult), sums, STEPS)
            for g in (1, 2):
                then_wait(dve.tensor_tensor(part[:, :, :], r[:, 8 * g:8 * g + 8, 0:HD], w(g), ALU.mult), sums, STEPS)
                then_wait(dve.tensor_tensor(out[:, :, :], out[:, :, :], part[:, :, :], ALU.add), sums, STEPS)

        def turn(pe, i, j):
            pe.wait_ge(sums, 1 + i * 8 * STEPS + STEPS * (j + 1))
            pe.wait_ge(copy_done, 1 + i * 8 + max(j - 1, 0))
            flat = joined[j % 2][:, :, :].rearrange("p h d -> p (h d)")
            for m in range(PAIRS):
                mm = pe.transpose(t_ps[j % 2][:, m, :], flat[:, m * P:(m + 1) * P], t["ident"][:, :])
            mm.then_inc(t_done, 1)

        def copy_turned(act, i, j):
            act.wait_ge(t_done, 1 + i * 8 + (j + 1))
            act.copy(oT_a[:, :, bass.ds(i * 8 * P + j * P, P)], t_ps[j % 2][:, :, :]).then_inc(copy_done, 1)

        with nc.Block() as block:
            @block.gpsimd
            def _(pool):
                first_signals(pool, sems)
                with pool.Fori(0, 2) as i:
                    for u in range(UNITS):
                        apply_z(pool, 0, i, u, oT_b)
                pool.wait_ge(copy_done, 1 + BLK)
                pool.wait_ge(s_copied, 1 + 1)
                with pool.Fori(0, 2) as i:
                    for u in range(UNITS):
                        apply_z(pool, 2 * UNITS, i, u, oT_a)

            @block.sync
            def _(sp):
                w_of = lambda n: dr["w_b"][n, 3] if n < BH else dr["w_za"][n - BH]
                src = dr["sums"].rearrange("g j (b p) c -> b p (g j) c", p=P)
                sp.dma_start(w_z[0][:, :, :], w_of(0)).then_inc(w_in[0], 16)
                sp.dma_start(w_z[1][:, :, :], w_of(1)).then_inc(w_in[1], 16)
                for b in range(BLK):
                    if b >= 2:
                        sp.wait_ge(sums, 1 + STEPS * (b - 1))
                    sp.dma_start(rows[b % 2][:, :, :].rearrange("p (a h) c -> p a (h c)", h=2), src[b]).then_inc(rows_in[b % 2], 16)
                    if b in (5, 9):
                        n = b // 4 + 1
                        sp.wait_ge(z_done, 1 + 5 * (n - 1))
                        sp.dma_start(w_z[n % 2][:, :, :], w_of(n)).then_inc(w_in[n % 2], 16)
                for n in range(4, 8):
                    sp.wait_ge(z_done, 1 + 5 * (n - 1))
                    sp.dma_start(w_z[n % 2][:, :, :], w_of(n)).then_inc(w_in[n % 2], 16)

            @block.tensor
            def _(pe):
                with pe.Fori(0, 2) as i:
                    for j in range(8):
                        for u in UNITS_OF_STEP[j]:
                            project_z(pe, 0, i, u, 16)
                        if j:
                            turn(pe, i, j - 1)
                    turn(pe, i, 7)
                with pe.Fori(0, 2) as i:
                    for u in range(UNITS):
                        project_z(pe, 2 * UNITS, i, u, 48)

            @block.scalar
            def _(act):
                act.preload_act_table_set("natural_log_exp_and_others")
                with act.Fori(0, 2) as i:
                    for j in range(8):
                        act.wait_ge(diff_done, 1 + i * 8 + (j + 1))
                        act.activation(wgt[:, :], wgt[:, :], ACT.Exp).then_inc(e_done, 1)
                        if j:
                            copy_turned(act, i, j - 1)
                        for u in UNITS_OF_STEP[j]:
                            log_z(act, 0, i, u)
                        for u in UNITS_OF_STEP[j]:
                            sigmoid_z(act, 0, i, u)
                    copy_turned(act, i, 7)
                with act.Fori(0, 2) as i:
                    for u in range(UNITS):
                        log_z(act, 2 * UNITS, i, u)
                        sigmoid_z(act, 2 * UNITS, i, u)

            @block.vector
            def _(dve):
                dve.tensor_copy(oT_a[:, :, SEQ:NT], t["oT_s"][:, :, :]).then_inc(s_copied, 1)
                with dve.Fori(0, 2) as i:
                    for j in range(8):
                        def between():
                            for u in UNITS_OF_STEP[j - 1] if j else ():
                                silu_z(dve, 0, i, u)
                            for u in UNITS_OF_STEP[j]:
                                clamp_z(dve, 0, i, u)

                        join(dve, i, j, between)
                        for u in UNITS_OF_STEP[j]:
                            larger_z(dve, 0, i, u)
                    for u in UNITS_OF_STEP[7]:
                        silu_z(dve, 0, i, u)
                with dve.Fori(0, 2) as i:
                    for u in range(UNITS):
                        clamp_z(dve, 2 * UNITS, i, u)
                        if u:
                            silu_z(dve, 2 * UNITS, i, u - 1)
                        larger_z(dve, 2 * UNITS, i, u)
                    silu_z(dve, 2 * UNITS, i, UNITS - 1)


def phase_merge(nc, t, dr):
    with ExitStack() as ctx:
        sb = lambda name, *a: ctx.enter_context(nc.sbuf_tensor("merge_" + name, *a))
        ps = lambda name, *a: ctx.enter_context(nc.psum_tensor("merge_" + name, *a))
        sems = []

        def sem(name):
            sems.append(ctx.enter_context(nc.semaphore("merge_" + name)))
            return sems[-1]

        branch, free = (t["oT_a"], t["oT_b"]), t["hT"]
        gates = [free[:, 0:4, b * CH:(b + 1) * CH] for b in range(2)]
        w_raw = free[:, 4:8, 0:CH]
        prod = free[:, 0:4, 2 * CH:3 * CH]
        out = [free[:, 4 + 2 * b:6 + 2 * b, 2 * CH:3 * CH] for b in range(2)]
        w_high, w_low = sb("w_high", [P, 4, CH], F32R), sb("w_low", [P, 4, CH], F32R)
        o_high = [sb(f"o_high{a}", [P, 4, CH], F32R) for a in range(2)]
        o_low = [sb(f"o_low{a}", [P, 4, CH], F32R) for a in range(2)]
        banks = [ps(f"banks{i}", [P, 4, CH], F32) for i in range(2)]
        w_in, g_in = sem("w_loaded"), [sem(f"gates{b}_loaded") for b in range(2)]
        stored = [sem(f"out{b}_stored") for b in range(2)]
        w_high_done, w_low_done, prod_done, m_done = (sem(n) for n in ("w_high_done", "w_low_done", "prod_done", "m_done"))
        o_high_done = [sem(f"o_high{a}_done") for a in range(2)]
        o_low_done = [sem(f"o_low{a}_done") for a in range(2)]
        side_done = [sem(f"branch{a}_done") for a in range(2)]
        width = lambda c: CH if c < NCH else NS
        cols = lambda c: slice(c * CH, c * CH + width(c))
        uses = lambda i, c: i * (3 - c % 2) + c // 2
        free_after = lambda i, c: i * 5 + max(c - 1, 0)

        def load_weights(sp, i):
            for a in range(2):
                for tile in range(2):
                    sp.dma_start(w_raw[:, a * 2 + tile, :], dr["w_br"][i * 2 + tile, a].rearrange("p k c -> p (k c)")) \
                      .then_inc(w_in, 16)

        def load_gates(sp, i, c):
            sp.wait_ge(prod_done, 1 + free_after(i, c))
            for tile in range(2):
                sp.dma_start(gates[c % 2][:, 2 * tile:2 * tile + 2, 0:width(c)],
                             dr["gates"][:, i * 2 + tile, :, cols(c)].rearrange("a p t -> p a t")).then_inc(g_in[c % 2], 16)

        def store(sp, i, c):
            sp.wait_ge(m_done, 1 + i * 5 + (c + 1))
            for tile in range(2):
                sp.dma_start(dr["merged"][i * 2 + tile, :, cols(c)], out[c % 2][:, tile, 0:width(c)]).then_inc(stored[c % 2], 16)

        def sp_pair(sp, i, last):
            for c in range(5):
                load_gates(sp, i, c)
                if c:
                    store(sp, i, c - 1)
                if c == 0 and not last:
                    sp.wait_ge(w_low_done, 1 + i * 4 + 4)
                    load_weights(sp, i + 1)
            store(sp, i, 4)

        def pe_pair(pe, i):
            for c in range(5):
                w = width(c)
                pe.wait_ge(prod_done, 1 + free_after(i, c))
                for a in range(2):
                    if c == 0:
                        pe.wait_ge(w_low_done, 1 + i * 4 + (2 * a + 2))
                    pe.wait_ge(o_low_done[a], 1 + i * 5 + (c + 1))
                    for tile in range(2):
                        bank = banks[c % 2][:, 2 * tile + a, 0:w]
                        for k in range(4):
                            f = slice(k * P, (k + 1) * P)
                            pe.matmul(bank, w_high[:, 2 * a + tile, f], o_high[a][:, k, 0:w], start=(k == 0), stop=False)
                            pe.matmul(bank, w_high[:, 2 * a + tile, f], o_low[a][:, k, 0:w], start=False, stop=False)
                            mm = pe.matmul(bank, w_low[:, 2 * a + tile, f], o_high[a][:, k, 0:w], start=False, stop=(k == 3))
                    mm.then_inc(side_done[a], 1)

        def act_pair(act, i):
            for c in range(5):
                for a in range(2):
                    if c == 0 and a == 1:
                        act.wait_ge(w_in, 1 + i * 64 + 64)
                        act.wait_ge(side_done[1], 1 + i * 5)
                        for p in range(4):
                            act.copy(w_high[:, p, :], w_raw[:, p, :]).then_inc(w_high_done, 1)
                    act.wait_ge(side_done[a], 1 + i * 5 + c)
                    act.copy(o_high[a][:, :, 0:width(c)], branch[a][:, :, cols(c)]).then_inc(o_high_done[a], 1)

        def merge(dve, i, c):
            nth, w = i * 5 + (c + 1), width(c)
            dve.wait_ge(side_done[1], 1 + nth)
            dve.wait_ge(g_in[c % 2], 1 + uses(i, c) * 32 + 32)
            dve.wait_ge(m_done, 1 + i * 5 + c)
            dve.tensor_tensor(prod[:, :, 0:w], banks[c % 2][:, :, 0:w], gates[c % 2][:, :, 0:w], ALU.mult).then_inc(prod_done, 1)
            dve.wait_ge(prod_done, 1 + nth)
            dve.wait_ge(stored[c % 2], 1 + uses(i, c) * 32)
            dve.tensor_tensor(out[c % 2][:, :, 0:w], prod[:, 0:4:2, 0:w], prod[:, 1:4:2, 0:w], ALU.add).then_inc(m_done, 1)

        def pool_pair(pool, i):
            for p in range(4):
                pool.wait_ge(w_high_done, 1 + i * 4 + (p + 1))
                pool.tensor_tensor(w_low[:, p, :], w_raw[:, p, :], w_high[:, p, :], ALU.subtract).then_inc(w_low_done, 1)

        def dve_pair(dve, i):
            for c in range(5):
                for a in range(2):
                    dve.wait_ge(o_high_done[a], 1 + i * 5 + (c + 1))
                    dve.tensor_tensor(o_low[a][:, :, 0:width(c)], branch[a][:, :, cols(c)], o_high[a][:, :, 0:width(c)],
                                      ALU.subtract).then_inc(o_low_done[a], 1)
                if c:
                    merge(dve, i, c - 1)
            merge(dve, i, 4)

        with nc.Block() as block:
            @block.gpsimd
            def _(pool):
                first_signals(pool, sems[::-1])
                with pool.Fori(0, 4) as i:
                    pool_pair(pool, i)

            @block.sync
            def _(sp):
                load_weights(sp, 0)
                with sp.Fori(0, 3) as i:
                    sp_pair(sp, i, False)
                sp_pair(sp, 3, True)
                for b in range(2):
                    sp.wait_ge(stored[b], 1 + 32 * 4 * (3 - b))

            @block.tensor
            def _(pe):
                with pe.Fori(0, 4) as i:
                    pe_pair(pe, i)

            @block.scalar
            def _(act):
                act.preload_act_table_set("natural_log_exp_and_others")
                with act.Fori(0, 4) as i:
                    act_pair(act, i)

            @block.vector
            def _(dve):
                with dve.Fori(0, 4) as i:
                    dve_pair(dve, i)


def phase_output(nc, t, dr):
    HALF = KD // 2
    with ExitStack() as ctx:
        sb = lambda name, *a: ctx.enter_context(nc.sbuf_tensor("output_" + name, *a))
        ps = lambda name, *a: ctx.enter_context(nc.psum_tensor("output_" + name, *a))
        sems = []

        def sem(name):
            sems.append(ctx.enter_context(nc.semaphore("output_" + name)))
            return sems[-1]

        gate = t["gate"]
        m_raw = [sb(f"m_raw{i}", [P, HALF, CH], F32) for i in range(2)]
        m_high, m_low = sb("m_high", [P, KD, NT], F32R), sb("m_low", [P, KD, NT], F32R)
        w_raw = [sb(f"w_raw{i}", [P, KD, P], F32) for i in range(2)]
        w_high = [sb(f"w_high{i}", [P, KD, P], F32R) for i in range(2)]
        w_low = [sb(f"w_low{i}", [P, KD, P], F32R) for i in range(2)]
        y_sb = [sb(f"y{i}", [P, NT], F32) for i in range(2)]
        gated = sb("gated", [P, NS], F32)
        gate_c = sb("gate_c", [P, 9], F32)
        banks = [ps(f"bank{i}", [P, CH], F32) for i in range(5)]
        m_in = [sem(f"m{i}_loaded") for i in range(2)]
        w_in = [sem(f"w{i}_loaded") for i in range(2)]
        x_in = [sem(f"x{i}_loaded") for i in range(2)]
        stored = [sem(f"y{i}_stored") for i in range(2)]
        m_high_done, m_low_done, w_high_done, w_low_done = (sem(n) for n in
            ("m_high_done", "m_low_done", "w_high_done", "w_low_done"))
        mm_done, y_done, gc_done, g_done = sem("mm_done"), sem("y_done"), sem("gc_done"), sem("g_done")
        width = lambda u: CH if u < NCH else NS
        cols = lambda u: slice(u * CH, u * CH + width(u))

        def tiles(eng, tile):
            tile(eng, 0, 0, 0, True, False)
            with eng.Fori(0, 3) as i:
                tile(eng, i * 2 + 1, 1, i, False, False)
                tile(eng, i * 2 + 2, 0, i + 1, False, False)
            tile(eng, 7, 1, 3, False, True)

        def halves_of(u):
            return [(h, u, slice(h * HALF, (h + 1) * HALF), cols(u), width(u)) for h in range(2)]

        def merged_high(act, u):
            for b, nth, k, c, n in halves_of(u):
                act.wait_ge(m_in[b], 1 + 16 * (nth + 1))
                act.copy(m_high[:, k, c], m_raw[b][:, :, 0:n]).then_inc(m_high_done, 1)

        def merged_low(dve, u):
            for b, nth, k, c, n in halves_of(u):
                dve.wait_ge(m_high_done, 1 + 2 * nth + (b + 1))
                dve.tensor_tensor(m_low[:, k, c], m_raw[b][:, :, 0:n], m_high[:, k, c], ALU.subtract) \
                   .then_inc(m_low_done, 1)

        def weights_high(act, m, b, nth):
            act.wait_ge(w_in[b], 1 + nth * 16 + 16)
            if not isinstance(m, int) or m >= 2:
                act.wait_ge(mm_done, 1 + m * 5 - 5)
            act.copy(w_high[b][:, :, :], w_raw[b][:, :, :]).then_inc(w_high_done, 1)

        def weights_low(dve, m, b):
            dve.wait_ge(w_high_done, 1 + m + 1)
            dve.tensor_tensor(w_low[b][:, :, :], w_raw[b][:, :, :], w_high[b][:, :, :], ALU.subtract) \
               .then_inc(w_low_done, 1)

        def pe_tile(pe, m, b, nth, first, last):
            pe.wait_ge(w_low_done, 1 + m + 1)
            for u in range(5):
                bank = banks[u][:, 0:width(u)]
                if not first:
                    pe.wait_ge(y_done, 1 + m * 5 + (u - 4))
                if first:
                    pe.wait_ge(m_low_done, 1 + 2 * (u + 1))
                for k in range(KD):
                    high, low = m_high[:, k, cols(u)], m_low[:, k, cols(u)]
                    pe.matmul(bank, w_high[b][:, k, :], high, start=(k == 0), stop=False)
                    pe.matmul(bank, w_high[b][:, k, :], low, start=False, stop=False)
                    mm = pe.matmul(bank, w_low[b][:, k, :], high, start=False, stop=(k == KD - 1))
                mm.then_inc(mm_done, 1)

        def act_tile(act, m, b, nth, first, last):
            if first:
                weights_high(act, 0, 0, 0)
                for u in range(5):
                    merged_high(act, u)
                weights_high(act, 1, 1, 0)
            elif not last:
                weights_high(act, m + 1, 1 - b, nth if b == 0 else nth + 1)
            act.wait_ge(y_done, 1 + m * 5 + 5)
            act.dma_start(dr["yT"][m], y_sb[b][:, :]).then_inc(stored[b], 16)

        def dve_tile(dve, m, b, nth, first, last):
            if first:
                weights_low(dve, 0, 0)
                merged_low(dve, 0)
            dve.wait_ge(x_in[b], 1 + nth * 16 + 16)
            dve.wait_ge(g_done, 1 + m)
            dve.tensor_copy(gate_c[:, :], gate[:, bass.ds(m, 1), :].rearrange("p a c -> p (a c)")).then_inc(gc_done, 1)
            dve.wait_ge(gc_done, 1 + m + 1)
            for u in range(5):
                y, bank = y_sb[b][:, cols(u)], banks[u]
                if first and u < 4:
                    merged_low(dve, u + 1)
                if u == (4 if first else 1) and not last:
                    weights_low(dve, m + 1, 1 - b)
                dve.wait_ge(mm_done, 1 + m * 5 + (u + 1))
                if u < NCH:
                    dve.scalar_tensor_tensor(out=y, in0=bank[:, :], scalar=gate_c[:, 0:1], in1=y,
                                             op0=ALU.mult, op1=ALU.add).then_inc(y_done, 1)
                else:
                    dve.tensor_tensor(gated[:, :].rearrange("p (b t) -> p b t", t=ST),
                                      bank[:, 0:NS].rearrange("p (b t) -> p b t", t=ST),
                                      gate_c[:, 1:9].unsqueeze(2).broadcast_to([P, SB, ST]), ALU.mult).then_inc(g_done, 1)
                    dve.wait_ge(g_done, 1 + m + 1)
                    dve.tensor_tensor(y, gated[:, :], y, ALU.add).then_inc(y_done, 1)

        def load_weights(sp, m, b):
            if not isinstance(m, int):
                sp.wait_ge(w_low_done, 1 + m - 1)
            sp.dma_start(w_raw[b][:, :, :], dr["w_o"][m]).then_inc(w_in[b], 16)

        def load_x(sp, m, b, nth):
            if not isinstance(m, int):
                sp.wait_ge(stored[b], 1 + nth * 16)
            sp.dma_start(y_sb[b][:, :], dr["xT"][:, m, :]).then_inc(x_in[b], 16)

        with nc.Block() as block:
            @block.gpsimd
            def _(pool):
                first_signals(pool, sems)

            @block.sync
            def _(sp):
                load_weights(sp, 0, 0)
                for u in range(5):
                    for b, nth, k, c, n in halves_of(u):
                        if nth:
                            sp.wait_ge(m_low_done, 1 + 2 * nth + (b - 1))
                        sp.dma_start(m_raw[b][:, :, 0:n], dr["merged"].rearrange("k p t -> p k t")[:, k, c]).then_inc(m_in[b], 16)
                    if u == 0:
                        load_x(sp, 0, 0, 0)
                load_weights(sp, 1, 1)
                load_x(sp, 1, 1, 0)
                with sp.Fori(0, 3) as i:
                    for b in range(2):
                        load_weights(sp, i * 2 + (b + 2), b)
                        load_x(sp, i * 2 + (b + 2), b, i + 1)

            @block.tensor
            def _(pe):
                tiles(pe, pe_tile)

            @block.scalar
            def _(act):
                act.preload_act_table_set("natural_log_exp_and_others")
                tiles(act, act_tile)
                for b in range(2):
                    act.wait_ge(stored[b], 1 + 64)

            @block.vector
            def _(dve):
                tiles(dve, dve_tile)


def decoder_step(nc, dr):
    with ExitStack() as whole:
        t = {}

        def keep(ctx, name, shape):
            t[name] = ctx.enter_context(nc.sbuf_tensor(name, shape, F32))

        keep(whole, "ident", [P, P])
        keep(whole, "eps", [P, 1])
        keep(whole, "gate", [P, 8, 9])
        const_in = whole.enter_context(nc.semaphore("const_loaded"))
        with nc.Block() as block:
            @block.sync
            def _(sp):
                sp.dma_start(t["ident"][:, :], dr["ident"]).then_inc(const_in, 16)
                sp.dma_start(t["eps"][:, :], dr["eps"]).then_inc(const_in, 16)
                sp.wait_ge(const_in, 32)
        with ExitStack() as ctx:
            keep(ctx, "mod", [P, 16, 9])
            keep(ctx, "oT_s", [P, PAIRS, NS])
            keep(ctx, "hT", [P, KD, NT])
            phase_input(nc, t, dr)
            phase_gates(nc, t, dr)
            phase_attention(nc, t, dr)
            phase_sample(nc, t, dr)
            keep(ctx, "oT_b", [P, BH, NT])
            phase_hgrn(nc, t, dr)
            keep(ctx, "oT_a", [P, PAIRS, NT])
            phase_join(nc, t, dr)
            phase_merge(nc, t, dr)
        phase_output(nc, t, dr)


BIG = 1.0e30


def _tables(np):
    c = {}
    c["ident"] = np.eye(P, dtype=np.float32)
    c["eps"] = np.full((P, 1), EPS, np.float32)
    c["ones_d"] = np.full((P, P), 1.0 / D, np.float32)
    half = np.arange(P) // HD
    c["ones_h"] = (half[:, None] == half[None, :]).astype(np.float32) / HD
    c["ones_i"] = np.full((P, P), 1.0 / P, np.float32)
    slopes = (2.0 ** (-8.0 * (np.arange(24) + 1) / 24)).astype(np.float32).reshape(G, 8)
    delta = np.arange(P)[:, None] + P - np.arange(2 * P)[None, :]
    dist = np.empty((PAIRS, G, P, 2, 2 * P), np.float32)
    for g in range(G):
        for s in range(8):
            dist[s // 2, g, :, s % 2] = np.where((delta >= 0) & (delta <= P),
                                                 slopes[g, s] * (delta * DIL[g]).astype(np.float32), np.float32(BIG))
    c["dist"] = dist
    pen = np.full((2, 8, ST, 4 * CH), BIG, np.float32)
    pos = np.arange(P)
    for s in range(8):
        for q in range(ST):
            def put(col, g, d):
                ok = (d >= 0) & (d <= DIL[g] * P) & (d % DIL[g] == 0)
                pen[:, s, q, col:col + len(d)] = np.where(ok, slopes[g, s] * d.astype(np.float32), np.float32(BIG))
            for r in range(4):
                put(r * P, 1, 512 + q - (4 * pos + r))
            for r in range(8):
                put(CH + r * P, 2, 2048 + q - (16 * pos + r))
            put(3 * CH, 0, P + q - pos)
            for g in range(G):
                put(3 * CH + P + 8 * g, g, q - np.arange(ST))
    c["pen_s"] = pen.reshape(P, 4 * CH)[:, :3 * CH + P + 24].copy()
    row = np.arange(P)
    c["own_s"] = (((row % 64) // 8)[:, None] == (np.arange(CH) // HD)[None, :]).astype(np.float32)
    c["sel_s"] = ((row // 64 * 8 + row % 8)[:, None] == np.arange(16)[None, :]).astype(np.float32)
    s_, t_ = np.arange(P)[:, None], np.arange(P)[None, :]
    lev = np.zeros((P, 8, P), np.uint32)
    lev[:, 0] = s_ == t_
    for l in range(1, 8):
        B = 1 << l
        lev[:, l] = (s_ // B == t_ // B) & (s_ % B < B // 2) & (t_ % B >= B // 2)
    c["level"] = lev
    c["seq_s"] = ((np.arange(NS) // ST)[:, None] == np.arange(SB)[None, :]).astype(np.float32)
    return c


def kernel(x_prompt, x_sample, cache_kv_g0, cache_kv_g1, cache_kv_g2, state_hgrn, c_prompt, c_sample,
           norm_gain, w_ada, b_ada, w_in, q_norm_gain, k_norm_gain, hgrn_lb_logits, hgrn_out_norm_gain,
           w_branch_a, w_branch_b, w_out):
    import numpy as np
    import concourse.bacc as bacc
    from concourse.bass_utils import run_bass_kernel_spmd as run

    A = np.asarray
    tiles = lambda w: A(w).reshape(-1, P, w.shape[-1] // P, P).transpose(2, 1, 0, 3)
    x = np.concatenate([A(x_prompt)[0], A(x_sample).reshape(NS, D)])
    c = np.concatenate([A(c_prompt), A(c_sample)])
    w = tiles(A(w_in)[0])
    kv = [A(cache_kv_g0)[0], A(cache_kv_g1)[0], A(cache_kv_g2)[0]]
    keys = []
    keys.append(kv[1].reshape(SB, P, 4, 2, CH).transpose(0, 2, 1, 3, 4))
    keys.append(kv[2].reshape(SB, P, 16, 2, CH)[:, :, :8].transpose(0, 2, 1, 3, 4))
    keys.append(kv[0].reshape(SB, 1, P, 2, CH))
    keys = np.concatenate(keys, axis=1)
    ins = {
        "xT": x.T.reshape(KD, P, NT).transpose(1, 0, 2),
        "cT": c.T.reshape(KD, P, 9).transpose(1, 0, 2),
        "w_ada": A(w_ada)[0].reshape(KD, P, 6, CH).transpose(2, 1, 0, 3),
        "b_ada": A(b_ada)[0].reshape(24, P).T,
        "norm_gain": A(norm_gain)[0].reshape(KD, P).T,
        "w_qkv": w[0:36].reshape(3, G, PAIRS, P, KD, P).transpose(2, 1, 0, 3, 4, 5),
        "w_za": w[36:40],
        "w_b": w[40:56].reshape(4, BH, P, KD, P).transpose(1, 0, 2, 3, 4),
        "w_g": w[56:72].reshape(2, 8, P, KD, P).transpose(1, 0, 2, 3, 4),
        "w_br": np.stack([tiles(A(w_branch_a)[0]), tiles(A(w_branch_b)[0])], axis=1),
        "w_o": tiles(A(w_out)[0]),
        "qk_gain": np.stack([np.tile(A(q_norm_gain)[0], 2), np.tile(A(k_norm_gain)[0], 2)], axis=1),
        "lb": A(hgrn_lb_logits).reshape(2, BH, P).transpose(2, 0, 1),
        "o_gain": A(hgrn_out_norm_gain)[0].reshape(P, 1),
        "kT_c": keys[:, :, :, 0].reshape(SB, KEYS * P, 4, P).transpose(0, 3, 2, 1),
        "v_c": keys[:, :, :, 1].transpose(0, 2, 1, 3),
        "state": A(state_hgrn)[0].transpose(1, 2, 0, 3),
    }
    ins.update(_tables(np))
    outs = {
        "yT": (8, P, NT), "kT_p0": (4, P, P), "kT_p1": (4, P, 512), "kT_p2": (4, P, SEQ),
        "v_p0": (4, P, 1, 2, 65), "v_p1": (4, P, 4, 2, 65), "v_p2": (4, P, 16, 2, 65),
        "kT_s0": (4, P, NS), "kT_s1": (4, P, NS), "kT_s2": (4, P, NS),
        "v_s0": (4, NS, P), "v_s1": (4, NS, P), "v_s2": (4, NS, P),
        "state_p": (BH, P, P), "state_s": (BH, P, SB, P),
    }
    scratch = {"gates": (2, 8, P, NT), "sums": (G, PAIRS, SEQ, ORow), "qT_s": (PAIRS, G, P, NS), "merged": (8, P, NT)}

    nc = bacc.Bacc("TRN2", target_bir_lowering=False, num_devices=1)
    arrays, dr = {}, {}
    for name, a in ins.items():
        arrays["in_" + name] = np.ascontiguousarray(a)
        dr[name] = nc.dram_tensor("in_" + name, a.shape, mybir.dt.from_np(a.dtype), kind="ExternalInput").ap()
    for name, shape in outs.items():
        dr[name] = nc.dram_tensor("out_" + name, shape, F32, kind="ExternalOutput").ap()
    for name, shape in scratch.items():
        dr[name] = nc.dram_tensor("scratch_" + name, shape, F32).ap()
    decoder_step(nc, dr)
    r = run(nc, [arrays], core_ids=[0]).results[0]
    o = {name: r["out_" + name] for name in outs}

    y = o["yT"].transpose(2, 0, 1).reshape(NT, D)
    kv_p, kv_s = [], []
    for g, W in enumerate((P, 512, SEQ)):
        k = o[f"kT_p{g}"].transpose(2, 0, 1).reshape(W, CH)
        v = o[f"v_p{g}"][..., :HD]
        v = v.transpose(1, 2, 0, 3, 4).reshape(W, CH)
        kv_p.append(np.stack([k.reshape(1, 1, W, 8, HD), v.reshape(1, 1, W, 8, HD)], axis=3))
        k = o[f"kT_s{g}"].transpose(2, 0, 1).reshape(1, SB, ST, 8, HD)
        v = o[f"v_s{g}"].transpose(1, 0, 2).reshape(1, SB, ST, 8, HD)
        kv_s.append(np.stack([k, v], axis=3))
    return (y[:SEQ].reshape(1, SEQ, D), y[SEQ:].reshape(SB, ST, D), *kv_p,
            o["state_p"].reshape(1, 1, BH, P, P), *kv_s, o["state_s"].transpose(2, 0, 1, 3).reshape(1, SB, BH, P, P))
```
